# Optimizing a Trainium2 kernel written in Bass

```python
import math
import jax, jax.numpy as jnp
from jax import lax
import numpy as np

D_MODEL = 1024
BATCH = 1
SEQ = 256
DEPTH = 2

CTX_LEN = 256
GRID_W = 64

MLA_HEADS = 8
MLA_Q_RANK = 384
MLA_KV_RANK = 256
MLA_NOPE = 64
MLA_ROPE = 32
MLA_V = 64
MLA_QK = MLA_NOPE + MLA_ROPE
MLA_SCALE = MLA_QK ** -0.5
ATTN_BLOCK = 128
ROPE_BASE = 10000.0

HG_HEADS = 4
HG_DK = 64
HG_DV = 64
HG_CHUNK = 64

SSM_HEADS = 4
SSM_HEADDIM = 64
SSM_GROUPS = 2
SSM_STATE = 64
SSM_CONV = 5
SSM_CHUNK = 128
SSM_INNER = SSM_HEADS * SSM_HEADDIM
SSM_XBC = SSM_INNER + 2 * SSM_GROUPS * SSM_STATE

FFN_HIDDEN = -(-8 * D_MODEL // (3 * 256)) * 256

MLA_COLS = MLA_Q_RANK + MLA_KV_RANK + MLA_ROPE
HG_W = HG_HEADS * HG_DK
HG_COLS = 3 * HG_W + 2 * HG_HEADS * HG_DV
SSM_COLS = SSM_INNER + SSM_XBC + 2 * SSM_HEADS
IN_COLS = MLA_COLS + HG_COLS + SSM_COLS
MIX_WIDTH = MLA_HEADS * MLA_V + HG_HEADS * HG_DV + SSM_INNER

kernel_name = "hybrid_mla_hgrn2_mamba2_diffusion_block"

def rms_norm(x, g, eps=1e-6):
    xf = x.astype(jnp.float32)
    y = xf * lax.rsqrt(jnp.mean(xf * xf, axis=-1, keepdims=True) + eps)
    return (y * g.astype(jnp.float32)).astype(x.dtype)

def modulate(h, shift, scale):
    return h * (1 + scale) + shift

def swiglu(h, w_in, w_out):
    a, b = jnp.split(h @ w_in, 2, axis=-1)
    return (jax.nn.silu(a) * b) @ w_out

def axial_rope_tables(n):
    rows = n // GRID_W
    row = jnp.repeat(jnp.arange(rows, dtype=jnp.float32), GRID_W)
    col = jnp.tile(jnp.arange(GRID_W, dtype=jnp.float32), rows)
    n_freq = MLA_ROPE // 4
    inv = ROPE_BASE ** (-jnp.arange(n_freq, dtype=jnp.float32) / n_freq)
    ang = jnp.stack([row[:, None] * inv, col[:, None] * inv], axis=1)
    return jnp.cos(ang), jnp.sin(ang)

def apply_axial_rope(x, cos, sin):
    xr = x.astype(jnp.float32).reshape(x.shape[:-1] + (2, 2, MLA_ROPE // 4))
    x1, x2 = xr[..., 0, :], xr[..., 1, :]
    out = jnp.stack([x1 * cos - x2 * sin, x2 * cos + x1 * sin], axis=-2)
    return out.reshape(x.shape).astype(x.dtype)

def mla_project(p, qa_g, wqb, kva_g, wkvb):
    bsz, n, _ = p.shape
    q_lat = rms_norm(p[..., :MLA_Q_RANK], qa_g)
    kv_lat = rms_norm(p[..., MLA_Q_RANK:MLA_Q_RANK + MLA_KV_RANK], kva_g)
    k_rope = p[..., MLA_Q_RANK + MLA_KV_RANK:MLA_COLS]
    q = (q_lat @ wqb).reshape(bsz, n, MLA_HEADS, MLA_QK)
    kv = (kv_lat @ wkvb).reshape(bsz, n, MLA_HEADS, MLA_NOPE + MLA_V)
    return q[..., :MLA_NOPE], q[..., MLA_NOPE:], kv[..., :MLA_NOPE], kv[..., MLA_NOPE:], k_rope

def mla_probs(qn, qr, kn, kr):
    s = jnp.einsum('bhqd,bhkd->bhqk', qn, kn) + jnp.einsum('bhqr,bkr->bhqk', qr, kr)
    return jax.nn.softmax(s.astype(jnp.float32) * MLA_SCALE, axis=-1)

def mla_mixer(p_ctx, p_lat, qa_g, wqb, kva_g, wkvb, cos, sin, with_ctx_out):
    bsz, n, _ = p_lat.shape
    n_ctx = p_ctx.shape[1]
    qn_c, qr_c, kn_c, v_c, kr_c = mla_project(p_ctx, qa_g, wqb, kva_g, wkvb)
    qn, qr, kn, v, kr = mla_project(p_lat, qa_g, wqb, kva_g, wkvb)
    qr = apply_axial_rope(qr, cos[:, None], sin[:, None])
    kr = apply_axial_rope(kr, cos, sin)
    heads = lambda a: a.transpose(0, 2, 1, 3)
    kn_all = jnp.concatenate([heads(kn_c), heads(kn)], axis=2)
    v_all = jnp.concatenate([heads(v_c), heads(v)], axis=2)
    kr_all = jnp.concatenate([kr_c, kr], axis=1)
    nb = n // ATTN_BLOCK
    to_blocks = lambda a: a.reshape(bsz, nb, ATTN_BLOCK, MLA_HEADS, a.shape[-1]).transpose(1, 0, 3, 2, 4)

    def block(qs):
        qn_b, qr_b = qs
        pr = mla_probs(qn_b, qr_b, kn_all, kr_all)
        return jnp.einsum('bhqk,bhkd->bhqd', pr.astype(v_all.dtype), v_all)

    o = lax.map(block, (to_blocks(qn), to_blocks(qr)))
    o_lat = o.transpose(1, 0, 3, 2, 4).reshape(bsz, n, MLA_HEADS * MLA_V)
    o_ctx = None
    if with_ctx_out:
        pr = mla_probs(heads(qn_c), heads(qr_c), heads(kn_c), kr_c)
        o_ctx = jnp.einsum('bhqk,bhkd->bqhd', pr.astype(v_c.dtype), heads(v_c)).reshape(bsz, n_ctx, MLA_HEADS * MLA_V)
    return o_lat, o_ctx

def gla_chunk_scan(q, k, logf, v, s0):
    bsz, nh, n, dk = q.shape
    dv = v.shape[-1]
    nc = n // HG_CHUNK
    to_chunks = lambda a: a.reshape(bsz, nh, nc, HG_CHUNK, a.shape[-1]).transpose(2, 0, 1, 3, 4)
    tri = jnp.tril(jnp.ones((HG_CHUNK, HG_CHUNK), bool))[:, :, None]

    def step(S, blk):
        qc, kc, gc, vc = blk
        b = jnp.cumsum(gc, axis=2)
        diff = b[:, :, :, None, :] - b[:, :, None, :, :]
        dec = jnp.where(tri, jnp.exp(jnp.where(tri, diff, 0.0)), 0.0)
        att = jnp.einsum('bhtk,bhsk,bhtsk->bhts', qc, kc, dec)
        o = jnp.einsum('bhts,bhsv->bhtv', att, vc) + jnp.einsum('bhtk,bhkv->bhtv', qc * jnp.exp(b), S)
        b_last = b[:, :, -1:, :]
        S = jnp.exp(b_last[:, :, 0, :, None]) * S + jnp.einsum('bhsk,bhsv->bhkv', kc * jnp.exp(b_last - b), vc)
        return S, o

    S, o = lax.scan(step, s0, (to_chunks(q), to_chunks(k), to_chunks(logf), to_chunks(v)))
    return o.transpose(1, 2, 0, 3, 4).reshape(bsz, nh, n, dv), S

def hgrn_gates(ff, lb):
    lb = lb.astype(jnp.float32).reshape(HG_HEADS, 1, HG_DK)
    f = lb + (1 - lb) * jax.nn.sigmoid(ff)
    k = (1 - lb) * jax.nn.sigmoid(-ff)
    return k, jnp.log(f)

def hgrn_split(p):
    bsz, n, _ = p.shape
    heads = lambda a: a.reshape(bsz, n, HG_HEADS, -1).transpose(0, 2, 1, 3).astype(jnp.float32)
    q = heads(jax.nn.silu(p[..., :HG_W]))
    ff_f = heads(p[..., HG_W:2 * HG_W])
    ff_b = heads(p[..., 2 * HG_W:3 * HG_W])
    iv = heads(p[..., 3 * HG_W:3 * HG_W + HG_HEADS * HG_DV])
    og = p[..., 3 * HG_W + HG_HEADS * HG_DV:]
    return q, ff_f, ff_b, iv, og

def hgrn_bidir(q, ff_f, ff_b, iv, lb_f, lb_b, s0_f, s0_b):
    k_f, g_f = hgrn_gates(ff_f, lb_f)
    o_f, s_f = gla_chunk_scan(q, k_f, g_f, iv, s0_f)
    k_b, g_b = hgrn_gates(ff_b, lb_b)
    flip = lambda a: jnp.flip(a, axis=2)
    o_b, s_b = gla_chunk_scan(flip(q), flip(k_b), flip(g_b), flip(iv), s0_b)
    return o_f + flip(o_b), s_f, s_b

def hgrn_readout(o, og, norm_g):
    bsz, _, n, _ = o.shape
    o = rms_norm(o, norm_g.reshape(HG_HEADS, 1, HG_DV))
    o = o.transpose(0, 2, 1, 3).reshape(bsz, n, HG_HEADS * HG_DV)
    return (o * jax.nn.silu(og.astype(jnp.float32))).astype(og.dtype)

def hgrn_mixer(p_ctx, p_lat, lb_f, lb_b, norm_g, with_ctx_out):
    bsz = p_lat.shape[0]
    zeros = jnp.zeros((bsz, HG_HEADS, HG_DK, HG_DV), jnp.float32)
    qc, ffc_f, ffc_b, ivc, ogc = hgrn_split(p_ctx)
    oc, sc_f, sc_b = hgrn_bidir(qc, ffc_f, ffc_b, ivc, lb_f, lb_b, zeros, zeros)
    q, ff_f, ff_b, iv, og = hgrn_split(p_lat)
    o, _, _ = hgrn_bidir(q, ff_f, ff_b, iv, lb_f, lb_b, sc_f, sc_b)
    o_ctx = hgrn_readout(oc, ogc, norm_g) if with_ctx_out else None
    return hgrn_readout(o, og, norm_g), o_ctx

def seg_decay(a):
    T = a.shape[-1]
    strict = jnp.tril(jnp.ones((T, T), bool), -1)
    lower = jnp.tril(jnp.ones((T, T), bool))
    ae = jnp.where(strict, jnp.broadcast_to(a[..., None], a.shape + (T,)), 0.0)
    cs = jnp.cumsum(ae, axis=-2)
    return jnp.where(lower, jnp.exp(jnp.where(lower, cs, 0.0)), 0.0)

def ssd_chunked(x, a, Bm, Cm, s0):
    bsz, n, nh, hp = x.shape
    nc = n // SSM_CHUNK
    X = x.reshape(bsz, nc, SSM_CHUNK, nh, hp)
    Bc = Bm.reshape(bsz, nc, SSM_CHUNK, nh, -1)
    Cc = Cm.reshape(bsz, nc, SSM_CHUNK, nh, -1)
    A = a.reshape(bsz, nc, SSM_CHUNK, nh).transpose(0, 3, 1, 2)
    A_cs = jnp.cumsum(A, axis=-1)
    L = seg_decay(A)
    scores = jnp.einsum('bclhn,bcshn->bhcls', Cc, Bc) * L
    y_diag = jnp.einsum('bhcls,bcshp->bclhp', scores, X)
    decay_states = jnp.exp(A_cs[..., -1:] - A_cs)
    states = jnp.einsum('bclhn,bhcl,bclhp->bchpn', Bc, decay_states, X)
    states = jnp.concatenate([s0[:, None], states], axis=1)
    decay_chunk = seg_decay(jnp.pad(A_cs[..., -1], ((0, 0), (0, 0), (1, 0))))
    new_states = jnp.einsum('bhzc,bchpn->bzhpn', decay_chunk, states)
    y_off = jnp.einsum('bclhn,bchpn,bhcl->bclhp', Cc, new_states[:, :-1], jnp.exp(A_cs))
    return (y_diag + y_off).reshape(bsz, n, nh, hp), new_states[:, -1]

def depthwise_conv(u, w, b):
    ch = u.shape[-1]
    y = lax.conv_general_dilated(u, w[:, None, :].astype(u.dtype), window_strides=(1,),
                                 padding=[(SSM_CONV // 2, SSM_CONV // 2)],
                                 dimension_numbers=('NWC', 'WIO', 'NWC'), feature_group_count=ch)
    return y + b

def ssm_split(p, conv_w, conv_b):
    bsz, n, _ = p.shape
    z = p[..., :SSM_INNER]
    xbc = jax.nn.silu(depthwise_conv(p[..., SSM_INNER:SSM_INNER + SSM_XBC], conv_w, conv_b)).astype(jnp.float32)
    xs = xbc[..., :SSM_INNER].reshape(bsz, n, SSM_HEADS, SSM_HEADDIM)
    rep = SSM_HEADS // SSM_GROUPS
    grp = lambda a: jnp.repeat(a.reshape(bsz, n, SSM_GROUPS, SSM_STATE), rep, axis=2)
    Bm = grp(xbc[..., SSM_INNER:SSM_INNER + SSM_GROUPS * SSM_STATE])
    Cm = grp(xbc[..., SSM_INNER + SSM_GROUPS * SSM_STATE:])
    dt_raw = p[..., SSM_INNER + SSM_XBC:].astype(jnp.float32).reshape(bsz, n, 2, SSM_HEADS)
    return z, xs, Bm, Cm, dt_raw

def ssm_bidir(xs, Bm, Cm, dt_raw, dt_bias, a_log, s0_f, s0_b):
    dt = jax.nn.softplus(dt_raw + dt_bias.astype(jnp.float32))
    A = -jnp.exp(a_log.astype(jnp.float32))
    y_f, s_f = ssd_chunked(xs * dt[..., 0, :, None], A[0] * dt[..., 0, :], Bm, Cm, s0_f)
    flip = lambda a: jnp.flip(a, axis=1)
    y_b, s_b = ssd_chunked(flip(xs * dt[..., 1, :, None]), flip(A[1] * dt[..., 1, :]), flip(Bm), flip(Cm), s0_b)
    return y_f + flip(y_b), s_f, s_b

def ssm_readout(y, xs, z, d_skip, norm_g):
    bsz, n = z.shape[:2]
    y = (y + d_skip.astype(jnp.float32)[:, None] * xs).reshape(bsz, n, SSM_INNER)
    yz = (y * jax.nn.silu(z.astype(jnp.float32))).reshape(bsz, n, SSM_GROUPS, SSM_INNER // SSM_GROUPS)
    out = rms_norm(yz, norm_g.reshape(SSM_GROUPS, -1))
    return out.reshape(bsz, n, SSM_INNER).astype(z.dtype)

def ssm_mixer(p_ctx, p_lat, conv_w, conv_b, dt_bias, a_log, d_skip, norm_g, with_ctx_out):
    bsz = p_lat.shape[0]
    zeros = jnp.zeros((bsz, SSM_HEADS, SSM_HEADDIM, SSM_STATE), jnp.float32)
    zc, xc, Bc, Cc, dtc = ssm_split(p_ctx, conv_w, conv_b)
    yc, sc_f, sc_b = ssm_bidir(xc, Bc, Cc, dtc, dt_bias, a_log, zeros, zeros)
    z, xs, Bm, Cm, dtr = ssm_split(p_lat, conv_w, conv_b)
    y, _, _ = ssm_bidir(xs, Bm, Cm, dtr, dt_bias, a_log, sc_f, sc_b)
    o_ctx = ssm_readout(yc, xc, zc, d_skip, norm_g) if with_ctx_out else None
    return ssm_readout(y, xs, z, d_skip, norm_g), o_ctx

def setup_inputs(seed: int = 0) -> dict:
    key = jax.random.key(seed)
    ks = jax.random.split(key, 25)
    D = D_MODEL
    nrm = lambda k, shape, scale: jax.random.normal(k, shape, jnp.float32) * scale
    gain = lambda k, shape: 1.0 + 0.02 * jax.random.normal(k, shape, jnp.float32)
    dt0 = jnp.exp(jax.random.uniform(ks[17], (DEPTH, 2, SSM_HEADS), jnp.float32, math.log(1e-3), math.log(1e-1)))
    dt_bias = dt0 + jnp.log(-jnp.expm1(-dt0))
    a_log = jnp.log(jax.random.uniform(ks[18], (DEPTH, 2, SSM_HEADS), jnp.float32, 1.0, 16.0))
    return {
        "x": nrm(ks[0], (BATCH, SEQ, D), 1.0),
        "c": nrm(ks[1], (BATCH, D), 1.0),
        "ctx": nrm(ks[2], (BATCH, CTX_LEN, D), 1.0),
        "c_ctx": nrm(ks[3], (D,), 1.0),
        "w_ada": nrm(ks[4], (DEPTH, D, 6 * D), 0.5 * D ** -0.5),
        "b_ada": nrm(ks[5], (DEPTH, 6 * D), 0.01),
        "norm1_g": gain(ks[6], (DEPTH, D)),
        "norm2_g": gain(ks[7], (DEPTH, D)),
        "w_in": nrm(ks[8], (DEPTH, D, IN_COLS), D ** -0.5),
        "mla_qa_g": gain(ks[9], (DEPTH, MLA_Q_RANK)),
        "mla_wqb": nrm(ks[10], (DEPTH, MLA_Q_RANK, MLA_HEADS * MLA_QK), MLA_Q_RANK ** -0.5),
        "mla_kva_g": gain(ks[11], (DEPTH, MLA_KV_RANK)),
        "mla_wkvb": nrm(ks[12], (DEPTH, MLA_KV_RANK, MLA_HEADS * (MLA_NOPE + MLA_V)), MLA_KV_RANK ** -0.5),
        "hg_lb_logits": nrm(ks[13], (DEPTH, 2, HG_W), 0.1),
        "hg_norm_g": gain(ks[14], (DEPTH, HG_HEADS * HG_DV)),
        "ssm_conv_w": nrm(ks[15], (DEPTH, SSM_CONV, SSM_XBC), SSM_CONV ** -0.5),
        "ssm_conv_b": nrm(ks[16], (DEPTH, SSM_XBC), 0.01),
        "ssm_dt_bias": dt_bias,
        "ssm_a_log": a_log,
        "ssm_d": gain(ks[19], (DEPTH, SSM_HEADS)),
        "ssm_norm_g": gain(ks[20], (DEPTH, SSM_INNER)),
        "w_out": nrm(ks[21], (DEPTH, MIX_WIDTH, D), MIX_WIDTH ** -0.5),
        "w_ffn_in": nrm(ks[22], (DEPTH, D, 2 * FFN_HIDDEN), D ** -0.5),
        "w_ffn_out": nrm(ks[23], (DEPTH, FFN_HIDDEN, D), FFN_HIDDEN ** -0.5),
        "final_g": gain(ks[24], (D,)),
    }

def reference(x, c, ctx, c_ctx, w_ada, b_ada, norm1_g, norm2_g, w_in, mla_qa_g, mla_wqb, mla_kva_g,
              mla_wkvb, hg_lb_logits, hg_norm_g, ssm_conv_w, ssm_conv_b, ssm_dt_bias, ssm_a_log, ssm_d,
              ssm_norm_g, w_out, w_ffn_in, w_ffn_out, final_g):
    n = x.shape[1]
    cos, sin = axial_rope_tables(n)
    lb_soft = jax.nn.softmax(hg_lb_logits.astype(jnp.float32), axis=0)
    lb_all = jnp.cumsum(lb_soft, axis=0) - lb_soft[0]
    silu_c = jax.nn.silu(c)
    silu_cc = jax.nn.silu(c_ctx)
    o1 = MLA_COLS
    o2 = MLA_COLS + HG_COLS
    h_ctx = ctx
    for l in range(DEPTH):
        ctx_out = l < DEPTH - 1
        mod = (silu_c @ w_ada[l] + b_ada[l])[:, None, :]
        modc = silu_cc @ w_ada[l] + b_ada[l]
        sh1, sc1, g1, sh2, sc2, g2 = jnp.split(mod, 6, axis=-1)
        csh1, csc1, cg1, csh2, csc2, cg2 = jnp.split(modc, 6, axis=-1)
        p = modulate(rms_norm(x, norm1_g[l]), sh1, sc1) @ w_in[l]
        pc = modulate(rms_norm(h_ctx, norm1_g[l]), csh1, csc1) @ w_in[l]
        a_lat, a_ctx = mla_mixer(pc[..., :o1], p[..., :o1], mla_qa_g[l], mla_wqb[l], mla_kva_g[l],
                                 mla_wkvb[l], cos, sin, ctx_out)
        r_lat, r_ctx = hgrn_mixer(pc[..., o1:o2], p[..., o1:o2], lb_all[l, 0], lb_all[l, 1], hg_norm_g[l], ctx_out)
        s_lat, s_ctx = ssm_mixer(pc[..., o2:], p[..., o2:], ssm_conv_w[l], ssm_conv_b[l], ssm_dt_bias[l],
                                 ssm_a_log[l], ssm_d[l], ssm_norm_g[l], ctx_out)
        x = x + g1 * (jnp.concatenate([a_lat, r_lat, s_lat], axis=-1) @ w_out[l])
        x = x + g2 * swiglu(modulate(rms_norm(x, norm2_g[l]), sh2, sc2), w_ffn_in[l], w_ffn_out[l])
        if ctx_out:
            h_ctx = h_ctx + cg1 * (jnp.concatenate([a_ctx, r_ctx, s_ctx], axis=-1) @ w_out[l])
            h_ctx = h_ctx + cg2 * swiglu(modulate(rms_norm(h_ctx, norm2_g[l]), csh2, csc2), w_ffn_in[l], w_ffn_out[l])
    return rms_norm(x, final_g)


_drawn_inputs = setup_inputs


def setup_inputs(seed=0):
    import zlib

    import numpy as np

    out = dict(_drawn_inputs(seed))
    spreads = {}
    factors = {'ctx': 2.859,
     'b_ada': 3.626,
     'norm1_g': 7.57,
     'norm2_g': 6.613,
     'mla_qa_g': 8.0,
     'mla_kva_g': 8.0,
     'hg_lb_logits': 8.0,
     'hg_norm_g': 8.0,
     'ssm_conv_b': 64.0,
     'ssm_d': 64.0,
     'ssm_norm_g': 49.838,
     'final_g': 8.116}
    for name, (base, spread) in spreads.items():
        noise = np.random.default_rng([zlib.crc32(name.encode()), seed]).standard_normal(out[name].shape)
        drawn = base * np.exp(spread * noise) if base else spread * noise
        out[name] = __import__('jax').numpy.asarray(drawn.astype(out[name].dtype))
    for name, factor in factors.items():
        out[name] = (out[name] * factor).astype(out[name].dtype)
    return out
```

```python
from contextlib import ExitStack

import numpy as np

import concourse.bass as bass
from concourse import mybir

F32 = mybir.dt.float32
F16 = mybir.dt.float16
BF16 = mybir.dt.bfloat16
U8 = mybir.dt.uint8
ALU = mybir.AluOpType
ACT = mybir.ActivationFunctionType
AX = mybir.AxisListType

D = 1024
SEQ = 256
DEPTH = 2
GRID_W = 64
P = 128
T = 2 * SEQ
KD = D // P
HEADS, NOPE, ROPE, VD = 8, 64, 32, 64
QK = NOPE + ROPE
Q_RANK, KV_RANK = 384, 256
KQ, KKV = Q_RANK // P, KV_RANK // P
HG_HEADS, HG_W = 4, 256
SSM_HEADS, SSM_INNER, SSM_STATE, TAPS = 4, 256, 64, 5
FFN = 2816
KF = FFN // P
C = 128
NCH = T // C
MLA_COLS = Q_RANK + KV_RANK + ROPE
HG_COLS = 5 * HG_W
SSM_AT = MLA_COLS + HG_COLS
SCALE = QK ** -0.5
EPS = 1e-6
WS = 64.0
GATE_MAX = 44.0
N_ADA, N_IN, N_OUT, N_FI, N_FO = 24, 11, 4, KF, 8
UNIT = 2816
PAD = SEQ + TAPS - 1
HALVES = (64, 32, 16, 8, 4, 2, 1)
ORDER = ((0, 1, 2, 3), (1, 0, 3, 2))

V_BADA, V_N1, V_N2, V_QA, V_KVA, V_LB, V_HGN, V_CW, V_CB, V_DTB, V_ALOG, V_D, V_SN = (
    0, 48, 56, 64, 67, 69, 73, 75, 95, 99, 100, 101, 103)
V_LAYER = 105
V_FINAL = DEPTH * V_LAYER
V_C = V_FINAL + KD
V_COLS = V_C + 2 * KD
C_ID, C_ONES, C_B64, C_RESET, C_MF, C_MB, C_SEL, C_SELT, C_COS, C_SIN, C_PERM, C_SGN = (
    0, 128, 256, 384, 896, 1024, 1152, 2176, 2688, 2944, 3200, 3328)
C_COLS = C_SGN + 6

R_QL, R_KV, R_MISC, R_HQ, R_FF, R_IV, R_OG, R_Z, R_XBC, R_T = (
    0, 1536, 2560, 3072, 4096, 6144, 7168, 8192, 9216, 11296)
R_SIZE = R_T + 9728


def unit_order():
    us = [("ada", 0, i) for i in range(8)]
    rest = [("ada", 0, i) for i in range(8, N_ADA)]
    for i in range(N_IN):
        us.append(("in", 0, i))
        us += rest[:2 if i < 5 else 1]
        rest = rest[2 if i < 5 else 1:]
    us += [("qb", 0, 0), ("kvb", 0, 0)] + [("out", 0, i) for i in range(N_OUT)]
    for i in range(N_FI):
        us += [("fi", 0, i), ("ada", 1, i)]
    for i in range(N_FO):
        us.append(("fo", 0, i))
        if i < N_ADA - N_FI:
            us.append(("ada", 1, N_FI + i))
    us += [("in", 1, i) for i in range(N_IN)] + [("qb", 1, 0), ("kvb", 1, 0)]
    us += [("out", 1, i) for i in range(N_OUT)] + [("fi", 1, i) for i in range(N_FI)]
    us += [("fo", 1, i) for i in range(N_FO)]
    return us


UNITS = unit_order()
AT_UNIT = {u: n for n, u in enumerate(UNITS)}
SIZE = {"ada": 2048, "in": 2048, "qb": KQ * 768, "kvb": KKV * 1024, "out": 2048, "fi": 2048, "fo": 11 * 256}
KT = {"ada": KD, "in": KD, "qb": KQ, "kvb": KKV, "out": KD, "fi": KD, "fo": 11}
GROUPS = [u for u in UNITS if u[0] in ("in", "out", "fi") or (u[0] == "fo" and u[2] % 2 == 0)]
AT_GROUP = {u: n for n, u in enumerate(GROUPS)}
IN_TILES = (("kv1", "misc"), ("xs0", "xs1"), ("B", "C"), ("z0", "z1"), ("q0", "q1"), ("ff0", "ff1"),
            ("fb0", "fb1"), ("og0", "og1"), ("iv", "iv"), ("ql0", "ql1"), ("ql2", "kv0"))
LAT_ONLY = ("C", "z0", "z1", "q0", "q1", "og0", "og1", "ql0", "ql1", "ql2")


FIRST = {"xw": 6, "krdma": 16, "ssq1": 1, "tr": 2, "cb": 4, "bcr": 1, "stp": 1, "rows_bc": 4, "y": 4, "yss": 2,
         "gKt": 1, "gSp": 1, "gO": 1, "gP": 16, "go": 1, "gss": 2, "lss": 5, "krp": 1, "qp": 12, "qrp": 2,
         "smx": 32, "mT": 1, "st": 32, "pv": 8, "ssq2": 1, "sq1": 8, "rstd1": 1, "xhi1": 16, "dsp": 1, "wexp": 2,
         "cth": 4, "tra": 1, "E_ssm": 8, "ysq": 2, "yrs": 2, "yhi": 2, "gl": 2, "gKe": 5, "gKe2": 4, "gE": 7,
         "gsq": 2, "grs": 2, "ghi": 2, "lsq": 5, "lrs": 2, "lhi": 5, "qb16": 2, "nm": 1, "ex": 32, "den": 8,
         "ohi": 4, "sq2": 8, "rstd2": 1, "xhi2": 16, "hhi": 22, "mod": 4, "tm1": 16, "xlo1": 16, "wrow": 2,
         "rowd": 2, "acc": 16, "conv": 7, "trv": 3, "cw": 8, "S_ssm": 24, "D": 32, "M": 8, "ym": 4, "ylo": 2,
         "gk": 1, "gT": 1, "gKa": 2, "gKm": 4, "gS": 24, "gA": 28, "gKQ": 8, "gAT": 32, "gm": 2, "glo": 2,
         "lh": 5, "llo": 5, "krc": 1, "qn": 6, "Kn": 4, "Vv": 4, "Qd": 8, "kb16": 2, "mx": 32, "on": 8, "olo": 4,
         "tm2": 16, "xlo2": 16, "hlo": 22}


class Layer:

    def __init__(self, signals, l):
        self.signals, self.l = signals, l

    def __getitem__(self, name):
        return self.signals[name]

    def __call__(self, name, n):
        return self.signals[name], (FIRST.get(name, 0) if self.l else 0) + n


def build(nc, w, vecs_d, consts_d, masks_d, x_d, out_d):
    with ExitStack() as ctx:
        def sb(name, shape, dt=F32):
            return ctx.enter_context(nc.sbuf_tensor(name, shape, dt))

        def sem(name):
            return ctx.enter_context(nc.semaphore(name))

        w32 = [sb(f"w32_{i}", [P, UNIT]) for i in range(2)]
        w16 = [sb(f"w16_{i}", [P, 2, UNIT], F16) for i in range(3)]
        xT = sb("xT", [P, KD, T])
        act16 = sb("act16", [P, 2, KD, T], F16)
        R = sb("R", [P, R_SIZE])
        vecs = sb("vecs_sb", [P, V_COLS])
        cst = sb("cst", [P, C_COLS])
        masks = sb("masks_sb", [P, 8, C], U8)
        S = sb("S", [P, 2, 3, 2, P])
        rows = sb("rows", [P, T])
        rstd = sb("rstd", [P, T])
        th = sb("th", [P, 2, T])
        mod = sb("mod", [P, DEPTH, 48, 2])
        aff = sb("aff", [P, DEPTH, 4, KD, 2])
        cs = sb("cs", [P, 2, KD, 2])
        cs16 = sb("cs16", [P, KD, 2, 2], F16)
        sel16 = sb("sel16", [8, 8, P], BF16)
        small = sb("small", [P, 128])
        rtok = sb("rtok", [P, NCH, 72])
        negm = sb("negm", [8, T], BF16)
        eps = small[:, 0:1]
        lb4, olb4 = small[:, 4:8], small[:, 8:12]
        lbt = small[:, 12:24]
        hcw = small[:, 24:44]
        hcb = small[:, 44:48]
        acol = small[0:8, 48:49]
        lastf = small[0:8, 50:54]
        lastb = small[0:8, 54:58]
        mcol = small[:, 64:96]
        ET = small[:, 96:112]
        one = small[:, 1:2]
        ED = small[:, 112:128]

        B = [ctx.enter_context(nc.psum_tensor(f"bank{i}", [P, 512], F32)) for i in range(8)]

        def rr(start, size, pat=None, **kw):
            v = R[:, start:start + size]
            return v.rearrange(pat, **kw) if pat else v

        def const(at, n, p=P):
            return cst[0:p, at:at + n]

        ident, ones, b64 = const(C_ID, P), const(C_ONES, P), const(C_B64, P)
        perm, reset = const(C_PERM, P), const(C_RESET, T)
        seqs = lambda ap: ap.rearrange("p (s t) -> p s t", s=2)

        def hi_w(n, k, c0, m):
            kind = UNITS[n][0]
            v = w16[n % 3][:, 0, 0:SIZE[kind]].rearrange("p (k c) -> p k c", k=KT[kind])
            return v[:, k, c0:c0 + m]

        def lo_w(n, k, c0, m):
            kind = UNITS[n][0]
            v = w16[n % 3][:, 1, 0:SIZE[kind]].rearrange("p (k c) -> p k c", k=KT[kind])
            return v[:, k, c0:c0 + m]

        params = sem("params_landed")
        x_in = sem("x_landed")
        landed = [sem(f"weights_landed{i}") for i in range(2)]
        w_hi = sem("weights_high")
        w_lo = sem("weights_low")
        prod = sem("unit_products")
        evac = sem("groups_evacuated")
        tanh_s = sem("group_tanh")
        setup = sem("setup_done")
        cs_t = sem("c_tanh")
        cs_v = sem("c_silu")
        masks_s = sem("masks_cast")
        ach = sem("scalar_chain")
        dch = sem("vector_chain")
        names = ("mod sq1 ssq1 rstd1 tm1 xhi1 xlo1 sq2 ssq2 rstd2 tm2 xhi2 xlo2 hhi hlo "
                 "acc cth conv dsp wrow wexp rowd tr trv tra cb bcr cw xw stp S_ssm rows_bc D E_ssm M y "
                 "ysq yss yrs ym yhi ylo "
                 "gl gk gT gKa gKe gKm gKt gKe2 gSp gS gO gA gE gKQ gP gAT go gsq gss grs gm ghi glo "
                 "lbd lbe qb16 kb16 lsq lss lrs lh lhi llo krc krp krdma qn qp qrp Qd Kn Vv smx mx mT nm st ex pv den on ohi olo"
                 ).split()
        signals = {n: sem(n) for n in names}
        L = [Layer(signals, l) for l in range(DEPTH)]
        fin = {n: sem(f"fin_{n}") for n in ("sq", "ssq", "rstd", "y", "out")}

        def t0_of(l):
            return 0 if l < DEPTH - 1 else SEQ

        def out_chunks(l):
            return range(0 if l < DEPTH - 1 else 2, NCH)

        def vec(l, at, n):
            return vecs[:, l * V_LAYER + at:l * V_LAYER + at + n]

        def act32_out():
            return rr(4096, KD * SEQ, "p (k t) -> p k t", k=KD)

        def norm_ops(l):
            return 2 if t0_of(l) == 0 else 1

        def max_copies():
            v = lambda at: rr(at, 2048).bitcast(BF16).rearrange("p (h t) -> p h t", h=HEADS)
            return v(R_HQ + 15872), v(R_HQ)

        def level_bufs(lv):
            at = R_T + 4096 if lv % 2 == 0 else R_XBC
            K = rr(at, 1024, "p (j t) -> p j t", j=2)
            Q = rr(at + 1024, 1024, "p (j t) -> p j t", j=2)
            if lv == len(HALVES):
                Q = rr(R_HQ, 1024, "p (j t) -> p j t", j=2)
            return K, Q

        def cvec():
            return vecs[:, V_C:V_C + 2 * KD].rearrange("p (k a) -> p k a", a=2)

        def h32(i):
            return rr(KF * T + (i % 2) * T, T)

        block = ctx.enter_context(nc.Block())

        @block.sync
        def _(sp):
            def load_unit(n):
                kind, l, i = UNITS[n]
                if n >= 2:
                    sp.wait_ge(w_hi, n - 1)
                    sp.wait_ge(w_lo, n - 1)
                sp.dma_start(w32[n % 2][:, 0:SIZE[kind]], w[kind][l, i]).then_inc(landed[n % 2], 16)

            sp.dma_start(vecs[:, :], vecs_d).then_inc(params, 16)
            load_unit(0)
            load_unit(1)
            sp.dma_start(cst[:, :], consts_d).then_inc(params, 16)
            sp.dma_start(rr(R_Z, 8 * C), masks_d).then_inc(params, 16)
            sp.dma_start(xT[:, :, :], x_d).then_inc(x_in, 16)
            for n in range(2, len(UNITS)):
                load_unit(n)
            sp.wait_ge(fin["y"], KD)
            sp.dma_start(out_d, act32_out()).then_inc(fin["out"], 16)
            sp.wait_ge(fin["out"], 16)

        @block.gpsimd
        def _(pool):
            pool.memset(S[:, :, :, :, :], 0.0).then_inc(setup, 1)
            pool.memset(rows[:, :], 0.0).then_inc(setup, 1)
            pool.memset(small[:, 0:1], EPS).then_inc(setup, 1)
            pool.memset(small[:, 1:2], 1.0).then_inc(setup, 1)
            for l in range(DEPTH):
                s = L[l]
                xtok = rr(R_T, 1024, "p (c h d) -> p c h d", c=NCH, h=SSM_HEADS)
                xw = rr(R_T + 6656, 1536, "p (n h d) -> p n h d", n=6, h=SSM_HEADS)
                pool.wait_ge(*s("tra", 1))
                pool.wait_ge(*s("trv", 3))
                for d in range(2):
                    for i in range(3):
                        c = ORDER[d][i]
                        wt = rtok[:, c, 64 + 4 * d:68 + 4 * d]
                        pool.tensor_tensor(xw[:, 3 * d + i, :, :], xtok[:, c, :, :],
                                           wt.unsqueeze(2).to_broadcast([P, SSM_HEADS, 64]),
                                           ALU.mult).then_inc(s["xw"], 1)
                pool.wait_ge(*s("krc", 1))
                KTt = rr(R_HQ + 6656, 4096, "p (h t) -> p h t", h=HEADS)
                pool.dma_start(KTt[NOPE:QK, :, :], rr(R_MISC, T)[0:ROPE, :].unsqueeze(1).to_broadcast([ROPE, HEADS, T])
                               ).then_inc(s["krdma"], 16)

        @block.tensor
        def _(pe):
            def mm3(ps, ahi, alo, bhi, blo, first, last):
                pe.matmul(ps, ahi, bhi, start=first, stop=False, skip_group_check=True)
                pe.matmul(ps, ahi, blo, start=False, stop=False, skip_group_check=True)
                return pe.matmul(ps, alo, bhi, start=False, stop=last, skip_group_check=True)

            def mm(ps, a, b, start=True, stop=True):
                return pe.matmul(ps, a, b, start=start, stop=stop, skip_group_check=True)

            def unit_ready(n):
                pe.wait_ge(w_hi, n + 1)
                pe.wait_ge(w_lo, n + 1)

            def ada(l, i):
                n = AT_UNIT["ada", l, i]
                unit_ready(n)
                if (l, i) == (0, 0):
                    pe.wait_ge(cs_t, 2)
                    pe.wait_ge(cs_v, 2)
                if (l, i) == (0, 8):
                    pe.wait_ge(*L[0]("mod", 2))
                if (l, i) == (1, 0):
                    pe.wait_ge(*L[0]("mod", 4))
                for m in range(2):
                    at = 4 * (2 * i + m)
                    for k in range(KD):
                        mm(B[7][:, at:at + 4], hi_w(n, k, m * P, P), cs16[:, k, :, :].rearrange("p a b -> p (a b)"),
                           k == 0, False)
                        last = mm(B[7][:, at:at + 2], lo_w(n, k, m * P, P), cs16[:, k, 0, :], False, k == KD - 1)
                last.then_inc(prod, 1)

            def group_banks(u):
                g = AT_GROUP[u]
                if g >= 2:
                    pe.wait_ge(evac, g - 1)
                return B[2 * (g % 2)], B[2 * (g % 2) + 1]

            def norm(s, q, t0):
                for k in range(KD):
                    pe.wait_ge(*s("sq" + q, k + 1))
                    last = mm(B[6][:, t0:T], ones, rr(k * T + t0, T - t0), k == 0, k == KD - 1)
                last.then_inc(s["ssq" + q], 1)

            def inproj(l, i):
                s, t0 = L[l], t0_of(l)
                n = AT_UNIT["in", l, i]
                banks = group_banks(("in", l, i))
                unit_ready(n)
                for m, name in enumerate(IN_TILES[i]):
                    a = t0 if name in LAT_ONLY else 0
                    for k in range(KD):
                        if i == 0 and m == 0:
                            pe.wait_ge(*s("xhi1", 2 * k + 2))
                            pe.wait_ge(*s("xlo1", 2 * k + 2))
                        if name != "iv":
                            M = 40 if name == "misc" else P
                            last = mm3(banks[m][0:M, a:T], hi_w(n, k, m * P, M), lo_w(n, k, m * P, M),
                                       act16[:, 0, k, a:T], act16[:, 1, k, a:T], k == 0, k == KD - 1)
                    if name == "iv":
                        for c in (2 * m, 2 * m + 1):
                            for k in range(KD):
                                last = mm3(banks[m][:, (c % 2) * 256:(c % 2) * 256 + 256],
                                           act16[:, 0, k, c * C:c * C + C], act16[:, 1, k, c * C:c * C + C],
                                           hi_w(n, k, 0, 256), lo_w(n, k, 0, 256), k == 0, k == KD - 1)
                last.then_inc(prod, 1)

            def ssm(l):
                s, OC = L[l], out_chunks(l)
                pe.wait_ge(evac, AT_GROUP["in", l, N_IN - 1] + 1)
                xs = rr(R_T + 4096, 1024, "p (g t) -> p g t", g=2)
                Bf = rr(R_T + 5120, 512)
                Cd = rr(R_T + 5632, 1024, "p (g t) -> p g t", g=2)
                xtok = rr(R_T, 1024, "p (c f) -> p c f", c=NCH)
                btok = rr(R_T + 1024, 1024, "p (c f) -> p c f", c=NCH)
                xw = rr(R_T + 6656, 1536, "p (n h d) -> p n h d", n=6, h=SSM_HEADS)
                Cw = rr(R_T + 2048, 2048, "p (d g t) -> p d g t", d=2, g=2)
                Mx = rr(R_XBC, 1024, "p (b h t) -> p b h t", b=2, h=SSM_HEADS)
                OE = rr(R_T + 6656 + 5 * 512, 512)
                pe.wait_ge(*s("conv", 7))
                for j in range(3):
                    for c in range(NCH):
                        src = (xs[:, j, :] if j < 2 else Bf)[:, c * C:c * C + C]
                        last = pe.transpose(B[4 + j][:, c * C:c * C + C], src, ident)
                last.then_inc(s["tr"], 1)
                pe.wait_ge(*s("rowd", 2))
                for c in range(NCH):
                    last = pe.transpose(B[0][:, c * C:c * C + 72], rows[0:72, c * C:c * C + C], const(C_ID, 72, 72))
                last.then_inc(s["tr"], 1)
                for c in range(NCH):
                    for g in range(2):
                        gs = slice(64 * g, 64 * g + 64)
                        if c in OC:
                            last = mm(B[1 + g][:, c * C:c * C + C],
                                      Bf[gs, c * C:c * C + C], Cd[gs, g, c * C:c * C + C])
                last.then_inc(s["cb"], 1)
                pe.wait_ge(*s("tra", 1))
                pe.wait_ge(*s("trv", 3))
                pe.wait_ge(*s("wexp", 2))
                for d, g, b in ((0, 0, 3), (0, 1, 0), (1, 0, 4), (1, 1, 5)):
                    last = mm(B[b][:, :], const(C_SELT + (2 * d + g) * P, P, 8), OE[0:8, :])
                    last.then_inc(s["cb"], 1) if (d, g) != (1, 1) else last.then_inc(s["bcr"], 1)
                pe.wait_ge(*s("cw", 8))
                pe.wait_ge(*s("xw", 6))
                for d, g, b in ((0, 0, 3), (0, 1, 0), (1, 0, 4), (1, 1, 5)):
                    for i in range(3):
                        c = ORDER[d][i]
                        last = mm(B[b][:, i * P:i * P + P], btok[:, c, g * P:g * P + P],
                                  xw[:, 3 * d + i, 2 * g:2 * g + 2, :].rearrange("p h d -> p (h d)"))
                last.then_inc(s["stp"], 1)
                pe.wait_ge(*s("S_ssm", 24))
                yb = (B[6], B[3])
                for g in range(2):
                    first = True
                    for c in OC:
                        for d in range(2):
                            i = ORDER[d].index(c) - 1
                            if i >= 0:
                                mm(yb[g][:, c * C:c * C + C], S[:, d, i, g, :], Cw[:, d, g, c * C:c * C + C],
                                   first, False)
                                first = False
                for n, c in enumerate(OC):
                    if n >= 1:
                        pe.wait_ge(*s("D", 8 * n))
                    for d in range(2):
                        for h in range(SSM_HEADS):
                            last = mm(B[4 + d][:, h * C:h * C + C], const(C_SEL + (4 * d + h) * P, P, 8),
                                      rows[0:8, c * C:c * C + C])
                    last.then_inc(s["rows_bc"], 1)
                    pe.wait_ge(*s("M", 2 * n + 2))
                    for h in range(SSM_HEADS):
                        r = 64 * (h % 2)
                        last = mm(yb[h // 2][r:r + 64, c * C:c * C + C], xtok[:, c, 64 * h:64 * h + 64],
                                  Mx[:, n % 2, h, :], False, True)
                    last.then_inc(s["y"], 1)
                t0 = t0_of(l)
                for g in range(2):
                    pe.wait_ge(*s("ysq", g + 1))
                    mm(B[4 + g][:, t0:T], ones, rr(R_XBC + 1024 + g * T + t0, T - t0)).then_inc(s["yss"], 1)

            def hgrn(l):
                s, OC, t0 = L[l], out_chunks(l), t0_of(l)
                KP = rr(R_T + 2048, 2048, "p (d j t) -> p d j t", d=2, j=2)
                QI = rr(R_T + 4096, 2048, "p (d j t) -> p d j t", d=2, j=2)
                KtT = rr(R_T + 8192, 1536, "p (d j i t) -> p d j i t", d=2, j=2, i=3)
                AT = rr(R_T + 6144, 2048, "p (c h t) -> p c h t", c=NCH, h=HG_HEADS)
                iv = rr(R_IV, 1024, "p (c f) -> p c f", c=NCH)
                pe.wait_ge(*s("gKm", 2))
                for d in range(2):
                    for j in range(2):
                        for i in range(3):
                            c = ORDER[d][i]
                            last = pe.transpose(B[2 * d + j][:, i * P:i * P + P], KP[:, d, j, c * C:c * C + C], ident)
                last.then_inc(s["gKt"], 1)
                pe.wait_ge(*s("gKe2", 4))
                pe.wait_ge(*s("ym", 4))
                for d, j, b in ((0, 0, 4), (0, 1, 5), (1, 0, 6), (1, 1, 0)):
                    for i in range(3):
                        c = ORDER[d][i]
                        last = mm(B[b][:, i * P:i * P + P], KtT[:, d, j, i, :], iv[:, c, j * P:j * P + P])
                last.then_inc(s["gSp"], 1)
                pe.wait_ge(*s("gS", 24))
                pe.wait_ge(*s("gKm", 4))
                for j in range(2):
                    first = True
                    for c in OC:
                        for d in range(2):
                            i = ORDER[d].index(c) - 1
                            if i >= 0:
                                last = mm(B[1 + j][:, c * C:c * C + C], S[:, d, i, j, :], QI[:, d, j, c * C:c * C + C],
                                          first, False)
                                first = False
                last.then_inc(s["gO"], 1)
                n = 0
                for lv in range(len(HALVES) + 1):
                    K, Q = level_bufs(lv)
                    pe.wait_ge(*s("gKQ", lv + 1))
                    for c2 in range(OC[0] // 2, 2):
                        if n >= 2:
                            pe.wait_ge(*s("gAT", 2 * n - 2))
                        for c in (2 * c2, 2 * c2 + 1):
                            for h in range(HG_HEADS):
                                hs = slice(64 * (h % 2), 64 * (h % 2) + 64)
                                to = 256 * (c % 2) + C * (h // 2)
                                last = mm(B[3 + 2 * (n % 2) + h % 2][:, to:to + C], K[hs, h // 2, c * C:c * C + C],
                                          Q[hs, h // 2, c * C:c * C + C])
                        last.then_inc(s["gP"], 1)
                        n += 1
                pe.wait_ge(*s("gAT", 2 * n))
                for c in OC:
                    for h in range(HG_HEADS):
                        r = 64 * (h % 2)
                        last = mm(B[1 + h // 2][r:r + 64, c * C:c * C + C], iv[:, c, 64 * h:64 * h + 64],
                                  AT[:, c, h, :], False, True)
                last.then_inc(s["go"], 1)
                for j in range(2):
                    pe.wait_ge(*s("gsq", j + 1))
                    mm(B[3 + j][:, t0:T], b64, rr(R_T + 2048 + j * T + t0, T - t0)).then_inc(s["gss"], 1)

            def mla(l):
                s, t0 = L[l], t0_of(l)
                lat16 = rr(R_HQ, 2560).bitcast(F16).rearrange("p (a k t) -> p a k t", a=2, k=5)
                QT = rr(R_HQ + 2560, 4096, "p (h t) -> p h t", h=HEADS)
                KTt = rr(R_HQ + 6656, 4096, "p (h t) -> p h t", h=HEADS)
                V = rr(R_HQ + 10752, 4096, "p (c h v) -> p c h v", c=NCH, h=HEADS)
                qr = rr(R_HQ + 14848, 1024, "p (j t) -> p j t", j=2)
                PT = rr(R_QL, 3072, "p (b x) -> p b x", b=2)
                pe.wait_ge(*s("gm", 2))
                for k in range(KQ + KKV):
                    pe.wait_ge(*s("lsq", k + 1))
                    b, a = (5, t0) if k < KQ else (6, 0)
                    mm(B[b][:, a:T], ones, rr(R_HQ + 14848 + (k % 2) * T + a, T - a), k in (0, KQ),
                       k in (KQ - 1, KQ + KKV - 1)).then_inc(s["lss"], 1)
                pe.wait_ge(params, 48)
                mm(B[4][0:ROPE, 0:SEQ], const(C_PERM, ROPE, ROPE), rr(R_MISC, T)[0:ROPE, SEQ:T]).then_inc(s["krp"], 1)
                n = AT_UNIT["qb", l, 0]
                unit_ready(n)
                pe.wait_ge(*s("lhi", KQ))
                pe.wait_ge(*s("llo", KQ))
                for m in range(6):
                    if m >= 4:
                        pe.wait_ge(*s("qn", m - 3))
                    for k in range(KQ):
                        last = mm3(B[m % 4][:, t0:T], hi_w(n, k, m * P, P), lo_w(n, k, m * P, P),
                                   lat16[:, 0, k, t0:T], lat16[:, 1, k, t0:T], k == 0, k == KQ - 1)
                    last.then_inc(s["qp"], 1) if m < 5 else last.then_inc(prod, 1)
                n = AT_UNIT["kvb", l, 0]
                unit_ready(n)
                pe.wait_ge(*s("lhi", KQ + KKV))
                pe.wait_ge(*s("llo", KQ + KKV))
                pe.wait_ge(*s("lrs", 2))
                pe.wait_ge(*s("krc", 1))
                kb = (2, 3, 5, 6, 0, 1, 2, 3)
                for m in range(8):
                    if m < 2:
                        pe.wait_ge(*s("qn", m + 3))
                    if m == 4:
                        pe.wait_ge(*s("qn", 6))
                    if m >= 6:
                        pe.wait_ge(*s("Kn", m - 5))
                    for k in range(KKV):
                        kh, kl = lat16[:, 0, KQ + k, :], lat16[:, 1, KQ + k, :]
                        if m < 4:
                            last = mm3(B[kb[m]][:, :], hi_w(n, k, m * P, P), lo_w(n, k, m * P, P), kh, kl,
                                       k == 0, k == KKV - 1)
                        else:
                            c = slice((m - 4) * C, (m - 4) * C + C)
                            last = mm3(B[kb[m]][:, :], kh[:, c], kl[:, c], hi_w(n, k, 512, 512), lo_w(n, k, 512, 512),
                                       k == 0, k == KKV - 1)
                    last.then_inc(s["qp"], 1) if m < 7 else last.then_inc(prod, 1)
                pe.wait_ge(*s("Kn", 4))
                for j in range(2):
                    mm(B[5 + j][:, 0:SEQ], perm, qr[:, j, SEQ:T]).then_inc(s["qrp"], 1)
                Qb, Kb = max_copies()
                pe.wait_ge(*s("Vv", 4))
                pe.wait_ge(*s("qb16", 2))
                pe.wait_ge(*s("kb16", 2))
                n = 0
                for qt in range(t0 // P, T // P):
                    keys = SEQ if qt < 2 else T
                    for h in range(HEADS):
                        if n >= 4:
                            pe.wait_ge(*s("mx", n - 3))
                        mm(B[n % 4][:, 0:keys], Qb[0:QK, h, qt * P:qt * P + P],
                           Kb[0:QK, h, 0:keys]).then_inc(s["smx"], 1)
                        n += 1
                pe.wait_ge(*s("mx", n))
                for i, qt in enumerate(range(t0 // P, T // P)):
                    last = pe.transpose(B[4][0:8, qt * P:qt * P + P], mcol[:, 8 * qt:8 * qt + 8], ident)
                last.then_inc(s["mT"], 1)
                pe.wait_ge(*s("nm", 1))
                for h in range(HEADS + 1):
                    if h < HEADS:
                        for kt in range(NCH):
                            a = t0 if kt < 2 else SEQ
                            st = B[kt][:, a:T]
                            if h >= 1:
                                pe.wait_ge(*s("ex", 4 * (h - 1) + kt + 1))
                            mm(st, KTt[0:QK, h, kt * C:kt * C + C], QT[0:QK, h, a:T], True, False)
                            mm(st, sel16[:, h, :], negm[:, a:T], False, True).then_inc(s["st"], 1)
                    if h >= 1:
                        g = h - 1
                        ob = B[5 + g % 2]
                        if g >= 2:
                            pe.wait_ge(*s("on", g - 1))
                        for kt in range(NCH):
                            a = t0 if kt < 2 else SEQ
                            pe.wait_ge(*s("ex", 4 * g + kt + 1))
                            off = 512 * kt if kt < 2 else 1024 + 256 * (kt - 2) - SEQ
                            last = mm(ob[:, a:T], V[:, kt, g, :], PT[:, g % 2, off + a:off + T],
                                      kt == 0, kt == NCH - 1)
                        last.then_inc(s["pv"], 1)

            def outproj(l):
                s, t0 = L[l], t0_of(l)
                for i in range(N_OUT):
                    n = AT_UNIT["out", l, i]
                    banks = group_banks(("out", l, i))
                    unit_ready(n)
                    if i == 0:
                        pe.wait_ge(*s("ohi", 4))
                        pe.wait_ge(*s("olo", 4))
                        pe.wait_ge(*s("ghi", 2))
                        pe.wait_ge(*s("glo", 2))
                        pe.wait_ge(*s("yhi", 2))
                        pe.wait_ge(*s("ylo", 2))
                    for m in range(2):
                        for k in range(KD):
                            last = mm3(banks[m][:, t0:T], hi_w(n, k, m * P, P), lo_w(n, k, m * P, P),
                                       act16[:, 0, k, t0:T], act16[:, 1, k, t0:T], k == 0, k == KD - 1)
                    last.then_inc(prod, 1)

            def ffn(l):
                s, t0 = L[l], t0_of(l)
                h16 = rr(0, KF * T).bitcast(F16).rearrange("p (a k t) -> p a k t", a=2, k=KF)
                for i in range(N_FI):
                    n = AT_UNIT["fi", l, i]
                    banks = group_banks(("fi", l, i))
                    unit_ready(n)
                    for m in range(2):
                        for k in range(KD):
                            if i == 0 and m == 0:
                                pe.wait_ge(*s("xhi2", norm_ops(l) * (k + 1)))
                                pe.wait_ge(*s("xlo2", norm_ops(l) * (k + 1)))
                            last = mm3(banks[m][:, t0:T], hi_w(n, k, m * P, P), lo_w(n, k, m * P, P),
                                       act16[:, 0, k, t0:T], act16[:, 1, k, t0:T], k == 0, k == KD - 1)
                    last.then_inc(prod, 1)
                    if l == 0:
                        ada(1, i)
                for i in range(N_FO):
                    n = AT_UNIT["fo", l, i]
                    if i % 2 == 0:
                        banks = group_banks(("fo", l, i))
                    unit_ready(n)
                    for m in range(2):
                        for k in range(11):
                            kf = 11 * (i % 2) + k
                            if i < 2 and m == 0:
                                pe.wait_ge(*s("hhi", kf + 1))
                                pe.wait_ge(*s("hlo", kf + 1))
                            last = mm3(banks[m][:, t0:T], hi_w(n, k, m * P, P), lo_w(n, k, m * P, P),
                                       h16[:, 0, kf, t0:T], h16[:, 1, kf, t0:T], kf == 0, kf == KF - 1)
                    last.then_inc(prod, 1)
                    if l == 0 and i < N_ADA - N_FI:
                        ada(1, N_FI + i)

            pe.wait_ge(params, 48)
            for i in range(8):
                ada(0, i)
            nxt = 8
            for l in range(DEPTH):
                norm(L[l], "1", 0)
                for i in range(N_IN):
                    inproj(l, i)
                    if l == 0:
                        for _ in range(2 if i < 5 else 1):
                            ada(0, nxt)
                            nxt += 1
                ssm(l)
                hgrn(l)
                mla(l)
                outproj(l)
                norm(L[l], "2", t0_of(l))
                ffn(l)
            for k in range(KD):
                pe.wait_ge(fin["sq"], k + 1)
                last = mm(B[6][:, 0:SEQ], ones, rr(k * SEQ, SEQ), k == 0, k == KD - 1)
            last.then_inc(fin["ssq"], 1)

        @block.scalar
        def _(act):
            chain = [0]

            def link(ins):
                chain[0] += 1
                ins.then_inc(ach, 1)
                act.wait_ge(ach, chain[0])

            def high(n):
                kind = UNITS[n][0]
                act.wait_ge(landed[n % 2], 16 * (n // 2 + 1))
                if n >= 3:
                    act.wait_ge(prod, n - 2)
                act.activation(w16[n % 3][:, 0, 0:SIZE[kind]], w32[n % 2][:, 0:SIZE[kind]], ACT.Copy,
                               scale=WS).then_inc(w_hi, 1)

            def ahead(u):
                if AT_UNIT[u] + 2 < len(UNITS):
                    high(AT_UNIT[u] + 2)

            def rsqrt_mean(out, ps, width, done):
                link(act.activation(out, ps, ACT.Ln, bias=eps, scale=1.0 / width))
                act.activation(out, out, ACT.Exp, scale=-0.5).then_inc(done, 1)

            def norm(l, q, t0, group_of):
                s = L[l]
                for k in range(KD):
                    if group_of is not None:
                        act.wait_ge(evac, AT_GROUP[group_of(k)] + 1)
                    act.activation(rr(k * T + t0, T - t0), xT[:, k, t0:T], ACT.Square).then_inc(s["sq" + q], 1)
                act.wait_ge(*s("ssq" + q, 1))
                rsqrt_mean(rstd[:, t0:T], B[6][:, t0:T], D, s["rstd" + q])
                m = 0
                for k in range(KD):
                    for sq in range(t0 // SEQ, 2):
                        m += 1
                        act.wait_ge(*s("tm" + q, m))
                        a = slice(sq * SEQ, sq * SEQ + SEQ)
                        act.activation(act16[:, 0, k, a], rr(4096 + k * T, T)[:, a], ACT.Identity,
                                       bias=mod[:, l, (0 if q == "1" else 24) + k, 1 - sq:2 - sq]
                                       ).then_inc(s["xhi" + q], 1)

            def inproj(l, i):
                t0 = t0_of(l)
                ahead(("in", l, i))
                if l == 0:
                    for _ in range(2 if i < 5 else 1):
                        ahead(("ada", 0, nxt[0]))
                        nxt[0] += 1
                if IN_TILES[i][0] in ("z0", "q0", "og0"):
                    act.wait_ge(prod, AT_UNIT["in", l, i] + 1)
                    g = AT_GROUP["in", l, i]
                    act.wait_ge(evac, g)
                    for m in range(2):
                        last = act.activation(th[:, m, t0:T], B[2 * (g % 2) + m][:, t0:T], ACT.Tanh, scale=0.5 / WS)
                    last.then_inc(tanh_s, 1)
                if i == 1:
                    dt_rows(l)
                if i == 3:
                    act.wait_ge(*L[l]("acc", 16))
                    cth = rr(R_T + 2048, 2048, "p (j t) -> p j t", j=4)
                    acc = rr(R_T, 2048, "p (j t) -> p j t", j=4)
                    for j in range(4):
                        a = t0 if j == 3 else 0
                        act.activation(cth[:, j, a:T], acc[:, j, a:T], ACT.Tanh).then_inc(L[l]["cth"], 1)

            def dt_rows(l):
                s = L[l]
                r = lambda i: rr(R_T + 6656 + 512 * i, 512)[0:8, :]
                act.wait_ge(evac, AT_GROUP["in", l, 0] + 1)
                link(act.activation(r(1), r(0), ACT.Abs))
                link(act.activation(r(1), r(1), ACT.Exp, scale=-1.0))
                act.activation(acol, vec(l, V_ALOG, 1)[0:8, :], ACT.Exp)
                act.activation(r(1), r(1), ACT.Ln, bias=one[0:8, :]).then_inc(s["dsp"], 1)
                act.wait_ge(*s("wrow", 2))
                act.activation(r(0), r(0), ACT.Exp).then_inc(s["wexp"], 1)
                act.activation(r(5), r(5), ACT.Exp).then_inc(s["wexp"], 1)

            nxt = [8]

            def ssm(l):
                s, t0, OC = L[l], t0_of(l), out_chunks(l)
                xtok = rr(R_T, 1024, "p (c g f) -> p c g f", c=NCH, g=2)
                act.wait_ge(*s("tr", 1))
                act.activation(xtok[:, :, 0, :], B[4][:, :].rearrange("p (c f) -> p c f", c=NCH), ACT.Copy)
                act.activation(xtok[:, :, 1, :], B[5][:, :].rearrange("p (c f) -> p c f", c=NCH),
                               ACT.Copy).then_inc(s["tra"], 1)
                Dx = rr(R_XBC + 1024, 1024)
                for n, c in enumerate(OC):
                    for d in range(2):
                        act.wait_ge(*s("D", 8 * n + 4 * d + 4))
                        act.activation(Dx[:, 512 * d:512 * d + 512], Dx[:, 512 * d:512 * d + 512], ACT.Exp,
                                       scale=1.0 if d == 0 else -1.0).then_inc(s["E_ssm"], 1)
                yz = rr(R_XBC, 1024, "p (g t) -> p g t", g=2)
                ysq = rr(R_XBC + 1024, 1024, "p (g t) -> p g t", g=2)
                for g in range(2):
                    act.wait_ge(*s("ym", g + 1))
                    act.activation(ysq[:, g, t0:T], yz[:, g, t0:T], ACT.Square).then_inc(s["ysq"], 1)
                for g in range(2):
                    act.wait_ge(*s("yss", g + 1))
                    rsqrt_mean(th[:, g, t0:T], B[4 + g][:, t0:T], P, s["yrs"])
                for g in range(2):
                    act.wait_ge(*s("ym", g + 3))
                    act.activation(act16[:, 0, 6 + g, t0:T], yz[:, g, t0:T], ACT.Copy).then_inc(s["yhi"], 1)

            def hgrn(l):
                s, t0, OC = L[l], t0_of(l), out_chunks(l)
                ff, E = rr(R_FF, 2048), rr(R_T + 2048, 2048)
                cum = rr(R_T, 2048, "p (d x) -> p d x", d=2)
                QI = rr(R_T + 4096, 2048, "p (d x) -> p d x", d=2)
                KtT = rr(R_T + 8192, 1536, "p (b x) -> p b x", b=4)
                act.wait_ge(*s("ylo", 2))
                if l:
                    act.wait_ge(*s("lbd", 1))
                    act.activation(lbt[:, 4:12], lbt[:, 4:12], ACT.Exp).then_inc(s["lbe"], 1)
                link(act.activation(E, ff, ACT.Exp))
                act.activation(E, E, ACT.Ln, bias=one).then_inc(s["gl"], 1)
                act.wait_ge(*s("gk", 1))
                if l == 0:
                    act.activation(ff, ff, ACT.Exp).then_inc(s["gl"], 1)
                else:
                    act.activation(ff, ff, ACT.Exp)
                    act.activation(E, E, ACT.Exp, scale=-1.0).then_inc(s["gl"], 1)
                    act.wait_ge(*s("gk", 5))
                    act.activation(E, E, ACT.Ln).then_inc(s["gl"], 1)
                act.wait_ge(*s("gT", 1))
                act.activation(ET, small[:, 96:112], ACT.Exp).then_inc(s["gKe"], 1)
                act.activation(QI[:, 0, :], cum[:, 0, :], ACT.Exp).then_inc(s["gKe"], 1)
                act.wait_ge(*s("gKa", 2))
                act.activation(E[:, 1024:2048], cum[:, 1, :], ACT.Exp).then_inc(s["gKe"], 1)
                act.activation(E[:, 0:1024], E[:, 0:1024], ACT.Exp).then_inc(s["gKe"], 1)
                act.activation(QI[:, 1, :], QI[:, 1, :], ACT.Exp).then_inc(s["gKe"], 1)
                act.wait_ge(*s("gKt", 1))
                for b in range(4):
                    act.activation(KtT[:, b, :], B[b][:, 0:384], ACT.Copy).then_inc(s["gKe2"], 1)
                E4 = rr(R_T + 2048, 2048, "p (d j t) -> p (d j) t", d=2, j=2)
                for lv in range(len(HALVES)):
                    act.wait_ge(*s("gA", 4 * lv + 4))
                    act.activation(E4[:, :, t0:T], E4[:, :, t0:T], ACT.Exp).then_inc(s["gE"], 1)
                sq = rr(R_T + 2048, 1024, "p (j t) -> p j t", j=2)
                r = rr(R_T + 3072, 1024, "p (j t) -> p j t", j=2)
                act.wait_ge(*s("go", 1))
                for j in range(2):
                    act.activation(sq[:, j, t0:T], B[1 + j][:, t0:T], ACT.Square).then_inc(s["gsq"], 1)
                for j in range(2):
                    act.wait_ge(*s("gss", j + 1))
                    rsqrt_mean(r[:, j, t0:T], B[3 + j][:, t0:T], 64, s["grs"])
                mx = rr(R_T + 4096, 1024, "p (j t) -> p j t", j=2)
                for j in range(2):
                    act.wait_ge(*s("gm", j + 1))
                    act.activation(act16[:, 0, 4 + j, t0:T], mx[:, j, t0:T], ACT.Copy).then_inc(s["ghi"], 1)

            def mla(l):
                s, t0 = L[l], t0_of(l)
                lat16 = rr(R_HQ, 2560).bitcast(F16).rearrange("p (a k t) -> p a k t", a=2, k=5)
                lh = rr(R_HQ + 10752, 2560, "p (k t) -> p k t", k=5)
                PT = rr(R_QL, 3072, "p (b x) -> p b x", b=2)
                QT = rr(R_HQ + 2560, 4096, "p (h t) -> p h t", h=HEADS)
                KTt = rr(R_HQ + 6656, 4096, "p (h t) -> p h t", h=HEADS)
                act.wait_ge(*s("glo", 2))
                for k in range(KQ + KKV):
                    a = t0 if k < KQ else 0
                    if k >= 2:
                        act.wait_ge(*s("lss", k - 1))
                    act.activation(rr(R_HQ + 14848 + (k % 2) * T + a, T - a), rr(R_QL + k * T + a, T - a),
                                   ACT.Square).then_inc(s["lsq"], 1)
                act.wait_ge(*s("lss", KQ))
                rsqrt_mean(th[:, 0, t0:T], B[5][:, t0:T], Q_RANK, s["lrs"])
                act.wait_ge(*s("lss", KQ + KKV))
                rsqrt_mean(th[:, 1, :], B[6][:, :], KV_RANK, s["lrs"])
                for k in range(KQ + KKV):
                    a = t0 if k < KQ else 0
                    act.wait_ge(*s("lh", k + 1))
                    act.activation(lat16[:, 0, k, a:T], lh[:, k, a:T], ACT.Copy).then_inc(s["lhi"], 1)
                ahead(("qb", l, 0))
                ahead(("kvb", l, 0))
                Qb, _ = max_copies()
                act.wait_ge(*s("Qd", 8))
                for h4 in (0, 4):
                    act.activation(Qb[0:QK, h4:h4 + 4, t0:T], QT[0:QK, h4:h4 + 4, t0:T], ACT.Copy
                                   ).then_inc(s["qb16"], 1)
                act.wait_ge(*s("mT", 1))
                act.activation(negm[:, t0:T], B[4][0:8, t0:T], ACT.Copy, scale=-1.0).then_inc(s["nm"], 1)
                for h in range(HEADS):
                    for kt in range(NCH):
                        a = t0 if kt < 2 else SEQ
                        off = 512 * kt if kt < 2 else 1024 + 256 * (kt - 2) - SEQ
                        if h >= 2 and kt == 0:
                            act.wait_ge(*s("pv", h - 1))
                        if h == 0 and kt == 0:
                            act.wait_ge(*s("llo", 5))
                        act.wait_ge(*s("st", 4 * h + kt + 1))
                        act.activation(PT[:, h % 2, off + a:off + T], B[kt][:, a:T], ACT.Exp,
                                       scale=SCALE).then_inc(s["ex"], 1)
                    if h >= 1:
                        mla_den(l, h - 1)
                mla_den(l, HEADS - 1)

            def mla_den(l, h):
                s, t0 = L[l], t0_of(l)
                rd = rstd if h % 2 == 0 else th[:, 0, :]
                o32 = rr(R_HQ + 14848, 1024, "p (b t) -> p b t", b=2)
                act.wait_ge(*s("pv", h + 1))
                if h >= 2:
                    act.wait_ge(*s("on", h - 1))
                link(act.activation(rd[0:64, t0:T], B[5 + h % 2][64:128, t0:T], ACT.Ln))
                act.activation(rd[0:64, t0:T], rd[0:64, t0:T], ACT.Exp, scale=-1.0).then_inc(s["den"], 1)
                if h % 2 == 1:
                    act.wait_ge(*s("on", h + 1))
                    act.activation(act16[:, 0, h // 2, t0:T], o32[:, (h // 2) % 2, t0:T], ACT.Copy
                                   ).then_inc(s["ohi"], 1)

            def ffn(l):
                s, t0 = L[l], t0_of(l)
                h16 = rr(0, KF * T).bitcast(F16).rearrange("p (a k t) -> p a k t", a=2, k=KF)

                def hidden_high(i):
                    act.wait_ge(evac, AT_GROUP["fi", l, i] + 1)
                    act.activation(h16[:, 0, i, t0:T], h32(i)[:, t0:T], ACT.Copy).then_inc(s["hhi"], 1)

                for i in range(N_FI):
                    ahead(("fi", l, i))
                    if l == 0:
                        ahead(("ada", 1, i))
                    if i >= 1:
                        hidden_high(i - 1)
                    g = AT_GROUP["fi", l, i]
                    act.wait_ge(prod, AT_UNIT["fi", l, i] + 1)
                    if i >= 2:
                        act.wait_ge(evac, g - 1)
                    act.activation(th[:, i % 2, t0:T], B[2 * (g % 2)][:, t0:T], ACT.Tanh,
                                   scale=0.5 / WS).then_inc(tanh_s, 1)
                hidden_high(N_FI - 1)
                for i in range(N_FO):
                    ahead(("fo", l, i))
                    if l == 0 and i < N_ADA - N_FI:
                        ahead(("ada", 1, N_FI + i))

            act.wait_ge(params, 48)
            act.wait_ge(setup, 4)
            act.activation(cs[:, 1, :, :], cvec(), ACT.Tanh, scale=0.5).then_inc(cs_t, 1)
            act.activation(masks[:, :, :], rr(R_Z, 8 * C, "p (n t) -> p n t", n=8), ACT.Copy).then_inc(masks_s, 1)
            act.activation(sel16[:, :, :], const(C_SEL, 1024, 8).rearrange("p (h t) -> p h t", h=8), ACT.Copy)
            act.wait_ge(cs_v, 1)
            act.activation(cs16[:, :, 0, :], cs[:, 0, :, :], ACT.Copy).then_inc(cs_t, 1)
            high(0)
            high(1)
            for i in range(8):
                ahead(("ada", 0, i))
            act.wait_ge(x_in, 16)
            for l in range(DEPTH):
                s = L[l]
                if l == 0:
                    norm(l, "1", 0, None)
                else:
                    norm(l, "1", 0, lambda k: ("fo", l - 1, N_FO - 2))
                for i in range(N_IN):
                    inproj(l, i)
                ssm(l)
                hgrn(l)
                mla(l)
                for i in range(N_OUT):
                    ahead(("out", l, i))
                norm(l, "2", t0_of(l), lambda k: ("out", l, k // 2))
                ffn(l)
            for k in range(KD):
                act.wait_ge(evac, len(GROUPS))
                act.activation(rr(k * SEQ, SEQ), xT[:, k, SEQ:T], ACT.Square).then_inc(fin["sq"], 1)
            act.wait_ge(fin["ssq"], 1)
            rsqrt_mean(rstd[:, SEQ:T], B[6][:, 0:SEQ], D, fin["rstd"])

        @block.vector
        def _(dve):
            chain = [0]

            def mark(ins):
                chain[0] += 1
                ins.then_inc(dch, 1)

            def sync():
                dve.wait_ge(dch, chain[0])

            def link(ins):
                mark(ins)
                sync()

            def low(n):
                kind = UNITS[n][0]
                dve.wait_ge(w_hi, n + 1)
                dve.scalar_tensor_tensor(w16[n % 3][:, 1, 0:SIZE[kind]], w32[n % 2][:, 0:SIZE[kind]], WS,
                                         w16[n % 3][:, 0, 0:SIZE[kind]], ALU.mult, ALU.subtract).then_inc(w_lo, 1)

            def ahead(u):
                if AT_UNIT[u] + 2 < len(UNITS):
                    low(AT_UNIT[u] + 2)

            def modulation(l, m0, m1):
                ps = B[7][:, 4 * m0:4 * m1].rearrange("p (m a) -> p m a", a=4)
                o = mod[:, l, m0:m1, :]
                b = vec(l, V_BADA + m0, m1 - m0).unsqueeze(2).to_broadcast([P, m1 - m0, 2])
                dve.scalar_tensor_tensor(o, ps[:, :, 0:2], 1.0 / WS, b, ALU.mult, ALU.add).then_inc(L[l]["mod"], 1)
                n = 1 if m0 == 0 else 3
                dve.wait_ge(*L[l]("mod", n))
                dve.scalar_tensor_tensor(o, ps[:, :, 2:4], 1.0 / WS, o, ALU.mult, ALU.add).then_inc(L[l]["mod"], 1)
                dve.wait_ge(*L[l]("mod", n + 1))

            def gains(l, which):
                g = vec(l, V_N1 if which == 0 else V_N2, KD).unsqueeze(2).to_broadcast([P, KD, 2])
                at = 8 if which == 0 else 32
                link(dve.scalar_tensor_tensor(aff[:, l, which, :, :], mod[:, l, at:at + 8, :], 1.0, g,
                                              ALU.add, ALU.mult))

            def gate(l, which):
                at = 16 if which == 0 else 40
                link(dve.tensor_scalar(aff[:, l, 2 + which, :, :], mod[:, l, at:at + 8, :], 1.0 / WS, None, ALU.mult))

            def norm(l, q, t0):
                s = L[l]
                dve.wait_ge(*s("rstd" + q, 1))
                tm = rr(4096, KD * T, "p (k t) -> p k t", k=KD)
                for k in range(KD):
                    for sq in range(t0 // SEQ, 2):
                        a = slice(sq * SEQ, sq * SEQ + SEQ)
                        dve.scalar_tensor_tensor(tm[:, k, a], xT[:, k, a],
                                                 aff[:, l, 0 if q == "1" else 1, k, 1 - sq:2 - sq], rstd[:, a],
                                                 ALU.mult, ALU.mult).then_inc(s["tm" + q], 1)
                m = 0
                for k in range(KD):
                    for sq in range(t0 // SEQ, 2):
                        a = slice(sq * SEQ, sq * SEQ + SEQ)
                        m += 1
                        dve.wait_ge(*s("xhi" + q, m))
                        dve.scalar_tensor_tensor(act16[:, 1, k, a], tm[:, k, a],
                                                 mod[:, l, (0 if q == "1" else 24) + k, 1 - sq:2 - sq],
                                                 act16[:, 0, k, a], ALU.add, ALU.subtract).then_inc(s["xlo" + q], 1)

            def inproj(l, i):
                s, t0 = L[l], t0_of(l)
                ahead(("in", l, i))
                if l == 0:
                    for _ in range(2 if i < 5 else 1):
                        ahead(("ada", 0, nxt[0]))
                        nxt[0] += 1
                g = AT_GROUP["in", l, i]
                ps = (B[2 * (g % 2)], B[2 * (g % 2) + 1])
                if IN_TILES[i][0] in ("z0", "q0", "og0"):
                    tanhs[0] += 1
                    dve.wait_ge(tanh_s, tanhs[0])
                else:
                    dve.wait_ge(prod, AT_UNIT["in", l, i] + 1)
                for m, name in enumerate(IN_TILES[i]):
                    a = t0 if name in LAT_ONLY else 0
                    if name in ("kv0", "kv1", "ql0", "ql1", "ql2"):
                        at = R_QL + T * ("ql0", "ql1", "ql2", "kv0", "kv1").index(name)
                        last = dve.tensor_scalar(rr(at + a, T - a), ps[m][:, a:T], 1.0 / WS, None, ALU.mult)
                    elif name == "misc":
                        dve.tensor_scalar(rr(R_MISC, T)[0:ROPE, :], ps[m][0:ROPE, :], 1.0 / WS, None, ALU.mult)
                        last = dve.tensor_scalar(rr(R_T + 6656, T)[0:8, :], ps[m][32:40, :], 1.0 / WS,
                                                 vec(l, V_DTB, 1)[0:8, :], ALU.mult, ALU.add)
                    elif name in ("xs0", "xs1", "B", "C"):
                        j = ("xs0", "xs1", "B", "C").index(name)
                        xbc = rr(R_XBC, 4 * 2 * PAD, "p (j s t) -> p j s t", j=4, s=2)
                        s0 = a // SEQ
                        last = dve.tensor_scalar(xbc[:, j, s0:2, 2:2 + SEQ], seqs(ps[m][:, :])[:, s0:2, :], 1.0 / WS,
                                                 None, ALU.mult)
                    elif name[0] == "f":
                        at = R_FF + T * (2 * (name[1] == "b") + int(name[2]))
                        last = dve.tensor_scalar(rr(at, T), ps[m][:, :], -1.0 / WS, GATE_MAX, ALU.mult, ALU.min)
                    elif name == "iv":
                        last = dve.tensor_scalar(rr(R_IV + 512 * m, 512), ps[m][:, :], 0.5 / WS / WS, None, ALU.mult)
                    else:
                        at = {"z": R_Z, "q": R_HQ, "o": R_OG}[name[0]] + T * int(name[-1])
                        last = dve.scalar_tensor_tensor(rr(at + a, T - a), th[:, m, a:T], 1.0, ps[m][:, a:T],
                                                        ALU.add, ALU.mult)
                last.then_inc(evac, 1)
                if i == 1:
                    dt_rows(l)
                if i == 2:
                    conv(l)
                if i == 3:
                    conv_silu(l)

            def dt_rows(l):
                s = L[l]
                r = lambda i: rr(R_T + 6656 + 512 * i, 512)[0:8, :]
                ch = lambda ap: ap.rearrange("p (c t) -> p c t", c=NCH)
                sg = lambda i: cst[0:8, C_SGN + i:C_SGN + i + 1]
                dve.wait_ge(*s("dsp", 1))
                link(dve.scalar_tensor_tensor(r(2), r(0), 0.0, r(1), ALU.max, ALU.add))
                link(dve.tensor_scalar(r(3), r(2), acol, -1.0, ALU.mult, ALU.mult))
                link(dve.tensor_tensor_scan(r(4), cst[0:8, C_RESET:C_RESET + T], r(3), 0.0, ALU.mult, ALU.add))
                mark(dve.tensor_scalar(lastf, ch(r(4))[:, :, C - 1], sg(0), None, ALU.mult))
                mark(dve.tensor_scalar(lastb, ch(r(4))[:, :, C - 1], sg(1), None, ALU.mult))
                link(dve.scalar_tensor_tensor(rows[0:8, :], r(3), sg(2), r(4), ALU.mult, ALU.add))
                dve.scalar_tensor_tensor(ch(r(0)), ch(rows[0:8, :]), sg(3), lastf.unsqueeze(2).to_broadcast([8, NCH, C]),
                                         ALU.mult, ALU.add).then_inc(s["wrow"], 1)
                dve.scalar_tensor_tensor(ch(r(5)), ch(rows[0:8, :]), sg(4), lastb.unsqueeze(2).to_broadcast([8, NCH, C]),
                                         ALU.mult, ALU.add).then_inc(s["wrow"], 1)
                dve.wait_ge(*s("wexp", 1))
                dve.tensor_tensor(rows[64:72, :], r(0), r(2), ALU.mult).then_inc(s["rowd"], 1)
                dve.tensor_copy(rows[32:40, :], r(2)).then_inc(s["rowd"], 1)

            def conv(l):
                s = L[l]
                xbc = rr(R_XBC, 4 * 2 * PAD, "p (j s t) -> p j s t", j=4, s=2)
                acc = rr(R_T, 2048, "p (j t) -> p j t", j=4)
                mark(dve.tensor_scalar(hcw, vec(l, V_CW, 20), 0.5, None, ALU.mult))
                mark(dve.tensor_scalar(hcb, vec(l, V_CB, 4), 0.5, None, ALU.mult))
                mark(dve.memset(xbc[:, :, :, 0:2].rearrange("p j s t -> p (j s) t"), 0.0))
                link(dve.memset(xbc[:, :, :, 2 + SEQ:PAD].rearrange("p j s t -> p (j s) t"), 0.0))
                dve.wait_ge(evac, AT_GROUP["in", l, 2] + 1)
                s0 = lambda j: t0_of(l) // SEQ if j == 3 else 0
                for tap in range(TAPS):
                    for j in range(4):
                        o = seqs(acc[:, j, :])[:, s0(j):2, :]
                        u = xbc[:, j, s0(j):2, tap:tap + SEQ]
                        wt = hcw[:, 4 * tap + j:4 * tap + j + 1]
                        if tap == 0:
                            mark(dve.tensor_scalar(o, u, wt, hcb[:, j:j + 1], ALU.mult, ALU.add))
                        else:
                            if tap >= 2:
                                dve.wait_ge(*s("acc", 4 * (tap - 2) + j + 1))
                            elif j == 0:
                                sync()
                            dve.scalar_tensor_tensor(o, u, wt, o, ALU.mult, ALU.add).then_inc(s["acc"], 1)

            def conv_silu(l):
                s, t0 = L[l], t0_of(l)
                acc = rr(R_T, 2048, "p (j t) -> p j t", j=4)
                cth = rr(R_T + 2048, 2048, "p (j t) -> p j t", j=4)
                xs = rr(R_T + 4096, 1024, "p (g t) -> p g t", g=2)
                Bf = rr(R_T + 5120, 512)
                Cd = rr(R_T + 5632, 1024, "p (g t) -> p g t", g=2)
                for j in range(3):
                    dve.wait_ge(*s("cth", j + 1))
                    o = xs[:, j, :] if j < 2 else Bf
                    dve.scalar_tensor_tensor(o, cth[:, j, :], 1.0, acc[:, j, :], ALU.add,
                                             ALU.mult).then_inc(s["conv"], 1)
                dve.wait_ge(*s("cth", 4))
                for g in range(2):
                    for dup in range(2):
                        gs, ds = slice(64 * g, 64 * g + 64), slice(64 * dup, 64 * dup + 64)
                        dve.scalar_tensor_tensor(Cd[ds, g, t0:T], cth[gs, 3, t0:T], 1.0, acc[gs, 3, t0:T], ALU.add,
                                                 ALU.mult).then_inc(s["conv"], 1)

            def ssm(l):
                s, t0, OC = L[l], t0_of(l), out_chunks(l)
                Cd = rr(R_T + 5632, 1024, "p (g t) -> p g t", g=2)
                Cw = rr(R_T + 2048, 2048, "p (d g t) -> p d g t", d=2, g=2)
                btok = rr(R_T + 1024, 1024, "p (cg u n) -> p cg u n", u=2, n=64)
                dve.wait_ge(*s("tr", 1))
                bsrc = B[6][:, :].rearrange("p (cg n) -> p cg n", n=64)
                for dup in range(2):
                    dve.tensor_copy(btok[:, :, dup, :], bsrc).then_inc(s["trv"], 1)
                dve.wait_ge(*s("tr", 2))
                dve.tensor_copy(rtok[:, :, :], B[0][:, :].rearrange("p (c r) -> p c r", c=NCH)[:, :, 0:72]
                                ).then_inc(s["trv"], 1)
                for n, (d, g, b) in enumerate(((0, 0, 3), (0, 1, 0), (1, 0, 4), (1, 1, 5))):
                    if n < 3:
                        dve.wait_ge(*s("cb", n + 2))
                    else:
                        dve.wait_ge(*s("bcr", 1))
                    e = B[b][:, :].rearrange("p (c t) -> p c t", c=NCH)[:, :, C - 1 if d == 0 else 0]
                    dve.tensor_copy(ED[:, 4 * n:4 * n + 4], e).then_inc(s["cw"], 1)
                    dve.tensor_tensor(Cw[:, d, g, t0:T], Cd[:, g, t0:T], B[b][:, t0:T],
                                      ALU.mult).then_inc(s["cw"], 1)
                dve.wait_ge(*s("stp", 1))
                dve.wait_ge(*s("cw", 8))
                if l > 0:
                    dve.wait_ge(*L[l - 1]("go", 1))
                states(s, "S_ssm", ((0, 0, 3), (0, 1, 0), (1, 0, 4), (1, 1, 5)),
                       lambda d, g, c: ED[:, 4 * (2 * d + g) + c:4 * (2 * d + g) + c + 1])
                Dx = rr(R_XBC + 1024, 1024, "p (d h t) -> p d h t", d=2, h=SSM_HEADS)
                Mx = rr(R_XBC, 1024, "p (b h t) -> p b h t", b=2, h=SSM_HEADS)
                for n, c in enumerate(OC):
                    dve.wait_ge(*s("rows_bc", n + 1))
                    for d in range(2):
                        for h in range(SSM_HEADS):
                            dve.tensor_scalar(Dx[:, d, h, :], B[4 + d][:, h * C:h * C + C],
                                              rtok[:, c, 4 * d + h:4 * d + h + 1], 0.0, ALU.subtract,
                                              ALU.min if d == 0 else ALU.max).then_inc(s["D"], 1)
                    for d in range(2):
                        dve.wait_ge(*s("E_ssm", 2 * n + d + 1))
                        for h in range(SSM_HEADS):
                            mark(dve.scalar_tensor_tensor(Dx[:, d, h, :], Dx[:, d, h, :],
                                                          rtok[:, c, 32 + 4 * d + h:33 + 4 * d + h],
                                                          const(C_MF if d == 0 else C_MB, C), ALU.mult, ALU.mult))
                    sync()
                    link(dve.tensor_tensor(Dx[:, 0, :, :], Dx[:, 0, :, :], Dx[:, 1, :, :], ALU.add))
                    if n >= 2:
                        dve.wait_ge(*s("y", n - 1))
                    for g in range(2):
                        dve.tensor_tensor(Mx[:, n % 2, 2 * g:2 * g + 2, :], Dx[:, 0, 2 * g:2 * g + 2, :],
                                          B[1 + g][:, c * C:c * C + C].unsqueeze(1).to_broadcast([P, 2, C]),
                                          ALU.mult).then_inc(s["M"], 1)
                xs = rr(R_T + 4096, 1024, "p (g t) -> p g t", g=2)
                z = rr(R_Z, 1024, "p (g t) -> p g t", g=2)
                yz = rr(R_XBC, 1024, "p (g t) -> p g t", g=2)
                dve.wait_ge(*s("y", len(OC)))
                yb = (B[6], B[3])
                for g in range(2):
                    mark(dve.scalar_tensor_tensor(yz[:, g, t0:T], xs[:, g, t0:T], vec(l, V_D + g, 1), yb[g][:, t0:T],
                                                  ALU.mult, ALU.add))
                sync()
                for g in range(2):
                    dve.scalar_tensor_tensor(yz[:, g, t0:T], yz[:, g, t0:T], 0.5 / WS, z[:, g, t0:T], ALU.mult,
                                             ALU.mult).then_inc(s["ym"], 1)
                for g in range(2):
                    dve.wait_ge(*s("yrs", g + 1))
                    dve.wait_ge(*s("ysq", g + 1))
                    dve.scalar_tensor_tensor(yz[:, g, t0:T], yz[:, g, t0:T], vec(l, V_SN + g, 1), th[:, g, t0:T],
                                             ALU.mult, ALU.mult).then_inc(s["ym"], 1)
                for g in range(2):
                    dve.wait_ge(*s("yhi", g + 1))
                    dve.tensor_tensor(act16[:, 1, 6 + g, t0:T], yz[:, g, t0:T], act16[:, 0, 6 + g, t0:T],
                                      ALU.subtract).then_inc(s["ylo"], 1)

            def states(s, done, banks, decay):
                n = 0
                for i in range(3):
                    if i:
                        dve.wait_ge(*s(done, 8 * i))
                    for d, g, b in banks:
                        for r in (slice(0, 64), slice(64, 128)):
                            new = B[b][r, i * P + r.start:i * P + r.stop]
                            to = S[r, d, i, g, r.start:r.stop]
                            if i == 0:
                                ins = dve.tensor_copy(to, new)
                            else:
                                ins = dve.scalar_tensor_tensor(to, S[r, d, i - 1, g, r.start:r.stop],
                                                               decay(d, g, ORDER[d][i])[r, :], new, ALU.mult, ALU.add)
                            ins.then_inc(s[done], 1)

            def hgrn(l):
                s, t0, OC = L[l], t0_of(l), out_chunks(l)
                ff, E = rr(R_FF, 2048), rr(R_T + 2048, 2048)
                k4 = rr(R_FF, 2048, "p (n t) -> p n t", n=4)
                cum = rr(R_T, 2048, "p (n t) -> p n t", n=4)
                c8 = lambda ap: ap.rearrange("p (n t) -> p n t", t=C)
                q = rr(R_HQ, 1024)
                QI = rr(R_T + 4096, 2048)
                if l:
                    a0, a1 = vec(0, V_LB, 4), vec(1, V_LB, 4)
                    link(dve.tensor_tensor(lbt[:, 0:4], a0, a1, ALU.max))
                    mark(dve.tensor_tensor(lbt[:, 4:8], a0, lbt[:, 0:4], ALU.subtract))
                    dve.tensor_tensor(lbt[:, 8:12], a1, lbt[:, 0:4], ALU.subtract).then_inc(s["lbd"], 1)
                    dve.wait_ge(*s("lbe", 1))
                    link(dve.tensor_tensor(lbt[:, 0:4], lbt[:, 4:8], lbt[:, 8:12], ALU.add))
                    link(dve.reciprocal(lbt[:, 0:4], lbt[:, 0:4]))
                    mark(dve.tensor_tensor(lb4, lbt[:, 8:12], lbt[:, 0:4], ALU.mult))
                    link(dve.tensor_tensor(olb4, lbt[:, 4:8], lbt[:, 0:4], ALU.mult))
                dve.wait_ge(*s("gl", 1))
                dve.tensor_tensor(ff, ff, E, ALU.subtract).then_inc(s["gk"], 1)
                dve.wait_ge(*s("gl", 2))
                if l:
                    for n in range(4):
                        dve.tensor_scalar(E[:, n * T:n * T + T], E[:, n * T:n * T + T], olb4[:, n:n + 1],
                                          lb4[:, n:n + 1], ALU.mult, ALU.add).then_inc(s["gk"], 1)
                    for n in range(4):
                        mark(dve.tensor_scalar(k4[:, n, :], k4[:, n, :], olb4[:, n:n + 1], None, ALU.mult))
                    dve.wait_ge(*s("gl", 3))
                for n in range(4):
                    mark(dve.tensor_tensor_scan(cum[:, n, :], reset, E[:, n * T:n * T + T], 0.0, ALU.mult,
                                                ALU.add if l else ALU.subtract))
                sync()
                dve.tensor_copy(ET.rearrange("p (n c) -> p n c", c=NCH),
                                cum.rearrange("p n (c t) -> p n c t", c=NCH)[:, :, :, C - 1]).then_inc(s["gT"], 1)
                dve.wait_ge(*s("gT", 1))
                Tb = lambda d: Tl[:, 8 * d:8 * d + 8].unsqueeze(2).to_broadcast([P, 8, C])
                Tl = mcol[:, 0:16]
                link(dve.tensor_copy(Tl, cum.rearrange("p n (c t) -> p (n c) t", c=NCH)[:, :, C - 1]))
                link(dve.tensor_tensor(cum[:, 2:4, :], cum[:, 2:4, :], rr(R_T + 3072, 1024, "p (n t) -> p n t", n=2),
                                       ALU.subtract if l else ALU.add))
                X = rr(R_T + 1024, 1024)
                dve.tensor_tensor(c8(E[:, 0:1024]), Tb(0), c8(rr(R_T, 1024)), ALU.subtract).then_inc(s["gKa"], 1)
                dve.tensor_tensor(c8(QI[:, 1024:2048]), Tb(1), c8(X), ALU.subtract).then_inc(s["gKa"], 1)
                dve.wait_ge(*s("gKe", 4))
                dve.tensor_tensor(E[:, 0:1024], E[:, 0:1024], ff[:, 0:1024], ALU.mult).then_inc(s["gKm"], 1)
                dve.tensor_tensor(E[:, 1024:2048], E[:, 1024:2048], ff[:, 1024:2048], ALU.mult).then_inc(s["gKm"], 1)
                dve.wait_ge(*s("gKe", 5))
                qi4 = rr(R_T + 4096, 2048, "p (d j t) -> p d j t", d=2, j=2)
                q2 = rr(R_HQ, 1024, "p (j t) -> p j t", j=2)
                for d in range(2):
                    dve.tensor_tensor(qi4[:, d, :, t0:T], qi4[:, d, :, t0:T], q2[:, :, t0:T],
                                      ALU.mult).then_inc(s["gKm"], 1)
                dve.wait_ge(*s("gSp", 1))
                states(s, "gS", ((0, 0, 4), (0, 1, 5), (1, 0, 6), (1, 1, 0)),
                       lambda d, j, c: ET[:, 4 * (2 * d + j) + c:4 * (2 * d + j) + c + 1])
                AT = rr(R_T + 6144, 2048, "p (n u t) -> p n u t", u=2, t=C)
                nh = T - t0

                def halves(at, h, side):
                    v = rr(at, 1024, "p (j b u t) -> p j b u t", j=2, u=2, t=h)
                    return v[:, :, t0 // (2 * h):, side, :]

                def middle(at, h, side):
                    v = rr(at, 1024, "p (j b u t) -> p j b u t", j=2, u=2, t=h)[:, :, t0 // (2 * h):, side, :]
                    v = v[:, :, :, h - 1:h] if side == 0 else v[:, :, :, 0:1]
                    return v.to_broadcast([P, 2, nh // (2 * h), h])

                def args(lv):
                    h = HALVES[lv]
                    f, b, ef, eb = R_T, R_T + 1024, R_T + 2048, R_T + 3072
                    dve.tensor_tensor(halves(ef, h, 1), halves(f, h, 1), middle(f, h, 0),
                                      ALU.subtract).then_inc(s["gA"], 1)
                    dve.tensor_tensor(halves(ef, h, 0), middle(f, h, 0), halves(f, h, 0),
                                      ALU.subtract).then_inc(s["gA"], 1)
                    dve.tensor_tensor(halves(eb, h, 0), middle(b, h, 1), halves(b, h, 0),
                                      ALU.subtract).then_inc(s["gA"], 1)
                    dve.tensor_tensor(halves(eb, h, 1), halves(b, h, 1), middle(b, h, 1),
                                      ALU.subtract).then_inc(s["gA"], 1)

                dve.wait_ge(*s("gKt", 1))
                dve.wait_ge(*s("gKm", 4))
                dve.wait_ge(masks_s, 1)
                args(0)
                n_at = 0
                for lv in range(len(HALVES) + 1):
                    at = R_T + 4096 if lv % 2 == 0 else R_XBC
                    if lv == 0:
                        dve.wait_ge(*s("gO", 1))
                    if lv >= 2:
                        dve.wait_ge(*s("gP", (lv - 1) * len(OC) // 2))
                    if lv < len(HALVES):
                        h = HALVES[lv]
                        ef, eb = R_T + 2048, R_T + 3072
                        dve.wait_ge(*s("gE", lv + 1))
                        mark(dve.tensor_tensor(halves(at, h, 0), halves(R_FF, h, 0), halves(ef, h, 0), ALU.mult))
                        mark(dve.tensor_tensor(halves(at, h, 1), halves(R_FF + 1024, h, 1), halves(eb, h, 1), ALU.mult))
                        mark(dve.tensor_tensor(halves(at + 1024, h, 1), halves(R_HQ, h, 1), halves(ef, h, 1), ALU.mult))
                        dve.tensor_tensor(halves(at + 1024, h, 0), halves(R_HQ, h, 0), halves(eb, h, 0),
                                          ALU.mult).then_inc(s["gKQ"], 1)
                        if lv + 1 < len(HALVES):
                            dve.wait_ge(*s("gKQ", lv + 1))
                            args(lv + 1)
                    else:
                        kk = rr(at, 1024, "p (j t) -> p j t", j=2)
                        dve.tensor_tensor(kk[:, :, t0:T], k4[:, 0:2, t0:T], k4[:, 2:4, t0:T],
                                          ALU.add).then_inc(s["gKQ"], 1)
                    for c2 in range(OC[0] // 2, 2):
                        dve.wait_ge(*s("gP", n_at + 1))
                        if lv:
                            dve.wait_ge(*s("gAT", 2 * (n_at + 1 - len(OC) // 2)))
                        for odd in range(2):
                            ps = B[3 + 2 * (n_at % 2) + odd][:, :].rearrange("p (n t) -> p n t", n=4)
                            to = AT[:, 4 * c2:4 * c2 + 4, odd, :]
                            if lv == 0:
                                ins = dve.tensor_copy(to, ps)
                            else:
                                ins = dve.copy_predicated(to, masks[:, lv, :].unsqueeze(1).to_broadcast([P, 4, C]), ps)
                            ins.then_inc(s["gAT"], 1)
                        n_at += 1
                r = rr(R_T + 3072, 1024, "p (j t) -> p j t", j=2)
                mx = rr(R_T + 4096, 1024, "p (j t) -> p j t", j=2)
                og = rr(R_OG, 1024, "p (j t) -> p j t", j=2)
                for j in range(2):
                    dve.wait_ge(*s("grs", j + 1))
                    mark(dve.scalar_tensor_tensor(r[:, j, t0:T], r[:, j, t0:T], vec(l, V_HGN + j, 1), B[1 + j][:, t0:T],
                                                  ALU.mult, ALU.mult))
                sync()
                for j in range(2):
                    dve.scalar_tensor_tensor(mx[:, j, t0:T], r[:, j, t0:T], 0.5 / WS, og[:, j, t0:T], ALU.mult,
                                             ALU.mult).then_inc(s["gm"], 1)
                for j in range(2):
                    dve.wait_ge(*s("ghi", j + 1))
                    dve.tensor_tensor(act16[:, 1, 4 + j, t0:T], mx[:, j, t0:T], act16[:, 0, 4 + j, t0:T],
                                      ALU.subtract).then_inc(s["glo"], 1)

            def mla(l):
                s, t0 = L[l], t0_of(l)
                lat16 = rr(R_HQ, 2560).bitcast(F16).rearrange("p (a k t) -> p a k t", a=2, k=5)
                lh = rr(R_HQ + 10752, 2560, "p (k t) -> p k t", k=5)
                QT = rr(R_HQ + 2560, 4096, "p (h t) -> p h t", h=HEADS)
                KTt = rr(R_HQ + 6656, 4096, "p (h t) -> p h t", h=HEADS)
                V = rr(R_HQ + 10752, 4096, "p (c h v) -> p c h v", c=NCH, h=HEADS)
                qr = rr(R_HQ + 14848, 1024, "p (j t) -> p j t", j=2)
                o32 = rr(R_HQ + 14848, 1024, "p (b t) -> p b t", b=2)
                cos, sin = const(C_COS, SEQ), const(C_SIN, SEQ)
                for k in range(KQ + KKV):
                    a = t0 if k < KQ else 0
                    dve.wait_ge(*s("lrs", 1 if k < KQ else 2))
                    g = vec(l, V_QA + k, 1) if k < KQ else vec(l, V_KVA + k - KQ, 1)
                    dve.scalar_tensor_tensor(lh[:, k, a:T], rr(R_QL + k * T + a, T - a), g,
                                             th[:, 0 if k < KQ else 1, a:T], ALU.mult, ALU.mult).then_inc(s["lh"], 1)
                for k in range(KQ + KKV):
                    a = t0 if k < KQ else 0
                    dve.wait_ge(*s("lhi", k + 1))
                    dve.tensor_tensor(lat16[:, 1, k, a:T], lh[:, k, a:T], lat16[:, 0, k, a:T],
                                      ALU.subtract).then_inc(s["llo"], 1)
                ahead(("qb", l, 0))
                kr = rr(R_MISC, T)[0:ROPE, :]
                dve.wait_ge(*s("krp", 1))
                mark(dve.tensor_tensor(rr(R_QL, SEQ)[0:ROPE, :], B[4][0:ROPE, 0:SEQ], sin[0:ROPE, :], ALU.mult))
                mark(dve.tensor_tensor(kr[:, SEQ:T], kr[:, SEQ:T], cos[0:ROPE, :], ALU.mult))
                sync()
                dve.tensor_tensor(kr[:, SEQ:T], kr[:, SEQ:T], rr(R_QL, SEQ)[0:ROPE, :], ALU.add).then_inc(s["krc"], 1)
                for m in range(6):
                    if m < 5:
                        dve.wait_ge(*s("qp", m + 1))
                    else:
                        dve.wait_ge(prod, AT_UNIT["qb", l, 0] + 1)
                    ps = B[m % 4]
                    if m < 4:
                        dve.tensor_scalar(QT[0:64, 2 * m, t0:T], ps[0:64, t0:T], 1.0 / WS, None, ALU.mult)
                        dve.tensor_scalar(QT[0:64, 2 * m + 1, t0:T], ps[64:128, t0:T], 1.0 / WS, None,
                                          ALU.mult).then_inc(s["qn"], 1)
                    else:
                        dve.tensor_scalar(qr[:, m - 4, t0:T], ps[:, t0:T], 1.0 / WS, None,
                                          ALU.mult).then_inc(s["qn"], 1)
                ahead(("kvb", l, 0))
                kb = (2, 3, 5, 6, 0, 1, 2, 3)
                for m in range(8):
                    if m < 7:
                        dve.wait_ge(*s("qp", 5 + m + 1))
                    else:
                        dve.wait_ge(prod, AT_UNIT["kvb", l, 0] + 1)
                    ps = B[kb[m]]
                    if m < 4:
                        dve.tensor_scalar(KTt[0:64, 2 * m, :], ps[0:64, :], 1.0 / WS, None, ALU.mult)
                        dve.tensor_scalar(KTt[0:64, 2 * m + 1, :], ps[64:128, :], 1.0 / WS, None,
                                          ALU.mult).then_inc(s["Kn"], 1)
                    else:
                        if m == 4:
                            dve.memset(V[:, :, :, 64:128].rearrange("p c h v -> p (c h) v"), 1.0)
                        dve.tensor_scalar(V[:, m - 4, :, 0:64], ps[:, :].rearrange("p (h v) -> p h v", h=HEADS), 1.0 / WS,
                                          None, ALU.mult).then_inc(s["Vv"], 1)
                rt = rr(R_QL, 2 * SEQ, "p (j t) -> p j t", j=2)
                for j in range(2):
                    dve.wait_ge(*s("qrp", j + 1))
                    mark(dve.tensor_tensor(rt[:, j, :], B[5 + j][:, 0:SEQ], sin, ALU.mult))
                    mark(dve.tensor_tensor(qr[:, j, SEQ:T], qr[:, j, SEQ:T], cos, ALU.mult))
                    if t0 == 0:
                        for i in range(4):
                            mark(dve.tensor_copy(QT[64:96, 4 * j + i, 0:SEQ], qr[32 * i:32 * i + 32, j, 0:SEQ]))
                    sync()
                    for i in range(4):
                        dve.tensor_tensor(QT[64:96, 4 * j + i, SEQ:T], qr[32 * i:32 * i + 32, j, SEQ:T],
                                          rt[32 * i:32 * i + 32, j, :], ALU.add).then_inc(s["Qd"], 1)
                Kb = max_copies()[1]
                dve.wait_ge(*s("krdma", 16))
                for h4 in (0, 4):
                    dve.tensor_copy(Kb[0:QK, h4:h4 + 4, :], KTt[0:QK, h4:h4 + 4, :]).then_inc(s["kb16"], 1)
                n = 0
                for qt in range(t0 // P, T // P):
                    keys = SEQ if qt < 2 else T
                    for h in range(HEADS):
                        dve.wait_ge(*s("smx", n + 1))
                        dve.tensor_reduce(mcol[:, 8 * qt + h:8 * qt + h + 1], B[n % 4][:, 0:keys], AX.X,
                                          ALU.max).then_inc(s["mx"], 1)
                        n += 1
                for h in range(HEADS):
                    rd = rstd if h % 2 == 0 else th[:, 0, :]
                    r = slice(64 * (h % 2), 64 * (h % 2) + 64)
                    dve.wait_ge(*s("den", h + 1))
                    if h >= 4 and h % 2 == 0:
                        dve.wait_ge(*s("ohi", h // 2 - 1))
                        dve.wait_ge(*s("olo", h // 2 - 1))
                    dve.tensor_tensor(o32[r, (h // 2) % 2, t0:T], B[5 + h % 2][0:64, t0:T], rd[0:64, t0:T],
                                      ALU.mult).then_inc(s["on"], 1)
                    if h % 2 == 1:
                        dve.wait_ge(*s("ohi", h // 2 + 1))
                        dve.tensor_tensor(act16[:, 1, h // 2, t0:T], o32[:, (h // 2) % 2, t0:T],
                                          act16[:, 0, h // 2, t0:T], ALU.subtract).then_inc(s["olo"], 1)

            def residual(l, u, m2, which):
                t0, g = t0_of(l), AT_GROUP[u]
                for m in range(2):
                    k = 2 * m2 + m
                    for sq in range(t0 // SEQ, 2):
                        a = slice(sq * SEQ, sq * SEQ + SEQ)
                        last = dve.scalar_tensor_tensor(xT[:, k, a], B[2 * (g % 2) + m][:, a],
                                                        aff[:, l, 2 + which, k, 1 - sq:2 - sq], xT[:, k, a], ALU.mult,
                                                        ALU.add)
                last.then_inc(evac, 1)

            def ffn(l):
                s, t0 = L[l], t0_of(l)
                h16 = rr(0, KF * T).bitcast(F16).rearrange("p (a k t) -> p a k t", a=2, k=KF)

                def hidden_low(i):
                    dve.wait_ge(*s("hhi", i + 1))
                    dve.tensor_tensor(h16[:, 1, i, t0:T], h32(i)[:, t0:T], h16[:, 0, i, t0:T],
                                      ALU.subtract).then_inc(s["hlo"], 1)

                for i in range(N_FI):
                    ahead(("fi", l, i))
                    if l == 0:
                        ahead(("ada", 1, i))
                    if i >= 1:
                        hidden_low(i - 1)
                    g = AT_GROUP["fi", l, i]
                    tanhs[0] += 1
                    dve.wait_ge(tanh_s, tanhs[0])
                    u = th[:, i % 2, t0:T]
                    link(dve.scalar_tensor_tensor(u, u, 1.0, B[2 * (g % 2)][:, t0:T], ALU.add, ALU.mult))
                    dve.scalar_tensor_tensor(h32(i)[:, t0:T], u, 0.5 / WS / WS, B[2 * (g % 2) + 1][:, t0:T],
                                             ALU.mult, ALU.mult).then_inc(evac, 1)
                hidden_low(N_FI - 1)
                for i in range(N_FO):
                    ahead(("fo", l, i))
                    if l == 0 and i < N_ADA - N_FI:
                        ahead(("ada", 1, N_FI + i))
                    if i % 2 == 1:
                        dve.wait_ge(prod, AT_UNIT["fo", l, i] + 1)
                        residual(l, ("fo", l, i - 1), i // 2, 1)

            nxt = [8]
            tanhs = [0]
            dve.wait_ge(params, 48)
            dve.wait_ge(setup, 4)
            dve.wait_ge(cs_t, 1)
            link(dve.scalar_tensor_tensor(cs[:, 0, :, :], cs[:, 1, :, :], 1.0, cvec(), ALU.add, ALU.mult))
            dve.tensor_scalar(cs[:, 0, :, :], cs[:, 0, :, :], 0.5, None, ALU.mult).then_inc(cs_v, 1)
            dve.wait_ge(cs_v, 1)
            dve.wait_ge(cs_t, 2)
            dve.tensor_tensor(cs16[:, :, 1, :], cs[:, 0, :, :], cs16[:, :, 0, :], ALU.subtract).then_inc(cs_v, 1)
            low(0)
            low(1)
            for i in range(8):
                ahead(("ada", 0, i))
            dve.wait_ge(prod, 8)
            modulation(0, 0, 16)
            gains(0, 0)
            dve.wait_ge(x_in, 16)
            for l in range(DEPTH):
                s = L[l]
                norm(l, "1", 0)
                for i in range(N_IN):
                    inproj(l, i)
                if l == 0:
                    dve.wait_ge(prod, AT_UNIT["ada", 0, N_ADA - 1] + 1)
                    modulation(0, 16, 48)
                    gains(0, 1)
                    gate(0, 0)
                    gate(0, 1)
                ssm(l)
                hgrn(l)
                mla(l)
                for i in range(N_OUT):
                    ahead(("out", l, i))
                    dve.wait_ge(prod, AT_UNIT["out", l, i] + 1)
                    residual(l, ("out", l, i), i, 0)
                norm(l, "2", t0_of(l))
                ffn(l)
                if l == 0:
                    modulation(1, 0, 48)
                    gains(1, 0)
                    gains(1, 1)
                    gate(1, 0)
                    gate(1, 1)
            dve.wait_ge(fin["rstd"], 1)
            for k in range(KD):
                dve.scalar_tensor_tensor(act32_out()[:, k, :], xT[:, k, SEQ:T], vecs[:, V_FINAL + k:V_FINAL + k + 1],
                                         rstd[:, SEQ:T], ALU.mult, ALU.mult).then_inc(fin["y"], 1)


def constants():
    c = np.zeros((P, C_COLS), np.float32)
    i = np.arange(P)
    c[:, C_ID:C_ID + P] = np.eye(P)
    c[:, C_ONES:C_ONES + P] = 1
    c[:, C_B64:C_B64 + P] = (i[:, None] // 64) == (i[None, :] // 64)
    c[:, C_RESET:C_RESET + T] = (np.arange(T) % C) != 0
    c[:, C_MF:C_MF + P] = i[:, None] <= i[None, :]
    c[:, C_MB:C_MB + P] = i[:, None] >= i[None, :]
    for r in range(8):
        c[r, C_SEL + r * P:C_SEL + r * P + P] = 1
    for d in range(2):
        for g in range(2):
            for h in range(2):
                at = C_SELT + (2 * d + g) * P + 64 * h
                c[4 * d + 2 * g + h, at:at + 64] = 1
    t = np.arange(SEQ, dtype=np.float32)
    pos = np.stack([np.floor(t / GRID_W), t % GRID_W])
    nf = ROPE // 4
    inv = np.float32(10000.0) ** (-np.arange(nf, dtype=np.float32) / np.float32(nf))
    for r in range(P):
        x = r % ROPE
        a, b, f = x // 16, (x // 8) % 2, x % 8
        ang = pos[a].astype(np.float32) * inv[f].astype(np.float32)
        c[r, C_COS:C_COS + SEQ] = np.cos(ang)
        c[r, C_SIN:C_SIN + SEQ] = np.sin(ang) * (-1 if b == 0 else 1)
        c[r ^ 8, C_PERM + r] = 1
    isf = (np.arange(8) < 4).astype(np.float32)
    isb = 1 - isf
    for n, v in enumerate((isf, isb, -isb, isb - isf, isf - isb)):
        c[0:8, C_SGN + n] = v
    m = np.zeros((P, 8, C), np.float32)
    for n, h in enumerate(HALVES):
        m[:, n] = ((i[:, None] // (2 * h)) == (i[None, :] // (2 * h))) & ((i[:, None] // h) != (i[None, :] // h))
    m[:, 7] = np.eye(P)
    return c, m.reshape(P, 8 * C)


def feature_major(a):
    a = np.asarray(a)
    return np.moveaxis(a.reshape(-1, P), 1, 0)


def tiled(a, cols):
    a = np.asarray(a)[:, cols]
    return a.reshape(-1, P, a.shape[1]).transpose(1, 0, 2)


def kernel(**inputs):
    import concourse.bacc as _bacc
    from concourse.bass_utils import run_bass_kernel_spmd as _run

    a = {k: np.asarray(v) for k, v in inputs.items()}
    v = np.zeros((P, V_COLS), np.float32)
    for l in range(DEPTH):
        o = l * V_LAYER

        def put(at, block):
            v[:block.shape[0], o + at:o + at + block.shape[1]] = block

        put(V_BADA, feature_major(a["b_ada"][l]))
        put(V_N1, feature_major(a["norm1_g"][l]))
        put(V_N2, feature_major(a["norm2_g"][l]))
        put(V_QA, feature_major(a["mla_qa_g"][l]))
        put(V_KVA, feature_major(a["mla_kva_g"][l]))
        put(V_LB, feature_major(a["hg_lb_logits"][l]))
        put(V_HGN, feature_major(a["hg_norm_g"][l]))
        put(V_CW, feature_major(a["ssm_conv_w"][l]))
        put(V_CB, feature_major(a["ssm_conv_b"][l]))
        put(V_DTB, a["ssm_dt_bias"][l].reshape(8, 1))
        put(V_ALOG, a["ssm_a_log"][l].reshape(8, 1))
        put(V_D, feature_major(np.repeat(a["ssm_d"][l], 64)))
        put(V_SN, feature_major(a["ssm_norm_g"][l]))
    v[:, V_FINAL:V_FINAL + KD] = feature_major(a["final_g"])
    v[:, V_C:V_C + 2 * KD] = np.stack([feature_major(a["c"]), feature_major(a["c_ctx"])], axis=2).reshape(P, -1)
    at = {"kv0": Q_RANK, "kv1": Q_RANK + P, "ql0": 0, "ql1": P, "ql2": 2 * P}
    for n, name in enumerate(("q0", "q1", "ff0", "ff1", "fb0", "fb1", "iv", "iv", "og0", "og1")):
        at.setdefault(name, MLA_COLS + P * n)
    for n, name in enumerate(("z0", "z1", "xs0", "xs1", "B", "C")):
        at[name] = SSM_AT + P * n
    span = lambda lo, n: np.arange(lo, lo + n)
    misc = np.concatenate([span(Q_RANK + KV_RANK, ROPE), span(SSM_AT + 6 * P, 8), np.zeros(88, np.int64)])
    cols = {"ada": [span(256 * i, 256) for i in range(N_ADA)],
            "in": [np.concatenate([misc if n == "misc" else span(at[n] + (P if (n == "iv" and j) else 0), P)
                                   for j, n in enumerate(names)]) for names in IN_TILES],
            "out": [span(256 * i, 256) for i in range(N_OUT)],
            "fi": [np.concatenate([span(P * i, P), span(FFN + P * i, P)]) for i in range(N_FI)]}
    per = np.arange(HEADS)[:, None]
    cols["qb"] = [np.concatenate([(per * QK + np.arange(NOPE)).ravel(), (per * QK + NOPE + np.arange(ROPE)).ravel()])]
    cols["kvb"] = [np.concatenate([(per * 128 + np.arange(NOPE)).ravel(), (per * 128 + NOPE + np.arange(VD)).ravel()])]
    src = {"ada": "w_ada", "in": "w_in", "qb": "mla_wqb", "kvb": "mla_wkvb", "out": "w_out", "fi": "w_ffn_in"}
    wt = {k: np.stack([np.stack([tiled(a[src[k]][l], c) for c in cols[k]]) for l in range(DEPTH)]) for k in src}
    fo = a["w_ffn_out"]
    wt["fo"] = np.stack([np.stack([tiled(fo[l][(i % 2) * 1408:(i % 2) * 1408 + 1408], span(256 * (i // 2), 256))
                                   for i in range(N_FO)]) for l in range(DEPTH)])
    c, m = constants()
    xin = np.concatenate([a["ctx"][0], a["x"][0]], axis=0)
    arrays = {f"in_w_{k}": np.ascontiguousarray(t.reshape(DEPTH, t.shape[1], P, -1)) for k, t in wt.items()}
    arrays |= {"in_vecs": v, "in_consts": c, "in_masks": m,
               "in_x": np.ascontiguousarray(xin.reshape(T, KD, P).transpose(2, 1, 0))}
    nc = _bacc.Bacc("TRN2", target_bir_lowering=False, num_devices=1)
    d = {n: nc.dram_tensor(n, x.shape, mybir.dt.from_np(x.dtype), kind="ExternalInput").ap() for n, x in arrays.items()}
    out = nc.dram_tensor("out_dram", (P, KD, SEQ), F32, kind="ExternalOutput").ap()
    build(nc, {k: d[f"in_w_{k}"] for k in wt}, d["in_vecs"], d["in_consts"], d["in_masks"], d["in_x"], out)
    r = _run(nc, [arrays], core_ids=[0])
    got = np.asarray(r.results[0]["out_dram"]).reshape(P, KD, SEQ)
    return np.ascontiguousarray(got.transpose(2, 1, 0).reshape(1, SEQ, D))
```

```python
from contextlib import ExitStack

import numpy as np

import concourse.bass as bass
from concourse import mybir

F32 = mybir.dt.float32
F16 = mybir.dt.float16
BF16 = mybir.dt.bfloat16
U8 = mybir.dt.uint8
ALU = mybir.AluOpType
ACT = mybir.ActivationFunctionType
AX = mybir.AxisListType

D = 1024
SEQ = 256
DEPTH = 2
GRID_W = 64
P = 128
T = 2 * SEQ
KD = D // P
HEADS, NOPE, ROPE, VD = 8, 64, 32, 64
QK = NOPE + ROPE
Q_RANK, KV_RANK = 384, 256
KQ, KKV = Q_RANK // P, KV_RANK // P
HG_HEADS, HG_W = 4, 256
SSM_HEADS, SSM_INNER, SSM_STATE, TAPS = 4, 256, 64, 5
FFN = 2816
KF = FFN // P
C = 128
NCH = T // C
MLA_COLS = Q_RANK + KV_RANK + ROPE
HG_COLS = 5 * HG_W
SSM_AT = MLA_COLS + HG_COLS
SCALE = QK ** -0.5
EPS = 1e-6
WS = 64.0
GATE_MAX = 44.0
N_ADA, N_IN, N_OUT, N_FI, N_FO = 24, 11, 4, KF, 12
UNIT = 2048
PAD = SEQ + TAPS - 1
HALVES = (64, 32, 16, 8, 4, 2, 1)
ORDER = ((0, 1, 2, 3), (1, 0, 3, 2))

V_BADA, V_N1, V_N2, V_QA, V_KVA, V_LB, V_HGN, V_CW, V_CB, V_DTB, V_ALOG, V_D, V_SN = (
    0, 48, 56, 64, 67, 69, 73, 75, 95, 99, 100, 101, 103)
V_LAYER = 105
V_FINAL = DEPTH * V_LAYER
V_C = V_FINAL + KD
V_COLS = V_C + 2 * KD
C_ID, C_ONES, C_B64, C_RESET, C_MF, C_MB, C_SEL, C_SELT, C_COS, C_SIN, C_PERM, C_SGN = (
    0, 128, 256, 384, 896, 1024, 1152, 2176, 2688, 2944, 3200, 3328)
C_COLS = C_SGN + 6

R_QL, R_KV, R_MISC, R_HQ, R_FF, R_IV, R_OG, R_Z, R_XBC, R_T = (
    0, 1536, 2560, 3072, 4096, 6144, 7168, 8192, 9216, 11296)
R_SIZE = R_T + 9728


def unit_order():
    us = [("ada", 0, i) for i in range(8)]
    rest = [("ada", 0, i) for i in range(8, N_ADA)]
    for i in range(N_IN):
        us.append(("in", 0, i))
        us += rest[:2 if i < 5 else 1]
        rest = rest[2 if i < 5 else 1:]
    us += [("qb", 0, 0), ("qb", 0, 1), ("kvb", 0, 0)] + [("out", 0, i) for i in range(N_OUT)]
    for i in range(N_FI):
        us += [("fi", 0, i), ("ada", 1, i)]
    for i in range(N_FO):
        us.append(("fo", 0, i))
        if i < N_ADA - N_FI:
            us.append(("ada", 1, N_FI + i))
    us += [("in", 1, i) for i in range(N_IN)] + [("qb", 1, 0), ("qb", 1, 1), ("kvb", 1, 0)]
    us += [("out", 1, i) for i in range(N_OUT)] + [("fi", 1, i) for i in range(N_FI)]
    us += [("fo", 1, i) for i in range(N_FO)]
    return us


UNITS = unit_order()
N_DIRECT = 8
AT_UNIT = {u: n for n, u in enumerate(UNITS)}
FO_KT = (8, 8, 6)
KT = [{"qb": KQ, "kvb": KKV, "fo": FO_KT[i % 3]}.get(kind, KD) for kind, l, i in UNITS]
SIZE = [kt * {"qb": 384, "kvb": 1024}.get(kind, 256) for kt, (kind, l, i) in zip(KT, UNITS)]
RING32, RING16 = 3, 4
AHEAD = RING16 - 1
GROUPS = [u for u in UNITS if u[0] in ("in", "out", "fi") or (u[0] == "fo" and u[2] % len(FO_KT) == 0)]
AT_GROUP = {u: n for n, u in enumerate(GROUPS)}
IN_TILES = (("kv1", "misc"), ("xs0", "xs1"), ("B", "C"), ("z0", "z1"), ("q0", "q1"), ("ff0", "ff1"),
            ("fb0", "fb1"), ("og0", "og1"), ("iv", "iv"), ("ql0", "ql1"), ("ql2", "kv0"))
LAT_ONLY = ("C", "z0", "z1", "q0", "q1", "og0", "og1", "ql0", "ql1", "ql2")


FIRST = {"xw": 6, "krdma": 16, "ssq1": 1, "tr": 2, "cb": 1, "bc": 4, "stp": 1, "rows_bc": 4, "y": 4, "yss": 2,
         "gKt": 1, "gSp": 1, "lss": 5, "gO": 1, "gP": 16, "go": 1, "gss": 2, "krp": 1, "qp": 11, "qrp": 2,
         "smx": 32, "mT": 8, "st": 32, "pv": 8, "ssq2": 1, "sq1": 8, "rstd1": 1, "xhi1": 16, "dsp": 1, "wexp": 2,
         "cth": 4, "tra": 1, "cbc": 2, "E_ssm": 8, "ysq": 2, "gl": 2, "yrs": 1, "gKe": 5, "gKe2": 3, "yhi": 2,
         "lsq": 5, "gE": 7, "lrs": 1, "lhi": 5, "gsq": 2, "grs": 2, "ghi": 2, "qb16": 2, "nm": 8, "ex": 32,
         "den": 8, "ohi": 4, "sq2": 8, "rstd2": 1, "xhi2": 16, "hhi": 22, "mod": 4, "tm1": 16, "xlo1": 16,
         "acc": 16, "wrow": 2, "rowd": 2, "conv": 7, "trv": 3, "cw": 8, "S_ssm": 24, "D": 32, "M": 8, "yv": 4,
         "ym": 4, "gk": 1, "gT": 1, "gKa": 2, "gKm": 4, "ylo": 2, "gS": 24, "gA": 28, "gKQ": 8, "gAT": 32,
         "lh": 5, "llo": 5, "gm": 2, "glo": 2, "krc": 1, "qn": 6, "Kn": 4, "Vv": 4, "Qd": 8, "kb16": 2, "mx": 32,
         "on": 8, "olo": 4, "tm2": 16, "xlo2": 16, "hlo": 22}


class Layer:

    def __init__(self, signals, l):
        self.signals, self.l = signals, l

    def __getitem__(self, name):
        return self.signals[name]

    def __call__(self, name, n):
        return self.signals[name], (FIRST.get(name, 0) if self.l else 0) + n


def build(nc, w, vecs_d, consts_d, masks_d, x_d, out_d):
    with ExitStack() as ctx:
        def sb(name, shape, dt=F32):
            return ctx.enter_context(nc.sbuf_tensor(name, shape, dt))

        def sem(name):
            return ctx.enter_context(nc.semaphore(name))

        w32 = [sb(f"w32_{i}", [P, UNIT]) for i in range(RING32)]
        w16 = [sb(f"w16_{i}", [P, 2, UNIT], F16) for i in range(RING16)]
        xT = sb("xT", [P, KD, T])
        act16 = sb("act16", [P, 2, KD, T], F16)
        R = sb("R", [P, R_SIZE])
        vecs = sb("vecs_sb", [P, V_COLS])
        cst = sb("cst", [P, C_COLS])
        masks = sb("masks_sb", [P, 8, C], U8)
        S = sb("S", [P, 2, 3, 2, P])
        rows = sb("rows", [P, T])
        rstd = sb("rstd", [P, T])
        th = sb("th", [P, 2, T])
        mod = sb("mod", [P, DEPTH, 48, 2])
        aff = sb("aff", [P, DEPTH, 4, KD, 2])
        cs = sb("cs", [P, 2, KD, 2])
        cs16 = sb("cs16", [P, KD, 2, 2], F16)
        ones16 = sb("ones16", [1, P], BF16)
        small = sb("small", [P, 128])
        rtok = sb("rtok", [P, NCH, 72])
        negm = sb("negm", [1, 2, T], BF16)
        eps = small[:, 0:1]
        lb4, olb4 = small[:, 4:8], small[:, 8:12]
        lbt = small[:, 12:24]
        hcw = small[:, 24:44]
        hcb = small[:, 44:48]
        acol = small[0:8, 48:49]
        lastf = small[0:8, 50:54]
        lastb = small[0:8, 54:58]
        mcol = small[:, 64:96]
        ET = small[:, 96:112]
        one = small[:, 1:2]
        ED = small[:, 112:128]

        B = [ctx.enter_context(nc.psum_tensor(f"bank{i}", [P, 512], F32)) for i in range(8)]

        def rr(start, size, pat=None, **kw):
            v = R[:, start:start + size]
            return v.rearrange(pat, **kw) if pat else v

        def const(at, n, p=P):
            return cst[0:p, at:at + n]

        ident, ones, b64 = const(C_ID, P), const(C_ONES, P), const(C_B64, P)
        perm, reset = const(C_PERM, P), const(C_RESET, T)
        seqs = lambda ap: ap.rearrange("p (s t) -> p s t", s=2)

        def hi_w(n, k, c0, m):
            v = w16[n % RING16][:, 0, 0:SIZE[n]].rearrange("p (k c) -> p k c", k=KT[n])
            return v[:, k, c0:c0 + m]

        def lo_w(n, k, c0, m):
            v = w16[n % RING16][:, 1, 0:SIZE[n]].rearrange("p (k c) -> p k c", k=KT[n])
            return v[:, k, c0:c0 + m]

        vecs_in = sem("vectors_landed")
        params = sem("constants_landed")
        masks_in = sem("masks_landed")
        direct = [sem(f"direct_unit_landed{i}") for i in range(N_DIRECT)]
        x_in = sem("x_landed")
        landed = [sem(f"weights_landed{i}") for i in range(RING32)]
        w_hi = sem("weights_high")
        w_lo = sem("weights_low")
        prod = sem("unit_products")
        evac = sem("groups_evacuated")
        tanh_s = sem("group_tanh")
        setup = sem("setup_done")
        cs_t = sem("c_tanh")
        cs_v = sem("c_silu")
        masks_s = sem("masks_cast")
        ach = sem("scalar_chain")
        dch = sem("vector_chain")
        names = ("mod sq1 ssq1 rstd1 tm1 xhi1 xlo1 sq2 ssq2 rstd2 tm2 xhi2 xlo2 hhi hlo "
                 "acc cth conv dsp wrow wexp rowd tr trv tra cb cbc bc cw xw stp S_ssm rows_bc D E_ssm M y yv "
                 "ysq yss yrs ym yhi ylo "
                 "gl gk gT gKa gKe gKm gKt gKe2 gSp gS gO gA gE gKQ gP gAT go gsq gss grs gm ghi glo "
                 "lbd lbe qb16 kb16 lsq lss lrs lh lhi llo krc krp krdma qn qp qrp Qd Kn Vv smx mx mT nm st ex pv den on ohi olo"
                 ).split()
        signals = {n: sem(n) for n in names}
        L = [Layer(signals, l) for l in range(DEPTH)]
        fin = {n: sem(f"fin_{n}") for n in ("sq", "ssq", "rstd", "y", "out")}

        def t0_of(l):
            return 0 if l < DEPTH - 1 else SEQ

        def out_chunks(l):
            return range(0 if l < DEPTH - 1 else 2, NCH)

        def vec(l, at, n):
            return vecs[:, l * V_LAYER + at:l * V_LAYER + at + n]

        def act32_out():
            return rr(4096, KD * SEQ, "p (k t) -> p k t", k=KD)

        def norm_ops(l):
            return 2 if t0_of(l) == 0 else 1

        def square_of(k, l=DEPTH):
            if l == 0:
                return rr(k * T, T)
            return act16[:, k // 4, 2 * (k % 4):2 * (k % 4) + 2, :].rearrange("p k t -> p (k t)").bitcast(F32)

        def max_copies():
            v = lambda at: rr(at, 2048).bitcast(BF16).rearrange("p (h t) -> p h t", h=HEADS)
            return v(R_HQ + 15872), v(R_HQ)

        def level_bufs(lv):
            at = R_T + 4096 if lv % 2 == 0 else R_XBC
            K = rr(at, 1024, "p (j t) -> p j t", j=2)
            Q = rr(at + 1024, 1024, "p (j t) -> p j t", j=2)
            if lv == len(HALVES):
                Q = rr(R_HQ, 1024, "p (j t) -> p j t", j=2)
            return K, Q

        def ssm_step(i, m):
            return 2 * (i - 4) + m

        def gates_after(l):
            return 4 + (5 + len(out_chunks(l))) // 2

        def chunk_step(l, step):
            n = step - 5
            return (n - 1 if 1 <= n <= len(out_chunks(l)) else None, n if n < len(out_chunks(l)) else None)

        def query_tiles(l):
            return range(t0_of(l) // P, T // P)

        def max_of(h, qt):
            return mcol[:, 4 * h + qt:4 * h + qt + 1]

        def latent16(k):
            if k < 4:
                return act16[:, :, k, :]
            return rstd[:, :].bitcast(F16).rearrange("p (a t) -> p a t", a=2)

        def latent_square(k):
            return rr(R_Z + (k % 2) * T, T)

        def ssm_bufs():
            return {
                "xs": rr(R_T + 4096, 1024, "p (g t) -> p g t", g=2),
                "yz": rr(R_Z, 1024, "p (g t) -> p g t", g=2),
                "B": rr(R_T + 5120, 512),
                "C": rr(R_T + 5632, 1024, "p (g t) -> p g t", g=2),
                "CB": rr(R_T + 8192, 1024, "p (g t) -> p g t", g=2),
                "Cw": rr(R_T + 2048, 2048, "p (d g t) -> p d g t", d=2, g=2),
                "M": rr(R_XBC, 1024, "p (b h t) -> p b h t", b=2, h=SSM_HEADS),
                "D": rr(R_XBC + 1024, 1024, "p (d h t) -> p d h t", d=2, h=SSM_HEADS),
                "sq": rr(R_XBC + 1024, 1024, "p (g t) -> p g t", g=2),
            }

        DG = ((0, 0), (0, 1), (1, 0), (1, 1))
        BC_BANK = (4, 5, 6, 4)

        def cvec():
            return vecs[:, V_C:V_C + 2 * KD].rearrange("p (k a) -> p k a", a=2)

        def h32(i):
            return rr(KF * T + (i % 2) * T, T)

        def direct_unit(n):
            return rr(KD * T + n * SIZE[n], SIZE[n])

        def landed_unit(n):
            return direct_unit(n) if n < N_DIRECT else w32[(n - N_DIRECT) % RING32][:, 0:SIZE[n]]

        masks32 = act16[:, 0, 0:4, :].rearrange("p k t -> p (k t)").bitcast(F32)

        block = ctx.enter_context(nc.Block())

        @block.sync
        def _(sp):
            def load_unit(n):
                kind, l, i = UNITS[n]
                if n >= N_DIRECT + RING32:
                    sp.wait_ge(w_hi, n - RING32 + 1)
                    sp.wait_ge(w_lo, n - RING32 + 1)
                sp.dma_start(landed_unit(n), w[kind][l, i, :, 0:SIZE[n]]).then_inc(landed[(n - N_DIRECT) % RING32], 16)

            def load_direct(n):
                kind, l, i = UNITS[n]
                sp.dma_start(direct_unit(n), w[kind][l, i]).then_inc(direct[n], 16)

            sp.dma_start(vecs[:, :], vecs_d).then_inc(vecs_in, 16)
            for n in range(N_DIRECT // 2):
                load_direct(n)
            sp.dma_start(cst[:, :], consts_d).then_inc(params, 16)
            sp.dma_start(xT[:, :, :], x_d).then_inc(x_in, 16)
            for n in range(N_DIRECT // 2, N_DIRECT):
                load_direct(n)
            sp.dma_start(masks32, masks_d).then_inc(masks_in, 16)
            for n in range(N_DIRECT, len(UNITS)):
                load_unit(n)
            sp.wait_ge(fin["y"], KD)
            sp.dma_start(out_d, act32_out()).then_inc(fin["out"], 16)
            sp.wait_ge(fin["out"], 16)

        @block.gpsimd
        def _(pool):
            pool.memset(S[:, :, :, :, :], 0.0).then_inc(setup, 1)
            pool.memset(rows[:, :], 0.0).then_inc(setup, 1)
            pool.memset(small[:, 0:1], EPS).then_inc(setup, 1)
            pool.memset(small[:, 1:2], 1.0).then_inc(setup, 1)
            for l in range(DEPTH):
                s = L[l]
                xtok = rr(R_T, 1024, "p (c h d) -> p c h d", c=NCH, h=SSM_HEADS)
                xw = rr(R_T + 6656, 1536, "p (n h d) -> p n h d", n=6, h=SSM_HEADS)
                pool.wait_ge(*s("tra", 1))
                pool.wait_ge(*s("trv", 3))
                for d in range(2):
                    for i in range(3):
                        c = ORDER[d][i]
                        wt = rtok[:, c, 64 + 4 * d:68 + 4 * d]
                        pool.tensor_tensor(xw[:, 3 * d + i, :, :], xtok[:, c, :, :],
                                           wt.unsqueeze(2).to_broadcast([P, SSM_HEADS, 64]),
                                           ALU.mult).then_inc(s["xw"], 1)
                pool.wait_ge(*s("krc", 1))
                KTt = rr(R_HQ + 6656, 4096, "p (h t) -> p h t", h=HEADS)
                pool.dma_start(KTt[NOPE:QK, :, :], rr(R_MISC, T)[0:ROPE, :].unsqueeze(1).to_broadcast([ROPE, HEADS, T])
                               ).then_inc(s["krdma"], 16)

        @block.tensor
        def _(pe):
            def mm3(ps, ahi, alo, bhi, blo, first, last):
                pe.matmul(ps, ahi, bhi, start=first, stop=False, skip_group_check=True)
                pe.matmul(ps, ahi, blo, start=False, stop=False, skip_group_check=True)
                return pe.matmul(ps, alo, bhi, start=False, stop=last, skip_group_check=True)

            def mm(ps, a, b, start=True, stop=True):
                return pe.matmul(ps, a, b, start=start, stop=stop, skip_group_check=True)

            def unit_ready(n):
                pe.wait_ge(w_hi, n + 1)
                pe.wait_ge(w_lo, n + 1)

            def ada(l, i):
                n = AT_UNIT["ada", l, i]
                unit_ready(n)
                if (l, i) == (0, 0):
                    pe.wait_ge(cs_t, 2)
                    pe.wait_ge(cs_v, 2)
                if (l, i) == (0, 8):
                    pe.wait_ge(*L[0]("mod", 2))
                if (l, i) == (1, 0):
                    pe.wait_ge(*L[0]("mod", 4))
                for m in range(2):
                    at = 4 * (2 * i + m)
                    for k in range(KD):
                        mm(B[7][:, at:at + 4], hi_w(n, k, m * P, P), cs16[:, k, :, :].rearrange("p a b -> p (a b)"),
                           k == 0, False)
                        last = mm(B[7][:, at:at + 2], lo_w(n, k, m * P, P), cs16[:, k, 0, :], False, k == KD - 1)
                last.then_inc(prod, 1)

            def group_banks(u):
                g = AT_GROUP[u]
                if g >= 2:
                    pe.wait_ge(evac, g - 1)
                return B[2 * (g % 2)], B[2 * (g % 2) + 1]

            def norm(s, q, t0):
                for k in range(KD):
                    pe.wait_ge(*s("sq" + q, k + 1))
                    last = mm(B[6][:, t0:T], ones, rr(k * T + t0, T - t0), k == 0, k == KD - 1)
                last.then_inc(s["ssq" + q], 1)

            def square_sums(l, g):
                t1, counted, done = ((0, L[l + 1]("sq1", 2 * g + 2), L[l + 1]["ssq1"]) if l + 1 < DEPTH else
                                     (SEQ, (fin["sq"], 2 * g + 2), fin["ssq"]))
                pe.wait_ge(*counted)
                for k in (2 * g, 2 * g + 1):
                    last = mm(B[6][:, t1:T], ones, square_of(k)[:, t1:T], k == 0, k == KD - 1)
                if k == KD - 1:
                    last.then_inc(done, 1)

            def inproj(l, i):
                s, t0 = L[l], t0_of(l)
                n = AT_UNIT["in", l, i]
                banks = group_banks(("in", l, i))
                unit_ready(n)
                if i == 0:
                    for k in range(KD):
                        pe.wait_ge(*s("xhi1", 2 * k + 2))
                        pe.wait_ge(*s("xlo1", 2 * k + 2))
                        for m, M in enumerate((P, 40)):
                            last = mm3(banks[m][0:M, :], hi_w(n, k, m * P, M), lo_w(n, k, m * P, M),
                                       act16[:, 0, k, :], act16[:, 1, k, :], k == 0, k == KD - 1)
                for m, name in enumerate(IN_TILES[i] if i else ()):
                    a = t0 if name in LAT_ONLY else 0
                    if m and i >= 4:
                        ssm(l, ssm_step(i, 0))
                    for k in range(KD):
                        if name != "iv":
                            last = mm3(banks[m][:, a:T], hi_w(n, k, m * P, P), lo_w(n, k, m * P, P),
                                       act16[:, 0, k, a:T], act16[:, 1, k, a:T], k == 0, k == KD - 1)
                    if name == "iv":
                        for c in (2 * m, 2 * m + 1):
                            for k in range(KD):
                                last = mm3(banks[m][:, (c % 2) * 256:(c % 2) * 256 + 256],
                                           act16[:, 0, k, c * C:c * C + C], act16[:, 1, k, c * C:c * C + C],
                                           hi_w(n, k, 0, 256), lo_w(n, k, 0, 256), k == 0, k == KD - 1)
                last.then_inc(prod, 1)
                if i >= 4:
                    ssm(l, ssm_step(i, 1))

            def ssm(l, step):
                s, OC, t0, b = L[l], out_chunks(l), t0_of(l), ssm_bufs()
                xtok = rr(R_T, 1024, "p (c f) -> p c f", c=NCH)
                btok = rr(R_T + 1024, 1024, "p (c f) -> p c f", c=NCH)
                xw = rr(R_T + 6656, 1536, "p (n h d) -> p n h d", n=6, h=SSM_HEADS)
                OE = rr(R_T + 6656 + 5 * 512, 512)
                if step == 0:
                    pe.wait_ge(*s("conv", 7))
                    for j in range(3):
                        for c in range(NCH):
                            src = (b["xs"][:, j, :] if j < 2 else b["B"])[:, c * C:c * C + C]
                            last = pe.transpose(B[4 + j][:, c * C:c * C + C], src, ident)
                    last.then_inc(s["tr"], 1)
                elif step == 1:
                    pe.wait_ge(*s("rowd", 2))
                    pe.wait_ge(*s("tra", 1))
                    for c in range(NCH):
                        last = pe.transpose(B[4][:, c * C:c * C + 72], rows[0:72, c * C:c * C + C],
                                            const(C_ID, 72, 72))
                    last.then_inc(s["tr"], 1)
                    pe.wait_ge(*s("trv", 2))
                    for g in range(2):
                        gs = slice(64 * g, 64 * g + 64)
                        for c in OC:
                            last = mm(B[5 + g][:, c * C:c * C + C], b["B"][gs, c * C:c * C + C],
                                      b["C"][gs, g, c * C:c * C + C])
                    last.then_inc(s["cb"], 1)
                elif step in (2, 3):
                    if step == 2:
                        pe.wait_ge(*s("trv", 3))
                        pe.wait_ge(*s("wexp", 2))
                    else:
                        pe.wait_ge(*s("cw", 2))
                    for n in (range(3) if step == 2 else (3,)):
                        if n in (1, 2):
                            pe.wait_ge(*s("cbc", n))
                        mm(B[BC_BANK[n]][:, :], const(C_SELT + n * P, P, 8), OE[0:8, :]).then_inc(s["bc"], 1)
                elif step == 4:
                    pe.wait_ge(*s("cw", 8))
                    pe.wait_ge(*s("xw", 6))
                    for i in range(3):
                        for n, (d, g) in enumerate(DG):
                            c = ORDER[d][i]
                            last = mm(B[4 + i][:, n * P:n * P + P], btok[:, c, g * P:g * P + P],
                                      xw[:, 3 * d + i, 2 * g:2 * g + 2, :].rearrange("p h d -> p (h d)"))
                    last.then_inc(s["stp"], 1)
                else:
                    done, new = chunk_step(l, step)
                    if new is not None:
                        if new:
                            pe.wait_ge(*s("D", 8 * new))
                        else:
                            pe.wait_ge(*s("S_ssm", 24))
                        c = OC[new]
                        for d in range(2):
                            for h in range(SSM_HEADS):
                                last = mm(B[4 + d][:, h * C:h * C + C], const(C_SEL + (4 * d + h) * P, P, 8),
                                          rows[0:8, c * C:c * C + C])
                        last.then_inc(s["rows_bc"], 1)
                    if done is not None:
                        c = OC[done]
                        to = lambda g: B[6][:, 256 * g + C * (c % 2):256 * g + C * (c % 2) + C]
                        if done == 2:
                            pe.wait_ge(*s("yv", 2))
                        for g in range(2):
                            for d in range(2):
                                i = ORDER[d].index(c) - 1
                                if i >= 0:
                                    mm(to(g), S[:, d, i, g, :], b["Cw"][:, d, g, c * C:c * C + C],
                                       c % 2 == 0 and g == 0 and (d == 0 or c == 0), False)
                        pe.wait_ge(*s("M", 2 * done + 2))
                        for h in range(SSM_HEADS):
                            r = 64 * (h % 2)
                            last = mm(to(h // 2)[r:r + 64, :], xtok[:, c, 64 * h:64 * h + 64],
                                      b["M"][:, done % 2, h, :], False, True)
                        last.then_inc(s["y"], 1)
                    elif new is None and step == 6 + len(OC):
                        for g in range(2):
                            pe.wait_ge(*s("ysq", g + 1))
                            mm(B[4 + g][:, t0:T], ones, b["sq"][:, g, t0:T]).then_inc(s["yss"], 1)

            def hgrn(l):
                s, OC, t0 = L[l], out_chunks(l), t0_of(l)
                KP = rr(R_T + 2048, 2048, "p (d j t) -> p d j t", d=2, j=2)
                QI = rr(R_T + 4096, 2048, "p (d j t) -> p d j t", d=2, j=2)
                KtT = rr(R_T + 8192, 1536, "p (d j i t) -> p d j i t", d=2, j=2, i=3)
                AT = rr(R_T + 6144, 2048, "p (c h t) -> p c h t", c=NCH, h=HG_HEADS)
                iv = rr(R_IV, 1024, "p (c f) -> p c f", c=NCH)
                pe.wait_ge(*s("ym", 4))
                pe.wait_ge(*s("gKm", 2))
                blocks = [(d, j, i) for d in range(2) for j in range(2) for i in range(3)]
                block_at = lambda n: B[4 + n // 4][:, (n % 4) * P:(n % 4) * P + P]
                for n, (d, j, i) in enumerate(blocks):
                    c = ORDER[d][i]
                    last = pe.transpose(block_at(n), KP[:, d, j, c * C:c * C + C], ident)
                last.then_inc(s["gKt"], 1)
                pe.wait_ge(*s("gKe2", 3))
                for n, (d, j, i) in enumerate(blocks):
                    last = mm(block_at(n), KtT[:, d, j, i, :], iv[:, ORDER[d][i], j * P:j * P + P])
                last.then_inc(s["gSp"], 1)
                pe.wait_ge(evac, AT_GROUP["in", l, N_IN - 1] + 1)
                pe.wait_ge(*s("mod", 3 if l == 0 else 2))
                for k in range(KQ + KKV):
                    if k == KQ:
                        pe.wait_ge(*s("gS", 24))
                    pe.wait_ge(*s("lsq", k + 1))
                    b, a = (7, t0) if k < KQ else (0, 0)
                    mm(B[b][:, a:T], ones, latent_square(k)[:, a:T], k in (0, KQ),
                       k in (KQ - 1, KQ + KKV - 1)).then_inc(s["lss"], 1)
                pe.wait_ge(*s("gKm", 4))
                for j in range(2):
                    first = True
                    for c in OC:
                        for d in range(2):
                            i = ORDER[d].index(c) - 1
                            if i >= 0:
                                last = mm(B[1 + j][:, c * C:c * C + C], S[:, d, i, j, :], QI[:, d, j, c * C:c * C + C],
                                          first, False)
                                first = False
                last.then_inc(s["gO"], 1)
                n = 0
                for lv in range(len(HALVES) + 1):
                    K, Q = level_bufs(lv)
                    pe.wait_ge(*s("gKQ", lv + 1))
                    for c2 in range(OC[0] // 2, 2):
                        if n >= 2:
                            pe.wait_ge(*s("gAT", 2 * n - 2))
                        for c in (2 * c2, 2 * c2 + 1):
                            for h in range(HG_HEADS):
                                hs = slice(64 * (h % 2), 64 * (h % 2) + 64)
                                to = 256 * (c % 2) + C * (h // 2)
                                last = mm(B[3 + 2 * (n % 2) + h % 2][:, to:to + C], K[hs, h // 2, c * C:c * C + C],
                                          Q[hs, h // 2, c * C:c * C + C])
                        last.then_inc(s["gP"], 1)
                        n += 1
                pe.wait_ge(*s("gAT", 2 * n))
                for c in OC:
                    for h in range(HG_HEADS):
                        r = 64 * (h % 2)
                        last = mm(B[1 + h // 2][r:r + 64, c * C:c * C + C], iv[:, c, 64 * h:64 * h + 64],
                                  AT[:, c, h, :], False, True)
                last.then_inc(s["go"], 1)
                for j in range(2):
                    pe.wait_ge(*s("gsq", j + 1))
                    mm(B[3 + j][:, t0:T], b64, rr(R_T + 2048 + j * T + t0, T - t0)).then_inc(s["gss"], 1)

            def mla(l):
                s, t0 = L[l], t0_of(l)
                QT = rr(R_HQ + 2560, 4096, "p (h t) -> p h t", h=HEADS)
                KTt = rr(R_HQ + 6656, 4096, "p (h t) -> p h t", h=HEADS)
                V = rr(R_HQ + 10752, 4096, "p (c h v) -> p c h v", c=NCH, h=HEADS)
                qr = rr(R_HQ + 14848, 1024, "p (j t) -> p j t", j=2)
                PT = rr(R_QL, 3072, "p (b x) -> p b x", b=2)
                pe.wait_ge(*s("gm", 2))
                mm(B[4][0:ROPE, 0:SEQ], const(C_PERM, ROPE, ROPE), rr(R_MISC, T)[0:ROPE, SEQ:T]).then_inc(s["krp"], 1)
                pe.wait_ge(*s("lhi", KQ))
                pe.wait_ge(*s("llo", KQ))
                for m in range(6):
                    n = AT_UNIT["qb", l, m // 3]
                    if m % 3 == 0:
                        unit_ready(n)
                    if m >= 4:
                        pe.wait_ge(*s("qn", m - 3))
                    for k in range(KQ):
                        last = mm3(B[m % 4][:, t0:T], hi_w(n, k, m % 3 * P, P), lo_w(n, k, m % 3 * P, P),
                                   latent16(k)[:, 0, t0:T], latent16(k)[:, 1, t0:T], k == 0, k == KQ - 1)
                    last.then_inc(s["qp"], 1) if m % 3 < 2 else last.then_inc(prod, 1)
                n = AT_UNIT["kvb", l, 0]
                unit_ready(n)
                pe.wait_ge(*s("lhi", KQ + KKV))
                pe.wait_ge(*s("llo", KQ + KKV))
                pe.wait_ge(*s("lrs", 1))
                pe.wait_ge(*s("krc", 1))
                kb = (2, 3, 5, 6, 0, 1, 2, 3)
                for m in range(8):
                    if m < 2:
                        pe.wait_ge(*s("qn", m + 3))
                    if m == 4:
                        pe.wait_ge(*s("qn", 6))
                    if m >= 6:
                        pe.wait_ge(*s("Kn", m - 5))
                    for k in range(KKV):
                        kh, kl = latent16(KQ + k)[:, 0, :], latent16(KQ + k)[:, 1, :]
                        if m < 4:
                            last = mm3(B[kb[m]][:, :], hi_w(n, k, m * P, P), lo_w(n, k, m * P, P), kh, kl,
                                       k == 0, k == KKV - 1)
                        else:
                            c = slice((m - 4) * C, (m - 4) * C + C)
                            last = mm3(B[kb[m]][:, :], kh[:, c], kl[:, c], hi_w(n, k, 512, 512), lo_w(n, k, 512, 512),
                                       k == 0, k == KKV - 1)
                    last.then_inc(s["qp"], 1) if m < 7 else last.then_inc(prod, 1)
                pe.wait_ge(*s("Kn", 4))
                for j in range(2):
                    mm(B[5 + j][:, 0:SEQ], perm, qr[:, j, SEQ:T]).then_inc(s["qrp"], 1)
                pe.wait_ge(*s("Vv", 4))
                for h in range(2):
                    for i in range(len(query_tiles(l))):
                        max_scores(l, h, i)
                    if h == 0:
                        max_row(l, 0)
                for h in range(HEADS + 1):
                    for kt in range(NCH):
                        if h < HEADS:
                            a = t0 if kt < 2 else SEQ
                            st = B[kt][:, a:T]
                            if kt == 0:
                                pe.wait_ge(*s("nm", h + 1))
                            if h >= 1:
                                pe.wait_ge(*s("ex", 4 * (h - 1) + kt + 1))
                            mm(st, KTt[0:QK, h, kt * C:kt * C + C], QT[0:QK, h, a:T], True, False)
                            mm(st, ones16[:, :], negm[:, h % 2, a:T], False, True).then_inc(s["st"], 1)
                            if kt == 0 and h + 1 < HEADS:
                                max_row(l, h + 1)
                            if h + 2 < HEADS and kt < len(query_tiles(l)):
                                max_scores(l, h + 2, kt)
                    if h >= 1:
                        g = h - 1
                        ob = B[5 + g % 2]
                        if g >= 2:
                            pe.wait_ge(*s("on", g - 1))
                        for kt in range(NCH):
                            a = t0 if kt < 2 else SEQ
                            pe.wait_ge(*s("ex", 4 * g + kt + 1))
                            off = 512 * kt if kt < 2 else 1024 + 256 * (kt - 2) - SEQ
                            last = mm(ob[:, a:T], V[:, kt, g, :], PT[:, g % 2, off + a:off + T],
                                      kt == 0, kt == NCH - 1)
                        last.then_inc(s["pv"], 1)

            def max_scores(l, h, i):
                s = L[l]
                Qb, Kb = max_copies()
                n = h * len(query_tiles(l)) + i
                qt = query_tiles(l)[i]
                keys = SEQ if qt < 2 else T
                if i == 0 and h % 4 == 0:
                    pe.wait_ge(*s("qb16", h // 4 + 1))
                    pe.wait_ge(*s("kb16", h // 4 + 1))
                if n >= 2:
                    pe.wait_ge(*s("mx", n - 1))
                if i == 1 and h >= 1:
                    pe.wait_ge(*s("nm", h))
                mm(B[(7, 4)[i % 2]][:, 0:keys], Qb[0:QK, h, qt * P:qt * P + P], Kb[0:QK, h, 0:keys]
                   ).then_inc(s["smx"], 1)

            def max_row(l, h):
                s = L[l]
                pe.wait_ge(*s("mx", (h + 1) * len(query_tiles(l))))
                for qt in query_tiles(l):
                    last = pe.transpose(B[4][0:1, qt * P:qt * P + P], max_of(h, qt), ident)
                last.then_inc(s["mT"], 1)

            def outproj(l):
                s, t0 = L[l], t0_of(l)
                for i in range(N_OUT):
                    n = AT_UNIT["out", l, i]
                    banks = group_banks(("out", l, i))
                    unit_ready(n)
                    if i == 0:
                        pe.wait_ge(*s("ohi", 4))
                        pe.wait_ge(*s("olo", 4))
                        pe.wait_ge(*s("ghi", 2))
                        pe.wait_ge(*s("glo", 2))
                        pe.wait_ge(*s("yhi", 2))
                        pe.wait_ge(*s("ylo", 2))
                    for m in range(2):
                        for k in range(KD):
                            last = mm3(banks[m][:, t0:T], hi_w(n, k, m * P, P), lo_w(n, k, m * P, P),
                                       act16[:, 0, k, t0:T], act16[:, 1, k, t0:T], k == 0, k == KD - 1)
                    last.then_inc(prod, 1)

            def ffn(l):
                s, t0 = L[l], t0_of(l)
                h16 = rr(0, KF * T).bitcast(F16).rearrange("p (a k t) -> p a k t", a=2, k=KF)
                for i in range(N_FI):
                    n = AT_UNIT["fi", l, i]
                    banks = group_banks(("fi", l, i))
                    unit_ready(n)
                    for m, k in (((m, k) for m in range(2) for k in range(KD)) if i else
                                 ((m, k) for k in range(KD) for m in range(2))):
                            if i == 0 and m == 0:
                                pe.wait_ge(*s("xhi2", norm_ops(l) * (k + 1)))
                                pe.wait_ge(*s("xlo2", norm_ops(l) * (k + 1)))
                            last = mm3(banks[m][:, t0:T], hi_w(n, k, m * P, P), lo_w(n, k, m * P, P),
                                       act16[:, 0, k, t0:T], act16[:, 1, k, t0:T], k == 0, k == KD - 1)
                    last.then_inc(prod, 1)
                    if l == 0:
                        ada(1, i)
                for i in range(N_FO):
                    n = AT_UNIT["fo", l, i]
                    if i % 3 == 0:
                        banks = group_banks(("fo", l, i))
                    unit_ready(n)
                    for m in range(2):
                        for k in range(FO_KT[i % 3]):
                            kf = 8 * (i % 3) + k
                            if i < 3 and m == 0:
                                pe.wait_ge(*s("hhi", kf + 1))
                                pe.wait_ge(*s("hlo", kf + 1))
                            last = mm3(banks[m][:, t0:T], hi_w(n, k, m * P, P), lo_w(n, k, m * P, P),
                                       h16[:, 0, kf, t0:T], h16[:, 1, kf, t0:T], kf == 0, kf == KF - 1)
                    last.then_inc(prod, 1)
                    if l == 0 and i < N_ADA - N_FI:
                        ada(1, N_FI + i)
                    if i % 3 == 2 and i > 2:
                        square_sums(l, i // 3 - 1)
                square_sums(l, N_FO // 3 - 1)

            for i in range(N_DIRECT // 2):
                ada(0, i)
            pe.wait_ge(params, 16)
            norm(L[0], "1", 0)
            for i in range(N_DIRECT // 2, N_DIRECT):
                ada(0, i)
            nxt = N_DIRECT
            for l in range(DEPTH):
                for i in range(N_IN):
                    inproj(l, i)
                    if l == 0:
                        for _ in range(2 if i < 5 else 1):
                            ada(0, nxt)
                            nxt += 1
                hgrn(l)
                mla(l)
                outproj(l)
                norm(L[l], "2", t0_of(l))
                ffn(l)

        @block.scalar
        def _(act):
            chain = [0]

            def link(ins):
                chain[0] += 1
                ins.then_inc(ach, 1)
                act.wait_ge(ach, chain[0])

            def high(n):
                if n < N_DIRECT:
                    act.wait_ge(direct[n], 16)
                else:
                    act.wait_ge(landed[(n - N_DIRECT) % RING32], 16 * ((n - N_DIRECT) // RING32 + 1))
                if n >= RING16:
                    act.wait_ge(prod, n - RING16 + 1)
                act.activation(w16[n % RING16][:, 0, 0:SIZE[n]], landed_unit(n), ACT.Copy,
                               scale=WS).then_inc(w_hi, 1)

            def ahead(u):
                if AT_UNIT[u] + AHEAD < len(UNITS):
                    high(AT_UNIT[u] + AHEAD)

            def exp_and_log():
                act.preload_act_table_set("natural_log_exp_and_others")

            def rsqrt_mean(out, ps, width, done):
                link(act.activation(out, ps, ACT.Ln, bias=eps, scale=1.0 / width))
                act.activation(out, out, ACT.Exp, scale=-0.5).then_inc(done, 1)

            def norm(l, q, t0, group_of):
                s = L[l]
                for k in range(KD if q == "2" or l == 0 else 0):
                    if group_of is not None:
                        act.wait_ge(evac, AT_GROUP[group_of(k)] + 1)
                    act.activation(rr(k * T + t0, T - t0), xT[:, k, t0:T], ACT.Square).then_inc(s["sq" + q], 1)
                if l == 0 and q == "1":
                    for n in range(N_DIRECT // 2, N_DIRECT):
                        high(n)
                act.wait_ge(*s("ssq" + q, 1))
                rsqrt_mean(rstd[:, t0:T], B[6][:, t0:T], D, s["rstd" + q])
                if l == 0 and q == "1":
                    act.wait_ge(masks_in, 16)
                    act.activation(masks[:, :, :], masks32.rearrange("p (n t) -> p n t", n=8), ACT.Copy
                                   ).then_inc(masks_s, 1)
                    act.wait_ge(masks_s, 1)
                    for n in range(N_DIRECT, N_DIRECT + AHEAD):
                        high(n)
                m = 0
                for k in range(KD):
                    for sq in range(t0 // SEQ, 2):
                        m += 1
                        act.wait_ge(*s("tm" + q, m))
                        a = slice(sq * SEQ, sq * SEQ + SEQ)
                        act.activation(act16[:, 0, k, a], rr(4096 + k * T, T)[:, a], ACT.Identity,
                                       bias=mod[:, l, (0 if q == "1" else 24) + k, 1 - sq:2 - sq]
                                       ).then_inc(s["xhi" + q], 1)

            def inproj(l, i):
                t0 = t0_of(l)
                ahead(("in", l, i))
                if i >= 4:
                    ssm(l, ssm_step(i, 0))
                if i == N_IN - 1:
                    hgrn_decays(l)
                if l == 0:
                    for _ in range(2 if i < 5 else 1):
                        ahead(("ada", 0, nxt[0]))
                        nxt[0] += 1
                if IN_TILES[i][0] in ("z0", "q0", "og0"):
                    act.wait_ge(prod, AT_UNIT["in", l, i] + 1)
                    g = AT_GROUP["in", l, i]
                    act.wait_ge(evac, g)
                    for m in range(2):
                        last = act.activation(th[:, m, t0:T], B[2 * (g % 2) + m][:, t0:T], ACT.Tanh, scale=0.5 / WS)
                    last.then_inc(tanh_s, 1)
                if i == 1:
                    dt_rows(l)
                if i in (2, 3):
                    act.wait_ge(*L[l]("acc", 8 * i - 8))
                    cth = rr(R_T + 2048, 2048, "p (j t) -> p j t", j=4)
                    acc = rr(R_T, 2048, "p (j t) -> p j t", j=4)
                    for j in ((0, 1) if i == 2 else (2, 3)):
                        a = t0 if j == 3 else 0
                        act.activation(cth[:, j, a:T], acc[:, j, a:T], ACT.Tanh).then_inc(L[l]["cth"], 1)
                if i >= 4:
                    ssm(l, ssm_step(i, 1))
                if i == gates_after(l):
                    hgrn_gates(l)

            def dt_rows(l):
                s = L[l]
                r = lambda i: rr(R_T + 6656 + 512 * i, 512)[0:8, :]
                act.wait_ge(evac, AT_GROUP["in", l, 0] + 1)
                link(act.activation(r(1), r(0), ACT.Abs))
                link(act.activation(r(1), r(1), ACT.Exp, scale=-1.0))
                act.activation(acol, vec(l, V_ALOG, 1)[0:8, :], ACT.Exp)
                act.activation(r(1), r(1), ACT.Ln, bias=one[0:8, :]).then_inc(s["dsp"], 1)
                act.wait_ge(*s("wrow", 2))
                act.activation(r(0), r(0), ACT.Exp).then_inc(s["wexp"], 1)
                act.activation(r(5), r(5), ACT.Exp).then_inc(s["wexp"], 1)

            nxt = [8]

            def ssm(l, step):
                s, t0, OC, b = L[l], t0_of(l), out_chunks(l), ssm_bufs()
                xtok = rr(R_T, 1024, "p (c g f) -> p c g f", c=NCH, g=2)
                if step == 0:
                    act.wait_ge(*s("tr", 1))
                    act.activation(xtok[:, :, 0, :], B[4][:, :].rearrange("p (c f) -> p c f", c=NCH), ACT.Copy)
                    act.activation(xtok[:, :, 1, :], B[5][:, :].rearrange("p (c f) -> p c f", c=NCH),
                                   ACT.Copy).then_inc(s["tra"], 1)
                elif step == 1:
                    act.wait_ge(*s("cb", 1))
                    for g in range(2):
                        act.activation(b["CB"][:, g, t0:T], B[5 + g][:, t0:T], ACT.Copy).then_inc(s["cbc"], 1)
                elif step >= 5:
                    n = chunk_step(l, step)[1]
                    if n is not None:
                        for d in range(2):
                            act.wait_ge(*s("D", 8 * n + 4 * d + 4))
                            act.activation(b["D"][:, d, :, :], b["D"][:, d, :, :], ACT.Exp,
                                           scale=1.0 if d == 0 else -1.0).then_inc(s["E_ssm"], 1)
                    elif step == 5 + len(OC):
                        for g in range(2):
                            act.wait_ge(*s("ym", g + 1))
                            act.activation(b["sq"][:, g, t0:T], b["yz"][:, g, t0:T], ACT.Square
                                           ).then_inc(s["ysq"], 1)
                    elif step == 6 + len(OC):
                        act.wait_ge(*s("yss", 2))
                        for g in range(2):
                            last = act.activation(b["sq"][:, g, t0:T], B[4 + g][:, t0:T], ACT.Ln, bias=eps,
                                                  scale=1.0 / P)
                        link(last)
                        act.activation(b["sq"][:, :, t0:T], b["sq"][:, :, t0:T], ACT.Exp,
                                       scale=-0.5).then_inc(s["yrs"], 1)

            def ssm_out(l):
                s, t0, b = L[l], t0_of(l), ssm_bufs()
                act.wait_ge(prod, AT_UNIT["in", l, N_IN - 1] + 1)
                for g in range(2):
                    act.wait_ge(*s("ym", g + 3))
                    act.activation(act16[:, 0, 6 + g, t0:T], b["yz"][:, g, t0:T], ACT.Copy).then_inc(s["yhi"], 1)

            def latent_square_of(l, k):
                s, a = L[l], t0_of(l) if k < KQ else 0
                if k >= 2:
                    act.wait_ge(*s("lss", k - 1))
                act.activation(latent_square(k)[:, a:T], rr(R_QL + k * T + a, T - a), ACT.Square
                               ).then_inc(s["lsq"], 1)

            def latent_norm(l):
                s, t0 = L[l], t0_of(l)
                act.wait_ge(*s("lss", KQ + KKV))
                act.activation(th[:, 0, t0:T], B[7][:, t0:T], ACT.Ln, bias=eps, scale=1.0 / Q_RANK)
                link(act.activation(th[:, 1, :], B[0][:, :], ACT.Ln, bias=eps, scale=1.0 / KV_RANK))
                act.activation(th[:, 0, t0:T], th[:, 0, t0:T], ACT.Exp, scale=-0.5)
                act.activation(th[:, 1, :], th[:, 1, :], ACT.Exp, scale=-0.5).then_inc(s["lrs"], 1)

            def hgrn_gates(l):
                s = L[l]
                ff, E = rr(R_FF, 2048), rr(R_T + 2048, 2048)
                act.wait_ge(*s("y", len(out_chunks(l))))
                act.wait_ge(evac, AT_GROUP["in", l, 6] + 1)
                if l:
                    act.wait_ge(*s("lbd", 1))
                    act.activation(lbt[:, 4:12], lbt[:, 4:12], ACT.Exp).then_inc(s["lbe"], 1)
                link(act.activation(E, ff, ACT.Exp))
                act.activation(E, E, ACT.Ln, bias=one).then_inc(s["gl"], 1)
                act.wait_ge(*s("gk", 1))
                if l == 0:
                    act.activation(ff, ff, ACT.Exp).then_inc(s["gl"], 1)
                else:
                    act.activation(ff, ff, ACT.Exp)
                    act.activation(E, E, ACT.Exp, scale=-1.0).then_inc(s["gl"], 1)
                    act.wait_ge(*s("gk", 5))
                    act.activation(E, E, ACT.Ln).then_inc(s["gl"], 1)

            def hgrn_decays(l):
                s = L[l]
                E = rr(R_T + 2048, 2048)
                cum = rr(R_T, 2048, "p (d x) -> p d x", d=2)
                QI = rr(R_T + 4096, 2048, "p (d x) -> p d x", d=2)
                act.wait_ge(*s("ym", 2))
                act.wait_ge(*s("gT", 1))
                act.activation(ET, small[:, 96:112], ACT.Exp).then_inc(s["gKe"], 1)
                act.activation(QI[:, 0, :], cum[:, 0, :], ACT.Exp).then_inc(s["gKe"], 1)
                act.wait_ge(*s("gKa", 2))
                act.activation(E[:, 1024:2048], cum[:, 1, :], ACT.Exp).then_inc(s["gKe"], 1)
                act.activation(E[:, 0:1024], E[:, 0:1024], ACT.Exp).then_inc(s["gKe"], 1)
                act.activation(QI[:, 1, :], QI[:, 1, :], ACT.Exp).then_inc(s["gKe"], 1)

            def hgrn(l):
                s, t0, OC = L[l], t0_of(l), out_chunks(l)
                KtT = rr(R_T + 8192, 1536, "p (b x) -> p b x", b=3)
                act.wait_ge(*s("gKt", 1))
                for b in range(3):
                    act.activation(KtT[:, b, :], B[4 + b][:, :], ACT.Copy).then_inc(s["gKe2"], 1)
                ssm_out(l)
                act.wait_ge(*s("ylo", 2))
                for k in range(2):
                    latent_square_of(l, k)
                for k in range(2, KQ + KKV):
                    latent_square_of(l, k)
                E4 = rr(R_T + 2048, 2048, "p (d j t) -> p (d j) t", d=2, j=2)
                for lv in range(len(HALVES)):
                    act.wait_ge(*s("gA", 4 * lv + 4))
                    act.activation(E4[:, :, t0:T], E4[:, :, t0:T], ACT.Exp).then_inc(s["gE"], 1)
                    if lv == 0:
                        latent_norm(l)
                    if lv == 1:
                        for k in range(KQ + KKV):
                            a = t0 if k < KQ else 0
                            act.wait_ge(*s("lh", k + 1))
                            act.activation(latent16(k)[:, 0, a:T], rr(R_QL + k * T + a, T - a), ACT.Copy
                                           ).then_inc(s["lhi"], 1)
                sq = rr(R_T + 2048, 1024, "p (j t) -> p j t", j=2)
                r = rr(R_T + 3072, 1024, "p (j t) -> p j t", j=2)
                act.wait_ge(*s("go", 1))
                for j in range(2):
                    act.activation(sq[:, j, t0:T], B[1 + j][:, t0:T], ACT.Square).then_inc(s["gsq"], 1)
                for j in range(2):
                    act.wait_ge(*s("gss", j + 1))
                    rsqrt_mean(r[:, j, t0:T], B[3 + j][:, t0:T], 64, s["grs"])
                mx = rr(R_T + 4096, 1024, "p (j t) -> p j t", j=2)
                for j in range(2):
                    act.wait_ge(*s("gm", j + 1))
                    act.activation(act16[:, 0, 4 + j, t0:T], mx[:, j, t0:T], ACT.Copy).then_inc(s["ghi"], 1)

            def mla(l):
                s, t0 = L[l], t0_of(l)
                PT = rr(R_QL, 3072, "p (b x) -> p b x", b=2)
                QT = rr(R_HQ + 2560, 4096, "p (h t) -> p h t", h=HEADS)
                KTt = rr(R_HQ + 6656, 4096, "p (h t) -> p h t", h=HEADS)
                ahead(("qb", l, 0))
                ahead(("qb", l, 1))
                ahead(("kvb", l, 0))
                Qb, _ = max_copies()
                act.wait_ge(*s("Qd", 8))
                for h4 in (0, 4):
                    act.activation(Qb[0:QK, h4:h4 + 4, t0:T], QT[0:QK, h4:h4 + 4, t0:T], ACT.Copy
                                   ).then_inc(s["qb16"], 1)
                exp_and_log()
                max_negative(l, 0)
                for h in range(HEADS):
                    for kt in range(NCH):
                        a = t0 if kt < 2 else SEQ
                        off = 512 * kt if kt < 2 else 1024 + 256 * (kt - 2) - SEQ
                        if h >= 2 and kt == 0:
                            act.wait_ge(*s("pv", h - 1))
                        if h == 0 and kt == 0:
                            act.wait_ge(*s("llo", 5))
                        act.wait_ge(*s("st", 4 * h + kt + 1))
                        act.activation(PT[:, h % 2, off + a:off + T], B[kt][:, a:T], ACT.Exp,
                                       scale=SCALE).then_inc(s["ex"], 1)
                        if kt == 0 and h + 1 < HEADS:
                            max_negative(l, h + 1)
                    if h >= 1:
                        mla_den(l, h - 1)
                mla_den(l, HEADS - 1)

            def max_negative(l, h):
                s, t0 = L[l], t0_of(l)
                act.wait_ge(*s("mT", h + 1))
                if h >= 2:
                    act.wait_ge(*s("st", 4 * (h - 1)))
                act.activation(negm[:, h % 2, t0:T], B[4][0:1, t0:T], ACT.Copy, scale=-1.0).then_inc(s["nm"], 1)

            def mla_den(l, h):
                s, t0 = L[l], t0_of(l)
                rd = rstd if h % 2 == 0 else th[:, 0, :]
                o32 = rr(R_HQ + 14848, 1024, "p (b t) -> p b t", b=2)
                act.wait_ge(*s("pv", h + 1))
                if h >= 2:
                    act.wait_ge(*s("on", h - 1))
                link(act.activation(rd[0:64, t0:T], B[5 + h % 2][64:128, t0:T], ACT.Ln))
                act.activation(rd[0:64, t0:T], rd[0:64, t0:T], ACT.Exp, scale=-1.0).then_inc(s["den"], 1)
                if h % 2 == 1:
                    act.wait_ge(*s("on", h + 1))
                    act.activation(act16[:, 0, h // 2, t0:T], o32[:, (h // 2) % 2, t0:T], ACT.Copy
                                   ).then_inc(s["ohi"], 1)

            def squares(l, g):
                t1, done = (0, L[l + 1]["sq1"]) if l + 1 < DEPTH else (SEQ, fin["sq"])
                act.wait_ge(evac, AT_GROUP["fo", l, 3 * g] + 1)
                for k in (2 * g, 2 * g + 1):
                    act.activation(square_of(k)[:, t1:T], xT[:, k, t1:T], ACT.Square).then_inc(done, 1)

            def ffn(l):
                s, t0 = L[l], t0_of(l)
                h16 = rr(0, KF * T).bitcast(F16).rearrange("p (a k t) -> p a k t", a=2, k=KF)

                def hidden_high(i):
                    act.wait_ge(evac, AT_GROUP["fi", l, i] + 1)
                    act.activation(h16[:, 0, i, t0:T], h32(i)[:, t0:T], ACT.Copy).then_inc(s["hhi"], 1)

                for i in range(N_FI):
                    ahead(("fi", l, i))
                    if l == 0:
                        ahead(("ada", 1, i))
                    if i >= 1:
                        hidden_high(i - 1)
                    g = AT_GROUP["fi", l, i]
                    act.wait_ge(prod, AT_UNIT["fi", l, i] + 1)
                    if i >= 2:
                        act.wait_ge(evac, g - 1)
                    act.activation(th[:, i % 2, t0:T], B[2 * (g % 2)][:, t0:T], ACT.Tanh,
                                   scale=0.5 / WS).then_inc(tanh_s, 1)
                hidden_high(N_FI - 1)
                for i in range(N_FO):
                    ahead(("fo", l, i))
                    if l == 0 and i < N_ADA - N_FI:
                        ahead(("ada", 1, N_FI + i))
                    if i % 3 == 2 and i > 2:
                        squares(l, i // 3 - 1)
                squares(l, N_FO // 3 - 1)

            act.wait_ge(vecs_in, 16)
            act.wait_ge(setup, 4)
            act.activation(cs[:, 1, :, :], cvec(), ACT.Tanh, scale=0.5).then_inc(cs_t, 1)
            act.wait_ge(cs_v, 1)
            act.activation(cs16[:, :, 0, :], cs[:, 0, :, :], ACT.Copy).then_inc(cs_t, 1)
            for n in range(N_DIRECT // 2):
                high(n)
            act.wait_ge(x_in, 16)
            for l in range(DEPTH):
                s = L[l]
                if l == 0:
                    norm(l, "1", 0, None)
                    act.wait_ge(params, 16)
                    act.activation(ones16[:, :], const(C_ONES, P, 1), ACT.Copy)
                else:
                    norm(l, "1", 0, None)
                for i in range(N_IN):
                    inproj(l, i)
                hgrn(l)
                mla(l)
                for i in range(N_OUT):
                    ahead(("out", l, i))
                norm(l, "2", t0_of(l), lambda k: ("out", l, k // 2))
                ffn(l)
            act.wait_ge(fin["ssq"], 1)
            rsqrt_mean(rstd[:, SEQ:T], B[6][:, SEQ:T], D, fin["rstd"])

        @block.vector
        def _(dve):
            chain = [0]

            def mark(ins):
                chain[0] += 1
                ins.then_inc(dch, 1)

            def sync():
                dve.wait_ge(dch, chain[0])

            def link(ins):
                mark(ins)
                sync()

            def low(n):
                dve.wait_ge(w_hi, n + 1)
                dve.scalar_tensor_tensor(w16[n % RING16][:, 1, 0:SIZE[n]], landed_unit(n), WS,
                                         w16[n % RING16][:, 0, 0:SIZE[n]], ALU.mult, ALU.subtract).then_inc(w_lo, 1)

            def ahead(u):
                if AT_UNIT[u] + AHEAD < len(UNITS):
                    low(AT_UNIT[u] + AHEAD)

            def modulation(l, m0, m1):
                ps = B[7][:, 4 * m0:4 * m1].rearrange("p (m a) -> p m a", a=4)
                o = mod[:, l, m0:m1, :]
                b = vec(l, V_BADA + m0, m1 - m0).unsqueeze(2).to_broadcast([P, m1 - m0, 2])
                dve.scalar_tensor_tensor(o, ps[:, :, 0:2], 1.0 / WS, b, ALU.mult, ALU.add).then_inc(L[l]["mod"], 1)
                n = 1 if m0 == 0 else 3
                dve.wait_ge(*L[l]("mod", n))
                dve.scalar_tensor_tensor(o, ps[:, :, 2:4], 1.0 / WS, o, ALU.mult, ALU.add).then_inc(L[l]["mod"], 1)
                dve.wait_ge(*L[l]("mod", n + 1))

            def gains(l, which):
                g = vec(l, V_N1 if which == 0 else V_N2, KD).unsqueeze(2).to_broadcast([P, KD, 2])
                at = 8 if which == 0 else 32
                link(dve.scalar_tensor_tensor(aff[:, l, which, :, :], mod[:, l, at:at + 8, :], 1.0, g,
                                              ALU.add, ALU.mult))

            def gate(l, which):
                at = 16 if which == 0 else 40
                link(dve.tensor_scalar(aff[:, l, 2 + which, :, :], mod[:, l, at:at + 8, :], 1.0 / WS, None, ALU.mult))

            def norm(l, q, t0):
                s = L[l]
                dve.wait_ge(*s("rstd" + q, 1))
                tm = rr(4096, KD * T, "p (k t) -> p k t", k=KD)
                parts = [(k, sq) for k in range(KD) for sq in range(t0 // SEQ, 2)]
                for m in range(len(parts) + 1):
                    if m < len(parts):
                        k, sq = parts[m]
                        a = slice(sq * SEQ, sq * SEQ + SEQ)
                        dve.scalar_tensor_tensor(tm[:, k, a], xT[:, k, a],
                                                 aff[:, l, 0 if q == "1" else 1, k, 1 - sq:2 - sq], rstd[:, a],
                                                 ALU.mult, ALU.mult).then_inc(s["tm" + q], 1)
                    if m:
                        k, sq = parts[m - 1]
                        a = slice(sq * SEQ, sq * SEQ + SEQ)
                        dve.wait_ge(*s("xhi" + q, m))
                        dve.scalar_tensor_tensor(act16[:, 1, k, a], tm[:, k, a],
                                                 mod[:, l, (0 if q == "1" else 24) + k, 1 - sq:2 - sq],
                                                 act16[:, 0, k, a], ALU.add, ALU.subtract).then_inc(s["xlo" + q], 1)

            def inproj(l, i):
                s, t0 = L[l], t0_of(l)
                ahead(("in", l, i))
                if i >= 4:
                    ssm(l, ssm_step(i, 0))
                if i == N_IN - 1:
                    hgrn_decays(l)
                if l == 0:
                    for _ in range(2 if i < 5 else 1):
                        ahead(("ada", 0, nxt[0]))
                        nxt[0] += 1
                g = AT_GROUP["in", l, i]
                ps = (B[2 * (g % 2)], B[2 * (g % 2) + 1])
                if IN_TILES[i][0] in ("z0", "q0", "og0"):
                    tanhs[0] += 1
                    dve.wait_ge(tanh_s, tanhs[0])
                else:
                    dve.wait_ge(prod, AT_UNIT["in", l, i] + 1)
                for m, name in enumerate(IN_TILES[i]):
                    a = t0 if name in LAT_ONLY else 0
                    if name in ("kv0", "kv1", "ql0", "ql1", "ql2"):
                        at = R_QL + T * ("ql0", "ql1", "ql2", "kv0", "kv1").index(name)
                        last = dve.tensor_scalar(rr(at + a, T - a), ps[m][:, a:T], 1.0 / WS, None, ALU.mult)
                    elif name == "misc":
                        dve.tensor_scalar(rr(R_MISC, T)[0:ROPE, :], ps[m][0:ROPE, :], 1.0 / WS, None, ALU.mult)
                        last = dve.tensor_scalar(rr(R_T + 6656, T)[0:8, :], ps[m][32:40, :], 1.0 / WS,
                                                 vec(l, V_DTB, 1)[0:8, :], ALU.mult, ALU.add)
                    elif name in ("xs0", "xs1", "B", "C"):
                        j = ("xs0", "xs1", "B", "C").index(name)
                        xbc = rr(R_XBC, 4 * 2 * PAD, "p (j s t) -> p j s t", j=4, s=2)
                        s0 = a // SEQ
                        last = dve.tensor_scalar(xbc[:, j, s0:2, 2:2 + SEQ], seqs(ps[m][:, :])[:, s0:2, :], 1.0 / WS,
                                                 None, ALU.mult)
                    elif name[0] == "f":
                        at = R_FF + T * (2 * (name[1] == "b") + int(name[2]))
                        last = dve.tensor_scalar(rr(at, T), ps[m][:, :], -1.0 / WS, GATE_MAX, ALU.mult, ALU.min)
                    elif name == "iv":
                        last = dve.tensor_scalar(rr(R_IV + 512 * m, 512), ps[m][:, :], 0.5 / WS / WS, None, ALU.mult)
                    else:
                        at = {"z": R_Z, "q": R_HQ, "o": R_OG}[name[0]] + T * int(name[-1])
                        last = dve.scalar_tensor_tensor(rr(at + a, T - a), th[:, m, a:T], 1.0, ps[m][:, a:T],
                                                        ALU.add, ALU.mult)
                last.then_inc(evac, 1)
                if i == 1:
                    conv(l, 0)
                    dt_rows(l)
                if i == 2:
                    conv(l, 1)
                    conv_silu(l, 0)
                if i == 3:
                    conv_silu(l, 1)
                if i >= 4:
                    ssm(l, ssm_step(i, 1))
                if i == gates_after(l):
                    hgrn_gates(l)

            def dt_rows(l):
                s = L[l]
                r = lambda i: rr(R_T + 6656 + 512 * i, 512)[0:8, :]
                ch = lambda ap: ap.rearrange("p (c t) -> p c t", c=NCH)
                sg = lambda i: cst[0:8, C_SGN + i:C_SGN + i + 1]
                dve.wait_ge(*s("dsp", 1))
                link(dve.scalar_tensor_tensor(r(2), r(0), 0.0, r(1), ALU.max, ALU.add))
                link(dve.tensor_scalar(r(3), r(2), acol, -1.0, ALU.mult, ALU.mult))
                link(dve.tensor_tensor_scan(r(4), cst[0:8, C_RESET:C_RESET + T], r(3), 0.0, ALU.mult, ALU.add))
                mark(dve.tensor_scalar(lastf, ch(r(4))[:, :, C - 1], sg(0), None, ALU.mult))
                mark(dve.tensor_scalar(lastb, ch(r(4))[:, :, C - 1], sg(1), None, ALU.mult))
                link(dve.scalar_tensor_tensor(rows[0:8, :], r(3), sg(2), r(4), ALU.mult, ALU.add))
                dve.scalar_tensor_tensor(ch(r(0)), ch(rows[0:8, :]), sg(3), lastf.unsqueeze(2).to_broadcast([8, NCH, C]),
                                         ALU.mult, ALU.add).then_inc(s["wrow"], 1)
                dve.scalar_tensor_tensor(ch(r(5)), ch(rows[0:8, :]), sg(4), lastb.unsqueeze(2).to_broadcast([8, NCH, C]),
                                         ALU.mult, ALU.add).then_inc(s["wrow"], 1)
                dve.wait_ge(*s("wexp", 1))
                dve.tensor_tensor(rows[64:72, :], r(0), r(2), ALU.mult).then_inc(s["rowd"], 1)
                dve.tensor_copy(rows[32:40, :], r(2)).then_inc(s["rowd"], 1)

            def conv(l, half):
                s = L[l]
                xbc = rr(R_XBC, 4 * 2 * PAD, "p (j s t) -> p j s t", j=4, s=2)
                acc = rr(R_T, 2048, "p (j t) -> p j t", j=4)
                if half == 0:
                    mark(dve.tensor_scalar(hcw, vec(l, V_CW, 20), 0.5, None, ALU.mult))
                    mark(dve.tensor_scalar(hcb, vec(l, V_CB, 4), 0.5, None, ALU.mult))
                    mark(dve.memset(xbc[:, :, :, 0:2].rearrange("p j s t -> p (j s) t"), 0.0))
                    link(dve.memset(xbc[:, :, :, 2 + SEQ:PAD].rearrange("p j s t -> p (j s) t"), 0.0))
                dve.wait_ge(evac, AT_GROUP["in", l, 1 + half] + 1)
                s0 = lambda j: t0_of(l) // SEQ if j == 3 else 0
                for tap in range(TAPS):
                    for n in range(2):
                        j = 2 * half + n
                        o = seqs(acc[:, j, :])[:, s0(j):2, :]
                        u = xbc[:, j, s0(j):2, tap:tap + SEQ]
                        wt = hcw[:, 4 * tap + j:4 * tap + j + 1]
                        if tap == 0:
                            mark(dve.tensor_scalar(o, u, wt, hcb[:, j:j + 1], ALU.mult, ALU.add))
                        else:
                            if tap >= 2:
                                dve.wait_ge(*s("acc", 8 * half + 2 * (tap - 2) + n + 1))
                            elif n == 0:
                                sync()
                            dve.scalar_tensor_tensor(o, u, wt, o, ALU.mult, ALU.add).then_inc(s["acc"], 1)

            def conv_silu(l, half):
                s, t0 = L[l], t0_of(l)
                acc = rr(R_T, 2048, "p (j t) -> p j t", j=4)
                cth = rr(R_T + 2048, 2048, "p (j t) -> p j t", j=4)
                b = ssm_bufs()
                for j in ((0, 1) if half == 0 else (2,)):
                    dve.wait_ge(*s("cth", j + 1))
                    o = b["xs"][:, j, :] if j < 2 else b["B"]
                    dve.scalar_tensor_tensor(o, cth[:, j, :], 1.0, acc[:, j, :], ALU.add,
                                             ALU.mult).then_inc(s["conv"], 1)
                if half == 0:
                    return
                dve.wait_ge(*s("cth", 4))
                for g in range(2):
                    for dup in range(2):
                        gs, ds = slice(64 * g, 64 * g + 64), slice(64 * dup, 64 * dup + 64)
                        dve.scalar_tensor_tensor(b["C"][ds, g, t0:T], cth[gs, 3, t0:T], 1.0, acc[gs, 3, t0:T], ALU.add,
                                                 ALU.mult).then_inc(s["conv"], 1)

            def ssm(l, step):
                s, t0, OC, b = L[l], t0_of(l), out_chunks(l), ssm_bufs()
                btok = rr(R_T + 1024, 1024, "p (cg u n) -> p cg u n", u=2, n=64)
                if step == 0:
                    dve.wait_ge(*s("tr", 1))
                    bsrc = B[6][:, :].rearrange("p (cg n) -> p cg n", n=64)
                    for dup in range(2):
                        dve.tensor_copy(btok[:, :, dup, :], bsrc).then_inc(s["trv"], 1)
                elif step == 1:
                    dve.wait_ge(*s("tr", 2))
                    dve.tensor_copy(rtok[:, :, :], B[4][:, :].rearrange("p (c r) -> p c r", c=NCH)[:, :, 0:72]
                                    ).then_inc(s["trv"], 1)
                elif step in (2, 3):
                    for n in (range(3) if step == 2 else (3,)):
                        d, g = DG[n]
                        ps = B[BC_BANK[n]]
                        dve.wait_ge(*s("bc", n + 1))
                        e = ps[:, :].rearrange("p (c t) -> p c t", c=NCH)[:, :, C - 1 if d == 0 else 0]
                        dve.tensor_copy(ED[:, 4 * n:4 * n + 4], e).then_inc(s["cw"], 1)
                        dve.tensor_tensor(b["Cw"][:, d, g, t0:T], b["C"][:, g, t0:T], ps[:, t0:T],
                                          ALU.mult).then_inc(s["cw"], 1)
                elif step == 4:
                    dve.wait_ge(*s("stp", 1))
                    dve.wait_ge(*s("cw", 8))
                    if l > 0:
                        dve.wait_ge(*L[l - 1]("go", 1))
                    states(s, "S_ssm", lambda d, g, i, r: B[4 + i][r, (2 * d + g) * P + r.start:(2 * d + g) * P + r.stop],
                           lambda d, g, c: ED[:, 4 * (2 * d + g) + c:4 * (2 * d + g) + c + 1])
                else:
                    done, n = chunk_step(l, step)
                    if n is not None:
                        c = OC[n]
                        D_ = b["D"]
                        dve.wait_ge(*s("rows_bc", n + 1))
                        if n:
                            dve.wait_ge(*s("M", 2 * n))
                        for d in range(2):
                            for h in range(SSM_HEADS):
                                dve.tensor_scalar(D_[:, d, h, :], B[4 + d][:, h * C:h * C + C],
                                                  rtok[:, c, 4 * d + h:4 * d + h + 1], 0.0, ALU.subtract,
                                                  ALU.min if d == 0 else ALU.max).then_inc(s["D"], 1)
                        for d in range(2):
                            dve.wait_ge(*s("E_ssm", 2 * n + d + 1))
                            for h in range(SSM_HEADS):
                                mark(dve.scalar_tensor_tensor(D_[:, d, h, :], D_[:, d, h, :],
                                                              rtok[:, c, 32 + 4 * d + h:33 + 4 * d + h],
                                                              const(C_MF if d == 0 else C_MB, C), ALU.mult, ALU.mult))
                        sync()
                        link(dve.tensor_tensor(D_[:, 0, :, :], D_[:, 0, :, :], D_[:, 1, :, :], ALU.add))
                        if n >= 2:
                            dve.wait_ge(*s("y", n - 1))
                        for g in range(2):
                            dve.tensor_tensor(b["M"][:, n % 2, 2 * g:2 * g + 2, :], D_[:, 0, 2 * g:2 * g + 2, :],
                                              b["CB"][:, g, c * C:c * C + C].unsqueeze(1).to_broadcast([P, 2, C]),
                                              ALU.mult).then_inc(s["M"], 1)
                    if done is not None and done % 2 == 1:
                        at = C * (OC[done] - 1)
                        dve.wait_ge(*s("y", done + 1))
                        for g in range(2):
                            y = b["xs"][:, g, at:at + 2 * C]
                            dve.scalar_tensor_tensor(y, y, vec(l, V_D + g, 1), B[6][:, 256 * g:256 * g + 256],
                                                     ALU.mult, ALU.add).then_inc(s["yv"], 1)
                    if step == 5 + len(OC):
                        dve.wait_ge(*s("yv", len(OC)))
                        for g in range(2):
                            z = b["yz"][:, g, t0:T]
                            dve.scalar_tensor_tensor(z, b["xs"][:, g, t0:T], 0.5 / WS, z, ALU.mult,
                                                     ALU.mult).then_inc(s["ym"], 1)
                    elif step == 6 + len(OC):
                        dve.wait_ge(*s("yrs", 1))
                        for g in range(2):
                            y = b["yz"][:, g, t0:T]
                            dve.scalar_tensor_tensor(y, y, vec(l, V_SN + g, 1), b["sq"][:, g, t0:T], ALU.mult,
                                                     ALU.mult).then_inc(s["ym"], 1)

            def ssm_out(l):
                s, t0, b = L[l], t0_of(l), ssm_bufs()
                for g in range(2):
                    dve.wait_ge(*s("yhi", g + 1))
                    dve.tensor_tensor(act16[:, 1, 6 + g, t0:T], b["yz"][:, g, t0:T], act16[:, 0, 6 + g, t0:T],
                                      ALU.subtract).then_inc(s["ylo"], 1)

            def states(s, done, added, decay):
                n = 0
                for i in range(3):
                    if i:
                        dve.wait_ge(*s(done, 8 * i))
                    for d, g in DG:
                        for r in (slice(0, 64), slice(64, 128)):
                            new = added(d, g, i, r)
                            to = S[r, d, i, g, r.start:r.stop]
                            if i == 0:
                                ins = dve.tensor_copy(to, new)
                            else:
                                ins = dve.scalar_tensor_tensor(to, S[r, d, i - 1, g, r.start:r.stop],
                                                               decay(d, g, ORDER[d][i])[r, :], new, ALU.mult, ALU.add)
                            ins.then_inc(s[done], 1)

            def hgrn_gates(l):
                s = L[l]
                ff, E = rr(R_FF, 2048), rr(R_T + 2048, 2048)
                k4 = rr(R_FF, 2048, "p (n t) -> p n t", n=4)
                cum = rr(R_T, 2048, "p (n t) -> p n t", n=4)
                if l:
                    a0, a1 = vec(0, V_LB, 4), vec(1, V_LB, 4)
                    link(dve.tensor_tensor(lbt[:, 0:4], a0, a1, ALU.max))
                    mark(dve.tensor_tensor(lbt[:, 4:8], a0, lbt[:, 0:4], ALU.subtract))
                    dve.tensor_tensor(lbt[:, 8:12], a1, lbt[:, 0:4], ALU.subtract).then_inc(s["lbd"], 1)
                    dve.wait_ge(*s("lbe", 1))
                    link(dve.tensor_tensor(lbt[:, 0:4], lbt[:, 4:8], lbt[:, 8:12], ALU.add))
                    link(dve.reciprocal(lbt[:, 0:4], lbt[:, 0:4]))
                    mark(dve.tensor_tensor(lb4, lbt[:, 8:12], lbt[:, 0:4], ALU.mult))
                    link(dve.tensor_tensor(olb4, lbt[:, 4:8], lbt[:, 0:4], ALU.mult))
                dve.wait_ge(*s("gl", 1))
                dve.tensor_tensor(ff, ff, E, ALU.subtract).then_inc(s["gk"], 1)
                dve.wait_ge(*s("gl", 2))
                if l:
                    for n in range(4):
                        dve.tensor_scalar(E[:, n * T:n * T + T], E[:, n * T:n * T + T], olb4[:, n:n + 1],
                                          lb4[:, n:n + 1], ALU.mult, ALU.add).then_inc(s["gk"], 1)
                    for n in range(4):
                        mark(dve.tensor_scalar(k4[:, n, :], k4[:, n, :], olb4[:, n:n + 1], None, ALU.mult))
                    dve.wait_ge(*s("gl", 3))
                for n in range(4):
                    mark(dve.tensor_tensor_scan(cum[:, n, :], reset, E[:, n * T:n * T + T], 0.0, ALU.mult,
                                                ALU.add if l else ALU.subtract))
                sync()
                dve.tensor_copy(ET.rearrange("p (n c) -> p n c", c=NCH),
                                cum.rearrange("p n (c t) -> p n c t", c=NCH)[:, :, :, C - 1]).then_inc(s["gT"], 1)
                dve.wait_ge(*s("gT", 1))

            def hgrn_decays(l):
                s, t0 = L[l], t0_of(l)
                ff, E = rr(R_FF, 2048), rr(R_T + 2048, 2048)
                cum = rr(R_T, 2048, "p (n t) -> p n t", n=4)
                c8 = lambda ap: ap.rearrange("p (n t) -> p n t", t=C)
                QI = rr(R_T + 4096, 2048)
                Tb = lambda d: Tl[:, 8 * d:8 * d + 8].unsqueeze(2).to_broadcast([P, 8, C])
                Tl = mcol[:, 0:16]
                link(dve.tensor_copy(Tl, cum.rearrange("p n (c t) -> p (n c) t", c=NCH)[:, :, C - 1]))
                link(dve.tensor_tensor(cum[:, 2:4, :], cum[:, 2:4, :], rr(R_T + 3072, 1024, "p (n t) -> p n t", n=2),
                                       ALU.subtract if l else ALU.add))
                X = rr(R_T + 1024, 1024)
                dve.tensor_tensor(c8(E[:, 0:1024]), Tb(0), c8(rr(R_T, 1024)), ALU.subtract).then_inc(s["gKa"], 1)
                dve.tensor_tensor(c8(QI[:, 1024:2048]), Tb(1), c8(X), ALU.subtract).then_inc(s["gKa"], 1)
                dve.wait_ge(*s("gKe", 4))
                dve.tensor_tensor(E[:, 0:1024], E[:, 0:1024], ff[:, 0:1024], ALU.mult).then_inc(s["gKm"], 1)
                dve.tensor_tensor(E[:, 1024:2048], E[:, 1024:2048], ff[:, 1024:2048], ALU.mult).then_inc(s["gKm"], 1)
                dve.wait_ge(*s("gKe", 5))
                qi4 = rr(R_T + 4096, 2048, "p (d j t) -> p d j t", d=2, j=2)
                q2 = rr(R_HQ, 1024, "p (j t) -> p j t", j=2)
                for d in range(2):
                    dve.tensor_tensor(qi4[:, d, :, t0:T], qi4[:, d, :, t0:T], q2[:, :, t0:T],
                                      ALU.mult).then_inc(s["gKm"], 1)

            def hgrn(l):
                s, t0, OC = L[l], t0_of(l), out_chunks(l)
                k4 = rr(R_FF, 2048, "p (n t) -> p n t", n=4)

                def added(d, j, i, r):
                    n = 3 * (2 * d + j) + i
                    return B[4 + n // 4][r, (n % 4) * P + r.start:(n % 4) * P + r.stop]

                dve.wait_ge(*s("gSp", 1))
                states(s, "gS", added,
                       lambda d, j, c: ET[:, 4 * (2 * d + j) + c:4 * (2 * d + j) + c + 1])
                AT = rr(R_T + 6144, 2048, "p (n u t) -> p n u t", u=2, t=C)
                nh = T - t0

                def halves(at, h, side):
                    v = rr(at, 1024, "p (j b u t) -> p j b u t", j=2, u=2, t=h)
                    return v[:, :, t0 // (2 * h):, side, :]

                def middle(at, h, side):
                    v = rr(at, 1024, "p (j b u t) -> p j b u t", j=2, u=2, t=h)[:, :, t0 // (2 * h):, side, :]
                    v = v[:, :, :, h - 1:h] if side == 0 else v[:, :, :, 0:1]
                    return v.to_broadcast([P, 2, nh // (2 * h), h])

                def args(lv):
                    h = HALVES[lv]
                    f, b, ef, eb = R_T, R_T + 1024, R_T + 2048, R_T + 3072
                    dve.tensor_tensor(halves(ef, h, 1), halves(f, h, 1), middle(f, h, 0),
                                      ALU.subtract).then_inc(s["gA"], 1)
                    dve.tensor_tensor(halves(ef, h, 0), middle(f, h, 0), halves(f, h, 0),
                                      ALU.subtract).then_inc(s["gA"], 1)
                    dve.tensor_tensor(halves(eb, h, 0), middle(b, h, 1), halves(b, h, 0),
                                      ALU.subtract).then_inc(s["gA"], 1)
                    dve.tensor_tensor(halves(eb, h, 1), halves(b, h, 1), middle(b, h, 1),
                                      ALU.subtract).then_inc(s["gA"], 1)

                dve.wait_ge(*s("gKt", 1))
                dve.wait_ge(*s("gKm", 4))
                dve.wait_ge(masks_s, 1)
                def keys_queries(lv):
                    at = R_T + 4096 if lv % 2 == 0 else R_XBC
                    if lv >= 2:
                        dve.wait_ge(*s("gP", (lv - 1) * len(OC) // 2))
                    if lv < len(HALVES):
                        h = HALVES[lv]
                        ef, eb = R_T + 2048, R_T + 3072
                        dve.wait_ge(*s("gE", lv + 1))
                        mark(dve.tensor_tensor(halves(at, h, 0), halves(R_FF, h, 0), halves(ef, h, 0), ALU.mult))
                        mark(dve.tensor_tensor(halves(at, h, 1), halves(R_FF + 1024, h, 1), halves(eb, h, 1), ALU.mult))
                        mark(dve.tensor_tensor(halves(at + 1024, h, 1), halves(R_HQ, h, 1), halves(ef, h, 1), ALU.mult))
                        dve.tensor_tensor(halves(at + 1024, h, 0), halves(R_HQ, h, 0), halves(eb, h, 0),
                                          ALU.mult).then_inc(s["gKQ"], 1)
                        if lv + 1 < len(HALVES):
                            dve.wait_ge(*s("gKQ", lv + 1))
                            args(lv + 1)
                    elif lv == len(HALVES):
                        kk = rr(at, 1024, "p (j t) -> p j t", j=2)
                        dve.tensor_tensor(kk[:, :, t0:T], k4[:, 0:2, t0:T], k4[:, 2:4, t0:T],
                                          ALU.add).then_inc(s["gKQ"], 1)

                args(0)
                n_at = 0
                dve.wait_ge(*s("gO", 1))
                keys_queries(0)
                for lv in range(len(HALVES) + 1):
                    if lv < len(HALVES):
                        keys_queries(lv + 1)
                    for c2 in range(OC[0] // 2, 2):
                        dve.wait_ge(*s("gP", n_at + 1))
                        if lv:
                            dve.wait_ge(*s("gAT", 2 * (n_at + 1 - len(OC) // 2)))
                        for odd in range(2):
                            ps = B[3 + 2 * (n_at % 2) + odd][:, :].rearrange("p (n t) -> p n t", n=4)
                            to = AT[:, 4 * c2:4 * c2 + 4, odd, :]
                            if lv == 0:
                                ins = dve.tensor_copy(to, ps)
                            else:
                                ins = dve.copy_predicated(to, masks[:, lv, :].unsqueeze(1).to_broadcast([P, 4, C]), ps)
                            ins.then_inc(s["gAT"], 1)
                        n_at += 1
                    for k in range(KQ + KKV):
                        a = t0 if k < KQ else 0
                        if lv == 0:
                            dve.wait_ge(*s("lrs", 1))
                            g = vec(l, V_QA + k, 1) if k < KQ else vec(l, V_KVA + k - KQ, 1)
                            x = rr(R_QL + k * T + a, T - a)
                            dve.scalar_tensor_tensor(x, x, g, th[:, 0 if k < KQ else 1, a:T], ALU.mult,
                                                     ALU.mult).then_inc(s["lh"], 1)
                        if lv == 2:
                            dve.wait_ge(*s("lhi", k + 1))
                            dve.tensor_tensor(latent16(k)[:, 1, a:T], rr(R_QL + k * T + a, T - a),
                                              latent16(k)[:, 0, a:T], ALU.subtract).then_inc(s["llo"], 1)
                r = rr(R_T + 3072, 1024, "p (j t) -> p j t", j=2)
                mx = rr(R_T + 4096, 1024, "p (j t) -> p j t", j=2)
                og = rr(R_OG, 1024, "p (j t) -> p j t", j=2)
                for j in range(2):
                    dve.wait_ge(*s("grs", j + 1))
                    mark(dve.scalar_tensor_tensor(r[:, j, t0:T], r[:, j, t0:T], vec(l, V_HGN + j, 1), B[1 + j][:, t0:T],
                                                  ALU.mult, ALU.mult))
                sync()
                for j in range(2):
                    dve.scalar_tensor_tensor(mx[:, j, t0:T], r[:, j, t0:T], 0.5 / WS, og[:, j, t0:T], ALU.mult,
                                             ALU.mult).then_inc(s["gm"], 1)
                for j in range(2):
                    dve.wait_ge(*s("ghi", j + 1))
                    dve.tensor_tensor(act16[:, 1, 4 + j, t0:T], mx[:, j, t0:T], act16[:, 0, 4 + j, t0:T],
                                      ALU.subtract).then_inc(s["glo"], 1)

            def mla(l):
                s, t0 = L[l], t0_of(l)
                QT = rr(R_HQ + 2560, 4096, "p (h t) -> p h t", h=HEADS)
                KTt = rr(R_HQ + 6656, 4096, "p (h t) -> p h t", h=HEADS)
                V = rr(R_HQ + 10752, 4096, "p (c h v) -> p c h v", c=NCH, h=HEADS)
                qr = rr(R_HQ + 14848, 1024, "p (j t) -> p j t", j=2)
                o32 = rr(R_HQ + 14848, 1024, "p (b t) -> p b t", b=2)
                cos, sin = const(C_COS, SEQ), const(C_SIN, SEQ)
                ahead(("qb", l, 0))
                kr = rr(R_MISC, T)[0:ROPE, :]
                dve.wait_ge(*s("krp", 1))
                mark(dve.tensor_tensor(rr(R_QL, SEQ)[0:ROPE, :], B[4][0:ROPE, 0:SEQ], sin[0:ROPE, :], ALU.mult))
                mark(dve.tensor_tensor(kr[:, SEQ:T], kr[:, SEQ:T], cos[0:ROPE, :], ALU.mult))
                sync()
                dve.tensor_tensor(kr[:, SEQ:T], kr[:, SEQ:T], rr(R_QL, SEQ)[0:ROPE, :], ALU.add).then_inc(s["krc"], 1)
                for m in range(6):
                    if m % 3 < 2:
                        dve.wait_ge(*s("qp", 2 * (m // 3) + m % 3 + 1))
                    else:
                        dve.wait_ge(prod, AT_UNIT["qb", l, m // 3] + 1)
                    if m == 3:
                        ahead(("qb", l, 1))
                    ps = B[m % 4]
                    if m < 4:
                        dve.tensor_scalar(QT[0:64, 2 * m, t0:T], ps[0:64, t0:T], 1.0 / WS, None, ALU.mult)
                        dve.tensor_scalar(QT[0:64, 2 * m + 1, t0:T], ps[64:128, t0:T], 1.0 / WS, None,
                                          ALU.mult).then_inc(s["qn"], 1)
                    else:
                        dve.tensor_scalar(qr[:, m - 4, t0:T], ps[:, t0:T], 1.0 / WS, None,
                                          ALU.mult).then_inc(s["qn"], 1)
                ahead(("kvb", l, 0))
                kb = (2, 3, 5, 6, 0, 1, 2, 3)
                for m in range(8):
                    if m < 7:
                        dve.wait_ge(*s("qp", 4 + m + 1))
                    else:
                        dve.wait_ge(prod, AT_UNIT["kvb", l, 0] + 1)
                    ps = B[kb[m]]
                    if m < 4:
                        dve.tensor_scalar(KTt[0:64, 2 * m, :], ps[0:64, :], 1.0 / WS, None, ALU.mult)
                        dve.tensor_scalar(KTt[0:64, 2 * m + 1, :], ps[64:128, :], 1.0 / WS, None,
                                          ALU.mult).then_inc(s["Kn"], 1)
                    else:
                        if m == 4:
                            dve.memset(V[:, :, :, 64:128].rearrange("p c h v -> p (c h) v"), 1.0)
                        dve.tensor_scalar(V[:, m - 4, :, 0:64], ps[:, :].rearrange("p (h v) -> p h v", h=HEADS), 1.0 / WS,
                                          None, ALU.mult).then_inc(s["Vv"], 1)
                rt = rr(R_QL, 2 * SEQ, "p (j t) -> p j t", j=2)
                for j in range(2):
                    dve.wait_ge(*s("qrp", j + 1))
                    mark(dve.tensor_tensor(rt[:, j, :], B[5 + j][:, 0:SEQ], sin, ALU.mult))
                    mark(dve.tensor_tensor(qr[:, j, SEQ:T], qr[:, j, SEQ:T], cos, ALU.mult))
                    if t0 == 0:
                        for i in range(4):
                            mark(dve.tensor_copy(QT[64:96, 4 * j + i, 0:SEQ], qr[32 * i:32 * i + 32, j, 0:SEQ]))
                    sync()
                    for i in range(4):
                        dve.tensor_tensor(QT[64:96, 4 * j + i, SEQ:T], qr[32 * i:32 * i + 32, j, SEQ:T],
                                          rt[32 * i:32 * i + 32, j, :], ALU.add).then_inc(s["Qd"], 1)
                Kb = max_copies()[1]
                dve.wait_ge(*s("krdma", 16))
                for h4 in (0, 4):
                    dve.tensor_copy(Kb[0:QK, h4:h4 + 4, :], KTt[0:QK, h4:h4 + 4, :]).then_inc(s["kb16"], 1)
                for h in range(3):
                    row_max(l, h)
                for h in range(HEADS):
                    if h + 3 < HEADS:
                        row_max(l, h + 3)
                    rd = rstd if h % 2 == 0 else th[:, 0, :]
                    r = slice(64 * (h % 2), 64 * (h % 2) + 64)
                    dve.wait_ge(*s("den", h + 1))
                    if h >= 4 and h % 2 == 0:
                        dve.wait_ge(*s("ohi", h // 2 - 1))
                        dve.wait_ge(*s("olo", h // 2 - 1))
                    dve.tensor_tensor(o32[r, (h // 2) % 2, t0:T], B[5 + h % 2][0:64, t0:T], rd[0:64, t0:T],
                                      ALU.mult).then_inc(s["on"], 1)
                    if h % 2 == 1:
                        dve.wait_ge(*s("ohi", h // 2 + 1))
                        dve.tensor_tensor(act16[:, 1, h // 2, t0:T], o32[:, (h // 2) % 2, t0:T],
                                          act16[:, 0, h // 2, t0:T], ALU.subtract).then_inc(s["olo"], 1)

            def row_max(l, h):
                for i, qt in enumerate(query_tiles(l)):
                    keys = SEQ if qt < 2 else T
                    dve.wait_ge(*L[l]("smx", h * len(query_tiles(l)) + i + 1))
                    dve.tensor_reduce(max_of(h, qt), B[(7, 4)[i % 2]][:, 0:keys], AX.X, ALU.max).then_inc(L[l]["mx"], 1)

            def residual(l, u, m2, which):
                t0, g = t0_of(l), AT_GROUP[u]
                for m in range(2):
                    k = 2 * m2 + m
                    for sq in range(t0 // SEQ, 2):
                        a = slice(sq * SEQ, sq * SEQ + SEQ)
                        last = dve.scalar_tensor_tensor(xT[:, k, a], B[2 * (g % 2) + m][:, a],
                                                        aff[:, l, 2 + which, k, 1 - sq:2 - sq], xT[:, k, a], ALU.mult,
                                                        ALU.add)
                last.then_inc(evac, 1)

            def ffn(l):
                s, t0 = L[l], t0_of(l)
                h16 = rr(0, KF * T).bitcast(F16).rearrange("p (a k t) -> p a k t", a=2, k=KF)

                def hidden_low(i):
                    dve.wait_ge(*s("hhi", i + 1))
                    dve.tensor_tensor(h16[:, 1, i, t0:T], h32(i)[:, t0:T], h16[:, 0, i, t0:T],
                                      ALU.subtract).then_inc(s["hlo"], 1)

                for i in range(N_FI):
                    ahead(("fi", l, i))
                    if l == 0:
                        ahead(("ada", 1, i))
                    if i >= 1:
                        hidden_low(i - 1)
                    g = AT_GROUP["fi", l, i]
                    tanhs[0] += 1
                    dve.wait_ge(tanh_s, tanhs[0])
                    u = th[:, i % 2, t0:T]
                    link(dve.scalar_tensor_tensor(u, u, 1.0, B[2 * (g % 2)][:, t0:T], ALU.add, ALU.mult))
                    dve.scalar_tensor_tensor(h32(i)[:, t0:T], u, 0.5 / WS / WS, B[2 * (g % 2) + 1][:, t0:T],
                                             ALU.mult, ALU.mult).then_inc(evac, 1)
                hidden_low(N_FI - 1)
                for i in range(N_FO):
                    ahead(("fo", l, i))
                    if l == 0 and i < N_ADA - N_FI:
                        ahead(("ada", 1, N_FI + i))
                    if i % 3 == 2:
                        dve.wait_ge(prod, AT_UNIT["fo", l, i] + 1)
                        residual(l, ("fo", l, i - 2), i // 3, 1)

            nxt = [8]
            tanhs = [0]
            dve.wait_ge(vecs_in, 16)
            dve.wait_ge(setup, 4)
            dve.wait_ge(cs_t, 1)
            link(dve.scalar_tensor_tensor(cs[:, 0, :, :], cs[:, 1, :, :], 1.0, cvec(), ALU.add, ALU.mult))
            dve.tensor_scalar(cs[:, 0, :, :], cs[:, 0, :, :], 0.5, None, ALU.mult).then_inc(cs_v, 1)
            dve.wait_ge(cs_v, 1)
            dve.wait_ge(cs_t, 2)
            dve.tensor_tensor(cs16[:, :, 1, :], cs[:, 0, :, :], cs16[:, :, 0, :], ALU.subtract).then_inc(cs_v, 1)
            for n in range(N_DIRECT):
                low(n)
            dve.wait_ge(prod, N_DIRECT)
            modulation(0, 0, 16)
            gains(0, 0)
            dve.wait_ge(x_in, 16)
            dve.wait_ge(params, 16)
            dve.wait_ge(*L[0]("rstd1", 1))
            low(N_DIRECT)
            for l in range(DEPTH):
                s = L[l]
                norm(l, "1", 0)
                if l == 0:
                    for n in range(N_DIRECT + 1, N_DIRECT + AHEAD):
                        low(n)
                for i in range(N_IN):
                    inproj(l, i)
                if l == 0:
                    dve.wait_ge(prod, AT_UNIT["ada", 0, N_ADA - 1] + 1)
                    modulation(0, 16, 48)
                    gains(0, 1)
                    gate(0, 0)
                    gate(0, 1)
                ssm_out(l)
                hgrn(l)
                mla(l)
                for i in range(N_OUT):
                    ahead(("out", l, i))
                    dve.wait_ge(prod, AT_UNIT["out", l, i] + 1)
                    residual(l, ("out", l, i), i, 0)
                norm(l, "2", t0_of(l))
                ffn(l)
                if l == 0:
                    modulation(1, 0, 48)
                    gains(1, 0)
                    gains(1, 1)
                    gate(1, 0)
                    gate(1, 1)
            dve.wait_ge(fin["rstd"], 1)
            for k in range(KD):
                dve.scalar_tensor_tensor(act32_out()[:, k, :], xT[:, k, SEQ:T], vecs[:, V_FINAL + k:V_FINAL + k + 1],
                                         rstd[:, SEQ:T], ALU.mult, ALU.mult).then_inc(fin["y"], 1)


def constants():
    c = np.zeros((P, C_COLS), np.float32)
    i = np.arange(P)
    c[:, C_ID:C_ID + P] = np.eye(P)
    c[:, C_ONES:C_ONES + P] = 1
    c[:, C_B64:C_B64 + P] = (i[:, None] // 64) == (i[None, :] // 64)
    c[:, C_RESET:C_RESET + T] = (np.arange(T) % C) != 0
    c[:, C_MF:C_MF + P] = i[:, None] <= i[None, :]
    c[:, C_MB:C_MB + P] = i[:, None] >= i[None, :]
    for r in range(8):
        c[r, C_SEL + r * P:C_SEL + r * P + P] = 1
    for d in range(2):
        for g in range(2):
            for h in range(2):
                at = C_SELT + (2 * d + g) * P + 64 * h
                c[4 * d + 2 * g + h, at:at + 64] = 1
    t = np.arange(SEQ, dtype=np.float32)
    pos = np.stack([np.floor(t / GRID_W), t % GRID_W])
    nf = ROPE // 4
    inv = np.float32(10000.0) ** (-np.arange(nf, dtype=np.float32) / np.float32(nf))
    for r in range(P):
        x = r % ROPE
        a, b, f = x // 16, (x // 8) % 2, x % 8
        ang = pos[a].astype(np.float32) * inv[f].astype(np.float32)
        c[r, C_COS:C_COS + SEQ] = np.cos(ang)
        c[r, C_SIN:C_SIN + SEQ] = np.sin(ang) * (-1 if b == 0 else 1)
        c[r ^ 8, C_PERM + r] = 1
    isf = (np.arange(8) < 4).astype(np.float32)
    isb = 1 - isf
    for n, v in enumerate((isf, isb, -isb, isb - isf, isf - isb)):
        c[0:8, C_SGN + n] = v
    m = np.zeros((P, 8, C), np.float32)
    for n, h in enumerate(HALVES):
        m[:, n] = ((i[:, None] // (2 * h)) == (i[None, :] // (2 * h))) & ((i[:, None] // h) != (i[None, :] // h))
    m[:, 7] = np.eye(P)
    return c, m.reshape(P, 8 * C)


def feature_major(a):
    a = np.asarray(a)
    return np.moveaxis(a.reshape(-1, P), 1, 0)


def tiled(a, cols):
    a = np.asarray(a)[:, cols]
    return a.reshape(-1, P, a.shape[1]).transpose(1, 0, 2)


def kernel(**inputs):
    import concourse.bacc as _bacc
    from concourse.bass_utils import run_bass_kernel_spmd as _run

    a = {k: np.asarray(v) for k, v in inputs.items()}
    v = np.zeros((P, V_COLS), np.float32)
    for l in range(DEPTH):
        o = l * V_LAYER

        def put(at, block):
            v[:block.shape[0], o + at:o + at + block.shape[1]] = block

        put(V_BADA, feature_major(a["b_ada"][l]))
        put(V_N1, feature_major(a["norm1_g"][l]))
        put(V_N2, feature_major(a["norm2_g"][l]))
        put(V_QA, feature_major(a["mla_qa_g"][l]))
        put(V_KVA, feature_major(a["mla_kva_g"][l]))
        put(V_LB, feature_major(a["hg_lb_logits"][l]))
        put(V_HGN, feature_major(a["hg_norm_g"][l]))
        put(V_CW, feature_major(a["ssm_conv_w"][l]))
        put(V_CB, feature_major(a["ssm_conv_b"][l]))
        put(V_DTB, a["ssm_dt_bias"][l].reshape(8, 1))
        put(V_ALOG, a["ssm_a_log"][l].reshape(8, 1))
        put(V_D, feature_major(np.repeat(a["ssm_d"][l], 64)))
        put(V_SN, feature_major(a["ssm_norm_g"][l]))
    v[:, V_FINAL:V_FINAL + KD] = feature_major(a["final_g"])
    v[:, V_C:V_C + 2 * KD] = np.stack([feature_major(a["c"]), feature_major(a["c_ctx"])], axis=2).reshape(P, -1)
    at = {"kv0": Q_RANK, "kv1": Q_RANK + P, "ql0": 0, "ql1": P, "ql2": 2 * P}
    for n, name in enumerate(("q0", "q1", "ff0", "ff1", "fb0", "fb1", "iv", "iv", "og0", "og1")):
        at.setdefault(name, MLA_COLS + P * n)
    for n, name in enumerate(("z0", "z1", "xs0", "xs1", "B", "C")):
        at[name] = SSM_AT + P * n
    span = lambda lo, n: np.arange(lo, lo + n)
    misc = np.concatenate([span(Q_RANK + KV_RANK, ROPE), span(SSM_AT + 6 * P, 8), np.zeros(88, np.int64)])
    cols = {"ada": [span(256 * i, 256) for i in range(N_ADA)],
            "in": [np.concatenate([misc if n == "misc" else span(at[n] + (P if (n == "iv" and j) else 0), P)
                                   for j, n in enumerate(names)]) for names in IN_TILES],
            "out": [span(256 * i, 256) for i in range(N_OUT)],
            "fi": [np.concatenate([span(P * i, P), span(FFN + P * i, P)]) for i in range(N_FI)]}
    per = np.arange(HEADS)[:, None]
    cols["qb"] = np.concatenate([(per * QK + np.arange(NOPE)).ravel(),
                                 (per * QK + NOPE + np.arange(ROPE)).ravel()]).reshape(2, 384)
    cols["kvb"] = [np.concatenate([(per * 128 + np.arange(NOPE)).ravel(), (per * 128 + NOPE + np.arange(VD)).ravel()])]
    src = {"ada": "w_ada", "in": "w_in", "qb": "mla_wqb", "kvb": "mla_wkvb", "out": "w_out", "fi": "w_ffn_in"}
    wt = {k: np.stack([np.stack([tiled(a[src[k]][l], c) for c in cols[k]]) for l in range(DEPTH)]) for k in src}
    fo = a["w_ffn_out"]
    wt["fo"] = np.zeros((DEPTH, N_FO, P, KD, 256), np.float32)
    for i in range(N_FO):
        k0, kt = 8 * (i % 3), FO_KT[i % 3]
        for l in range(DEPTH):
            wt["fo"][l, i, :, 0:kt] = tiled(fo[l][k0 * P:(k0 + kt) * P], span(256 * (i // 3), 256))
    c, m = constants()
    xin = np.concatenate([a["ctx"][0], a["x"][0]], axis=0)
    arrays = {f"in_w_{k}": np.ascontiguousarray(t.reshape(DEPTH, t.shape[1], P, -1)) for k, t in wt.items()}
    arrays |= {"in_vecs": v, "in_consts": c, "in_masks": m,
               "in_x": np.ascontiguousarray(xin.reshape(T, KD, P).transpose(2, 1, 0))}
    nc = _bacc.Bacc("TRN2", target_bir_lowering=False, num_devices=1)
    d = {n: nc.dram_tensor(n, x.shape, mybir.dt.from_np(x.dtype), kind="ExternalInput").ap() for n, x in arrays.items()}
    out = nc.dram_tensor("out_dram", (P, KD, SEQ), F32, kind="ExternalOutput").ap()
    build(nc, {k: d[f"in_w_{k}"] for k in wt}, d["in_vecs"], d["in_consts"], d["in_masks"], d["in_x"], out)
    r = _run(nc, [arrays], core_ids=[0])
    got = np.asarray(r.results[0]["out_dram"]).reshape(P, KD, SEQ)
    return np.ascontiguousarray(got.transpose(2, 1, 0).reshape(1, SEQ, D))
```
